# Optimizing a Trainium2 kernel written in Bass

```python
import math
import jax
import jax.numpy as jnp
from jax import lax
import numpy as np
import jax, jax.numpy as jnp

D_MODEL = 1024
BATCH = 1
SEQ = 512
DEPTH = 1

HEAD_DIM = 64
D_MIX = D_MODEL
H_RWKV = D_MIX // (4 * HEAD_DIM)
C_RWKV = H_RWKV * HEAD_DIM
H_FOX = (D_MIX - C_RWKV) // (2 * HEAD_DIM)
C_FOX = H_FOX * HEAD_DIM
H_NSA = (D_MIX - C_RWKV - C_FOX) // HEAD_DIM
C_NSA = H_NSA * HEAD_DIM
G_NSA = 2
HPG = H_NSA // G_NSA
C_KV_NSA = G_NSA * HEAD_DIM
R_DECAY = 32
R_AAA = 32
R_GATE = 64
L_CMP = 32
D_CMP = 16
CMP_HID = 128
L_SLC = 64
N_SLC = 16
N_LOCAL = 2
WINDOW = 512
Q_BLOCK = 128
SLC_Q_CHUNK = 64
NUM_BUCKETS = 32
MAX_DISTANCE = 128
D_FF = 2816
CONV_W = 3
RMS_EPS = 1e-6
GN_EPS = 64e-5
NEG_INF = -1e30
FORCE_SCORE = 1e4

RWKV_COLS = (C_RWKV, C_RWKV, C_RWKV, R_DECAY, R_AAA, R_GATE)
FOX_COLS = (C_FOX, C_FOX, C_FOX, H_FOX)
NSA_COLS = (C_NSA,) + (C_KV_NSA,) * 6 + (3 * H_NSA,)
N_RWKV_IN = sum(RWKV_COLS)
N_FOX_IN = sum(FOX_COLS)
N_NSA_IN = sum(NSA_COLS)
N_IN = N_RWKV_IN + N_FOX_IN + N_NSA_IN


def rmsnorm(x, g):
    xf = x.astype(jnp.float32)
    y = xf * lax.rsqrt(jnp.mean(xf * xf, axis=-1, keepdims=True) + RMS_EPS)
    return (y * g.astype(jnp.float32)).astype(x.dtype)

def split_cols(p, sizes):
    idx = np.cumsum(np.array(sizes))[:-1].tolist()
    return jnp.split(p, idx, axis=-1)

def shift_right(x):
    return jnp.pad(x, ((0, 0), (1, 0), (0, 0)))[:, : x.shape[1]]

def masked_softmax(logits, mask):
    p = jax.nn.softmax(jnp.where(mask, logits, NEG_INF), axis=-1)
    return jnp.where(mask, p, 0.0)

def t5_bucket(dist):
    n = jnp.maximum(dist, 0)
    max_exact = NUM_BUCKETS // 2
    nf = jnp.maximum(n, 1).astype(jnp.float32)
    large = max_exact + (jnp.log(nf / max_exact) / math.log(MAX_DISTANCE / max_exact)
                         * (NUM_BUCKETS - max_exact)).astype(jnp.int32)
    large = jnp.minimum(large, NUM_BUCKETS - 1)
    return jnp.where(n < max_exact, n, large)

def wkv7_scan(r, w, k, v, a, b):
    B, S, H, N = r.shape

    def step(state, inp):
        r_t, w_t, k_t, v_t, a_t, b_t = inp
        sa = jnp.einsum('bhvk,bhk->bhv', state, a_t)
        state = (state * w_t[:, :, None, :] + sa[..., None] * b_t[:, :, None, :]
                 + v_t[..., None] * k_t[:, :, None, :])
        return state, jnp.einsum('bhvk,bhk->bhv', state, r_t)

    xs = tuple(jnp.moveaxis(t, 1, 0) for t in (r, w, k, v, a, b))
    state0 = jnp.zeros((B, H, N, N), jnp.float32)
    _, ys = lax.scan(step, state0, xs)
    return jnp.moveaxis(ys, 0, 1)

def rwkv7_mix(p, mu, w0, w_up, a0, a_up, g_up, k_k, k_a, r_k, ln_w, ln_b):
    B, S, _ = p.shape
    dt = p.dtype
    p = p + (shift_right(p) - p) * mu
    r, k, v, xw, xa, xg = split_cols(p.astype(jnp.float32), RWKV_COLS)
    w = -jax.nn.softplus(-(w0 + jnp.tanh(xw) @ w_up)) - 0.5
    decay = jnp.exp(-jnp.exp(w))
    a = jax.nn.sigmoid(a0 + xa @ a_up)
    g = jax.nn.sigmoid(xg) @ g_up
    heads = lambda t: t.reshape(B, S, H_RWKV, HEAD_DIM)
    kk = heads(k * k_k)
    kk = kk / jnp.maximum(jnp.linalg.norm(kk, axis=-1, keepdims=True), 1e-12)
    k = k * (1.0 + (a - 1.0) * k_a)
    r_h, k_h, v_h, a_h = heads(r), heads(k), heads(v), heads(a)
    y = wkv7_scan(r_h, heads(decay), k_h, v_h, -kk, kk * a_h)
    mean = jnp.mean(y, axis=-1, keepdims=True)
    var = jnp.mean(jnp.square(y - mean), axis=-1, keepdims=True)
    yn = ((y - mean) * lax.rsqrt(var + GN_EPS)).reshape(B, S, C_RWKV) * ln_w + ln_b
    bonus = jnp.sum(r_h * k_h * r_k, axis=-1, keepdims=True) * v_h
    return ((yn + bonus.reshape(B, S, C_RWKV)) * g).astype(dt)

def fox_mix(p, b_f):
    B, S, _ = p.shape
    q, k, v, f_logit = split_cols(p, FOX_COLS)
    to_heads = lambda t: t.reshape(B, S, H_FOX, HEAD_DIM).transpose(0, 2, 1, 3)
    q, k, v = to_heads(q), to_heads(k), to_heads(v)
    log_f = jax.nn.log_sigmoid((f_logit + b_f).astype(jnp.float32))
    cum = jnp.cumsum(log_f, axis=1).transpose(0, 2, 1)
    scale = HEAD_DIM ** -0.5
    kpos = jnp.arange(S)

    def block(i):
        q0 = i * Q_BLOCK
        qb = lax.dynamic_slice_in_dim(q, q0, Q_BLOCK, axis=2)
        cb = lax.dynamic_slice_in_dim(cum, q0, Q_BLOCK, axis=2)
        logits = (jnp.einsum('bhqd,bhkd->bhqk', qb, k).astype(jnp.float32) * scale
                  + cb[..., None] - cum[:, :, None, :])
        qpos = q0 + jnp.arange(Q_BLOCK)
        probs = masked_softmax(logits, kpos[None, :] <= qpos[:, None])
        return jnp.einsum('bhqk,bhkd->bhqd', probs.astype(v.dtype), v)

    out = lax.map(block, jnp.arange(S // Q_BLOCK))
    return out.transpose(1, 0, 3, 2, 4).reshape(B, S, C_FOX)

def nsa_mix(p, pe_k, pe_v, ck_w1, ck_w2, cv_w1, cv_w2, rel_bias):
    B, S, _ = p.shape
    dt = p.dtype
    q, kc, vc, ks, vs, kw, vw, gate_logit = split_cols(p, NSA_COLS)
    q = q.reshape(B, S, G_NSA, HPG, HEAD_DIM)
    kvh = lambda t: t.reshape(B, S, G_NSA, HEAD_DIM)
    kc, vc, ks, vs, kw, vw = (kvh(t) for t in (kc, vc, ks, vs, kw, vw))
    scale = HEAD_DIM ** -0.5
    tpos = jnp.arange(S)

    n_ch = S // D_CMP
    ov = L_CMP // D_CMP
    n_cmp = n_ch - ov + 1

    def compress(t, pe, w1, w2):
        ch = t.reshape(B, n_ch, D_CMP, G_NSA, HEAD_DIM)
        blocks = jnp.concatenate([ch[:, j:j + n_cmp] for j in range(ov)], axis=2)
        blocks = blocks + pe[:, None, :]
        flat = blocks.transpose(0, 1, 3, 2, 4).reshape(B, n_cmp, G_NSA, L_CMP * HEAD_DIM)
        return jax.nn.gelu(flat @ w1) @ w2

    k_cmp = compress(kc, pe_k, ck_w1, ck_w2)
    v_cmp = compress(vc, pe_v, cv_w1, cv_w2)
    cmp_start = jnp.arange(n_cmp) * D_CMP
    cmp_end = cmp_start + L_CMP - 1
    dist_c = tpos[:, None] - cmp_end[None, :]
    bias_c = rel_bias[t5_bucket(dist_c)].reshape(S, n_cmp, G_NSA, HPG).transpose(2, 3, 0, 1)
    logits_c = jnp.einsum('bsghd,bcgd->bghsc', q, k_cmp).astype(jnp.float32) * scale + bias_c
    p_cmp = masked_softmax(logits_c, dist_c >= 0)
    o_cmp = jnp.einsum('bghsc,bcgd->bsghd', p_cmp.astype(dt), v_cmp)

    nsb = S // L_SLC
    slc_start = jnp.arange(nsb) * L_SLC
    overlap = ((cmp_start[:, None] <= slc_start[None, :] + L_SLC - 1)
               & (cmp_end[:, None] >= slc_start[None, :])).astype(jnp.float32)
    imp = jnp.einsum('bghsc,cj->bgsj', p_cmp, overlap)
    cur = tpos // L_SLC
    jb = jnp.arange(nsb)
    back = cur[:, None] - jb[None, :]
    valid = back >= 0
    forced = (jb[None, :] == 0) | (valid & (back < N_LOCAL))
    score = jnp.where(valid, jnp.where(forced, FORCE_SCORE, imp), -1.0)
    n_sel = min(N_SLC, nsb)
    top_val, top_idx = lax.top_k(score, n_sel)
    sel_ok = top_val >= 0.0

    kb = ks.reshape(B, nsb, L_SLC, G_NSA, HEAD_DIM).transpose(0, 3, 1, 2, 4)
    vb = vs.reshape(B, nsb, L_SLC, G_NSA, HEAD_DIM).transpose(0, 3, 1, 2, 4)
    gather = jax.vmap(jax.vmap(lambda blocks, idx: blocks[idx]))
    qg = q.transpose(0, 2, 1, 3, 4)
    tbl_g = rel_bias.reshape(NUM_BUCKETS, G_NSA, HPG).transpose(1, 0, 2)
    g_idx = jnp.arange(G_NSA)[None, :, None, None, None]

    def slc_chunk(i):
        q0 = i * SLC_Q_CHUNK
        qc = lax.dynamic_slice_in_dim(qg, q0, SLC_Q_CHUNK, axis=2)
        ic = lax.dynamic_slice_in_dim(top_idx, q0, SLC_Q_CHUNK, axis=2)
        okc = lax.dynamic_slice_in_dim(sel_ok, q0, SLC_Q_CHUNK, axis=2)
        kg = gather(kb, ic)
        vg = gather(vb, ic)
        qpos = q0 + jnp.arange(SLC_Q_CHUNK)
        kpos = ic[..., None] * L_SLC + jnp.arange(L_SLC)
        dist = qpos[None, None, :, None, None] - kpos
        mask = (okc[..., None] & (dist >= 0))[:, :, :, None]
        bias = tbl_g[g_idx, t5_bucket(dist)].transpose(0, 1, 2, 5, 3, 4)
        logits = jnp.einsum('bgqhd,bgqnld->bgqhnl', qc, kg).astype(jnp.float32) * scale + bias
        shp = logits.shape
        flat_mask = jnp.broadcast_to(mask, shp).reshape(shp[:4] + (n_sel * L_SLC,))
        probs = masked_softmax(logits.reshape(shp[:4] + (n_sel * L_SLC,)), flat_mask).reshape(shp)
        return jnp.einsum('bgqhnl,bgqnld->bgqhd', probs.astype(dt), vg)

    o_slc = lax.map(slc_chunk, jnp.arange(S // SLC_Q_CHUNK))
    o_slc = o_slc.transpose(1, 0, 3, 2, 4, 5).reshape(B, S, G_NSA, HPG, HEAD_DIM)

    kw_pad = jnp.pad(kw, ((0, 0), (WINDOW, 0), (0, 0), (0, 0)))
    vw_pad = jnp.pad(vw, ((0, 0), (WINDOW, 0), (0, 0), (0, 0)))
    n_keys = Q_BLOCK + WINDOW

    def win_block(i):
        q0 = i * Q_BLOCK
        qb = lax.dynamic_slice_in_dim(q, q0, Q_BLOCK, axis=1)
        kblk = lax.dynamic_slice_in_dim(kw_pad, q0, n_keys, axis=1)
        vblk = lax.dynamic_slice_in_dim(vw_pad, q0, n_keys, axis=1)
        qpos = q0 + jnp.arange(Q_BLOCK)
        kpos = q0 - WINDOW + jnp.arange(n_keys)
        dist = qpos[:, None] - kpos[None, :]
        mask = (dist >= 0) & (dist < WINDOW) & (kpos[None, :] >= 0)
        bias = rel_bias[t5_bucket(dist)].reshape(Q_BLOCK, n_keys, G_NSA, HPG).transpose(2, 3, 0, 1)
        logits = jnp.einsum('bqghd,bkgd->bghqk', qb, kblk).astype(jnp.float32) * scale + bias
        probs = masked_softmax(logits, mask)
        return jnp.einsum('bghqk,bkgd->bqghd', probs.astype(dt), vblk)

    o_win = lax.map(win_block, jnp.arange(S // Q_BLOCK))
    o_win = o_win.transpose(1, 0, 2, 3, 4, 5).reshape(B, S, G_NSA, HPG, HEAD_DIM)

    gates = jax.nn.sigmoid(gate_logit).reshape(B, S, G_NSA, HPG, 3)
    o = gates[..., 0:1] * o_cmp + gates[..., 1:2] * o_slc + gates[..., 2:3] * o_win
    return o.reshape(B, S, C_NSA)

def conv_ffn(h, w_up, conv_w, conv_b, w_down):
    S = h.shape[1]
    u = h @ w_up
    u_pad = jnp.pad(u, ((0, 0), (CONV_W - 1, 0), (0, 0)))
    u = conv_b + sum(conv_w[j] * u_pad[:, j:j + S] for j in range(CONV_W))
    gate, val = jnp.split(u, 2, axis=-1)
    return (jax.nn.silu(gate) * val) @ w_down

def first_inputs(seed: int = 0) -> dict:
    key = jax.random.key(seed)
    ks = iter(jax.random.split(key, 40))

    def nrm(shape, scale):
        return scale * jax.random.normal(next(ks), shape, jnp.float32)

    L, D = DEPTH, D_MODEL
    return {
        "x": nrm((BATCH, SEQ, D), 1.0),
        "c": nrm((BATCH, D), 1.0),
        "ada_w": nrm((L, D, 6 * D), 0.5 * D ** -0.5),
        "ada_b": nrm((L, 6 * D), 0.1),
        "norm_g": 1.0 + nrm((L, 4, D), 0.02),
        "w_in": nrm((L, D, N_IN), D ** -0.5),
        "rwkv_mu": 0.5 + nrm((L, N_RWKV_IN), 0.1),
        "rwkv_w0": nrm((L, C_RWKV), 0.5),
        "rwkv_w_up": nrm((L, R_DECAY, C_RWKV), 0.5 * R_DECAY ** -0.5),
        "rwkv_a0": nrm((L, C_RWKV), 0.3),
        "rwkv_a_up": nrm((L, R_AAA, C_RWKV), 0.5 * R_AAA ** -0.5),
        "rwkv_g_up": nrm((L, R_GATE, C_RWKV), R_GATE ** -0.5),
        "rwkv_k_k": 0.85 + nrm((L, C_RWKV), 0.05),
        "rwkv_k_a": 1.0 + nrm((L, C_RWKV), 0.05),
        "rwkv_r_k": nrm((L, H_RWKV, HEAD_DIM), 0.1),
        "rwkv_ln_w": 1.0 + nrm((L, C_RWKV), 0.02),
        "rwkv_ln_b": nrm((L, C_RWKV), 0.02),
        "fox_b_f": 3.0 + nrm((L, H_FOX), 0.5),
        "nsa_pe_k": nrm((L, L_CMP, HEAD_DIM), 0.1),
        "nsa_pe_v": nrm((L, L_CMP, HEAD_DIM), 0.1),
        "nsa_ck_w1": nrm((L, L_CMP * HEAD_DIM, CMP_HID), (L_CMP * HEAD_DIM) ** -0.5),
        "nsa_ck_w2": nrm((L, CMP_HID, HEAD_DIM), CMP_HID ** -0.5),
        "nsa_cv_w1": nrm((L, L_CMP * HEAD_DIM, CMP_HID), (L_CMP * HEAD_DIM) ** -0.5),
        "nsa_cv_w2": nrm((L, CMP_HID, HEAD_DIM), CMP_HID ** -0.5),
        "rel_bias": nrm((NUM_BUCKETS, H_NSA), 0.5),
        "w_out": nrm((L, D_MIX, D), D_MIX ** -0.5),
        "ffn_up": nrm((L, D, 2 * D_FF), D ** -0.5),
        "ffn_conv_w": nrm((L, CONV_W, 2 * D_FF), 0.3).at[:, -1].add(1.0),
        "ffn_conv_b": nrm((L, 2 * D_FF), 0.02),
        "ffn_down": nrm((L, D_FF, D), D_FF ** -0.5),
    }

def first_block(x, c, ada_w, ada_b, norm_g, w_in, rwkv_mu, rwkv_w0, rwkv_w_up, rwkv_a0,
              rwkv_a_up, rwkv_g_up, rwkv_k_k, rwkv_k_a, rwkv_r_k, rwkv_ln_w, rwkv_ln_b,
              fox_b_f, nsa_pe_k, nsa_pe_v, nsa_ck_w1, nsa_ck_w2, nsa_cv_w1, nsa_cv_w2,
              rel_bias, w_out, ffn_up, ffn_conv_w, ffn_conv_b, ffn_down):
    for l in range(DEPTH):
        mod = jax.nn.silu(c) @ ada_w[l] + ada_b[l]
        sh_m, sc_m, g_m, sh_f, sc_f, g_f = jnp.split(mod[:, None, :], 6, axis=-1)

        h = rmsnorm(x, norm_g[l, 0]) * (1.0 + sc_m) + sh_m
        p = h @ w_in[l]
        p_a, p_b, p_c = split_cols(p, (N_RWKV_IN, N_FOX_IN, N_NSA_IN))
        y_a = rwkv7_mix(p_a, rwkv_mu[l], rwkv_w0[l], rwkv_w_up[l], rwkv_a0[l], rwkv_a_up[l],
                        rwkv_g_up[l], rwkv_k_k[l], rwkv_k_a[l], rwkv_r_k[l],
                        rwkv_ln_w[l], rwkv_ln_b[l])
        y_b = fox_mix(p_b, fox_b_f[l])
        y_c = nsa_mix(p_c, nsa_pe_k[l], nsa_pe_v[l], nsa_ck_w1[l], nsa_ck_w2[l],
                      nsa_cv_w1[l], nsa_cv_w2[l], rel_bias)
        y = jnp.concatenate([y_a, y_b, y_c], axis=-1) @ w_out[l]
        x = x + g_m * rmsnorm(y, norm_g[l, 1])

        h = rmsnorm(x, norm_g[l, 2]) * (1.0 + sc_f) + sh_f
        f = conv_ffn(h, ffn_up[l], ffn_conv_w[l], ffn_conv_b[l], ffn_down[l])
        x = x + g_f * rmsnorm(f, norm_g[l, 3])
    return x


_first_inputs = first_inputs


def first_inputs(seed=0):
    import zlib

    import numpy as np

    out = dict(_first_inputs(seed))
    spreads = {}
    factors = {'norm_g': 3.876,
     'rwkv_w_up': 3.832,
     'rwkv_k_k': 8.0,
     'rwkv_k_a': 4.012,
     'rwkv_ln_w': 8.0,
     'rwkv_ln_b': 8.0,
     'fox_b_f': 7.439,
     'nsa_pe_k': 8.0,
     'nsa_pe_v': 4.427,
     'ffn_conv_b': 8.0}
    for name, (base, spread) in spreads.items():
        noise = np.random.default_rng([zlib.crc32(name.encode()), seed]).standard_normal(out[name].shape)
        drawn = base * np.exp(spread * noise) if base else spread * noise
        out[name] = jnp.asarray(drawn.astype(out[name].dtype))
    for name, factor in factors.items():
        out[name] = (out[name] * factor).astype(out[name].dtype)
    return out


_narrow_inputs = first_inputs


def first_inputs(seed=0):

    out = dict(_narrow_inputs(seed))
    wider = {'rwkv_k_k': 12.0,
     'rwkv_ln_w': 11.88,
     'rwkv_ln_b': 11.02,
     'fox_b_f': 12.0,
     'nsa_pe_v': 4.84}
    for name, times in wider.items():
        mean = out[name].mean()
        out[name] = (mean + times * (out[name] - mean)).astype(out[name].dtype)
    return out


DIL_GROUPS = ((128, 1), (512, 4), (2048, 16))
A_HEADS_PER_GROUP = 4
A_HEADS = A_HEADS_PER_GROUP * len(DIL_GROUPS)
A_OUT = A_HEADS_PER_GROUP * HEAD_DIM
B_HEADS = 4
B_V_DIM = 2 * HEAD_DIM
B_OUT = B_HEADS * B_V_DIM
C_HEADS = 4
C_OUT = C_HEADS * HEAD_DIM
IDX_HEADS = 8
IDX_DIM = 64
TOPK_MAX = 256
MAX_DISTANCE_2 = 2048
BIAS_HEADS = A_HEADS + B_HEADS + C_HEADS

A_QKV_COLS = 3 * A_HEADS * HEAD_DIM
B_QK_COLS = 4 * B_HEADS * HEAD_DIM
B_V_COLS = B_HEADS * B_V_DIM
C_COLS = C_HEADS * HEAD_DIM + 2 * HEAD_DIM
IDX_COLS = IDX_HEADS * IDX_DIM + IDX_DIM + IDX_HEADS
GATE_COLS = 3 * D_MODEL
N_IN_2 = A_QKV_COLS + B_QK_COLS + B_V_COLS + C_COLS + IDX_COLS + GATE_COLS
SPLIT_POINTS = [A_QKV_COLS,
                A_QKV_COLS + B_QK_COLS,
                A_QKV_COLS + B_QK_COLS + B_V_COLS,
                A_QKV_COLS + B_QK_COLS + B_V_COLS + C_COLS,
                A_QKV_COLS + B_QK_COLS + B_V_COLS + C_COLS + IDX_COLS]


def rms_norm(x, g):
    xf = x.astype(jnp.float32)
    y = xf * lax.rsqrt(jnp.mean(xf * xf, axis=-1, keepdims=True) + RMS_EPS)
    return (y * g.astype(jnp.float32)).astype(x.dtype)

def swiglu(x, w_gate, w_up, w_down):
    return (jax.nn.silu(x @ w_gate) * (x @ w_up)) @ w_down

def rel_bucket(dist):
    n = jnp.maximum(dist, 0)
    max_exact = NUM_BUCKETS // 2
    nf = jnp.maximum(n, 1).astype(jnp.float32)
    large = max_exact + (jnp.log(nf / max_exact) / math.log(MAX_DISTANCE_2 / max_exact)
                         * (NUM_BUCKETS - max_exact)).astype(jnp.int32)
    large = jnp.minimum(large, NUM_BUCKETS - 1)
    return jnp.where(n < max_exact, n, large)

def dilated_window_group(q, k, v, window, dilation, bias_table):
    b, t, h, dh = q.shape
    n = t // dilation
    wn = window // dilation
    nb = -(-n // wn)
    pad = nb * wn - n

    def to_sub(z):
        z = z.reshape(b, n, dilation, h, dh).transpose(0, 2, 1, 3, 4)
        return jnp.pad(z, ((0, 0), (0, 0), (0, pad), (0, 0), (0, 0)))

    qs, ks, vs = to_sub(q), to_sub(k), to_sub(v)
    qb = qs.reshape(b, dilation, nb, wn, h, dh)

    def band(z):
        zp = jnp.pad(z, ((0, 0), (0, 0), (wn, 0), (0, 0), (0, 0))).reshape(b, dilation, nb + 1, wn, h, dh)
        return jnp.concatenate([zp[:, :, :-1], zp[:, :, 1:]], axis=3)

    kb, vb = band(ks), band(vs)
    logits = jnp.einsum('brnqhe,brnkhe->brnhqk', qb, kb).astype(jnp.float32) * (dh ** -0.5)
    a = jnp.arange(wn)[:, None]
    c = jnp.arange(2 * wn)[None, :]
    sub_dist = wn + a - c
    bias = bias_table[rel_bucket(sub_dist * dilation)].astype(jnp.float32)
    logits = logits + bias.transpose(2, 0, 1)
    key_pos = (jnp.arange(nb)[:, None] - 1) * wn + c
    mask = ((sub_dist >= 0) & (sub_dist <= wn))[None] & (key_pos >= 0)[:, None, :]
    logits = jnp.where(mask[:, None], logits, -jnp.inf)
    m = jnp.max(logits, axis=-1)
    p = jnp.exp(logits - m[..., None])
    s = jnp.sum(p, axis=-1)
    o = jnp.einsum('brnhqk,brnkhe->brnqhe', p, vb.astype(jnp.float32))

    def from_sub(z):
        z = z.reshape((b, dilation, nb * wn) + z.shape[4:])[:, :, :n]
        z = jnp.moveaxis(z, 1, 2)
        return z.reshape((b, t) + z.shape[3:])

    return from_sub(o), from_sub(jnp.swapaxes(m, 3, 4)), from_sub(jnp.swapaxes(s, 3, 4))

def dilated_attention(q, k, v, bias_table):
    outs = []
    for g, (w, d) in enumerate(DIL_GROUPS):
        sl = slice(g * A_HEADS_PER_GROUP, (g + 1) * A_HEADS_PER_GROUP)
        outs.append(dilated_window_group(q[:, :, sl], k[:, :, sl], v[:, :, sl], w, d, bias_table[:, sl]))
    m_all = jnp.stack([m for _, m, _ in outs])
    scale = jnp.exp(m_all - jnp.max(m_all, axis=0))
    num = sum(scale[g][..., None] * outs[g][0] for g in range(len(DIL_GROUPS)))
    den = sum(scale[g] * outs[g][2] for g in range(len(DIL_GROUPS)))
    return num / den[..., None]

def diff_attention(qs, ks, v, lam, bias_table):
    t = qs.shape[1]
    dh = qs.shape[-1]
    outs = []
    for start in range(0, t, Q_BLOCK):
        end = start + Q_BLOCK
        logits = jnp.einsum('bqmhe,bkmhe->bmhqk', qs[:, start:end], ks[:, :end]).astype(jnp.float32) * (dh ** -0.5)
        dist = jnp.arange(start, end)[:, None] - jnp.arange(end)[None, :]
        bias = bias_table[rel_bucket(dist)].astype(jnp.float32).transpose(2, 0, 1)
        logits = jnp.where(dist >= 0, logits + bias, -jnp.inf)
        p = jax.nn.softmax(logits, axis=-1)
        w = p[:, 0] - lam * p[:, 1]
        outs.append(jnp.einsum('bhqk,bkhe->bqhe', w, v[:, :end].astype(jnp.float32)))
    return jnp.concatenate(outs, axis=1)

def dsa_attention(q, k, v, q_idx, k_idx, w_idx, bias_table):
    t = q.shape[1]
    dh = q.shape[-1]
    k_sel = min(TOPK_MAX, t // 4)
    gather = jax.vmap(lambda z, i: z[i])
    outs = []
    for start in range(0, t, Q_BLOCK):
        end = start + Q_BLOCK
        n_sel = min(k_sel, end)
        qpos = jnp.arange(start, end)
        raw = jnp.einsum('bqhe,bke->bqhk', q_idx[:, start:end], k_idx[:, :end]).astype(jnp.float32) * (IDX_DIM ** -0.5)
        score = jnp.einsum('bqh,bqhk->bqk', w_idx[:, start:end].astype(jnp.float32) * (IDX_HEADS ** -0.5),
                           jax.nn.relu(raw))
        score = jnp.where(jnp.arange(end)[None, :] <= qpos[:, None], score, -jnp.inf)
        top_val, top_idx = lax.top_k(score, n_sel)
        valid = jnp.isfinite(top_val)
        k_g = gather(k[:, :end], top_idx)
        v_g = gather(v[:, :end], top_idx)
        logits = jnp.einsum('bqhe,bqne->bhqn', q[:, start:end], k_g).astype(jnp.float32) * (dh ** -0.5)
        bias = bias_table[rel_bucket(qpos[None, :, None] - top_idx)].astype(jnp.float32)
        logits = jnp.where(valid[:, None], logits + jnp.moveaxis(bias, 3, 1), -jnp.inf)
        p = jax.nn.softmax(logits, axis=-1)
        outs.append(jnp.einsum('bhqn,bqne->bqhe', p, v_g.astype(jnp.float32)))
    return jnp.concatenate(outs, axis=1)

def token_mixer(h, w_in, qk_gain, diff_lambda, diff_out_norm, w_branch_a, w_branch_b, w_branch_c,
                w_out, rel_bias, layer_idx):
    b, t, _ = h.shape
    proj = h @ w_in
    a_qkv, b_qk, b_v, c_qkv, ix, gates = jnp.split(proj, SPLIT_POINTS, axis=-1)

    a_qkv = a_qkv.reshape(b, t, 3, A_HEADS, HEAD_DIM)
    qa = rms_norm(a_qkv[:, :, 0], qk_gain[0, 0])
    ka = rms_norm(a_qkv[:, :, 1], qk_gain[0, 1])
    o_a = dilated_attention(qa, ka, a_qkv[:, :, 2], rel_bias[:, :A_HEADS])
    o_a = o_a.reshape(b, t, A_OUT).astype(h.dtype)

    b_qk = b_qk.reshape(b, t, 4, B_HEADS, HEAD_DIM)
    qb = rms_norm(b_qk[:, :, 0:2], qk_gain[1, 0])
    kb = rms_norm(b_qk[:, :, 2:4], qk_gain[1, 1])
    lam_init = 0.8 - 0.6 * math.exp(-0.3 * layer_idx)
    lv = diff_lambda.astype(jnp.float32)
    lam = jnp.exp(jnp.sum(lv[0] * lv[1])) - jnp.exp(jnp.sum(lv[2] * lv[3])) + lam_init
    o_b = diff_attention(qb, kb, b_v.reshape(b, t, B_HEADS, B_V_DIM), lam, rel_bias[:, A_HEADS:A_HEADS + B_HEADS])
    o_b = rms_norm(o_b, diff_out_norm) * (1.0 - lam_init)
    o_b = o_b.reshape(b, t, B_OUT).astype(h.dtype)

    qc = rms_norm(c_qkv[..., :C_HEADS * HEAD_DIM].reshape(b, t, C_HEADS, HEAD_DIM), qk_gain[2, 0])
    kc = rms_norm(c_qkv[..., C_HEADS * HEAD_DIM:C_HEADS * HEAD_DIM + HEAD_DIM], qk_gain[2, 1])
    vc = c_qkv[..., C_HEADS * HEAD_DIM + HEAD_DIM:]
    q_idx = ix[..., :IDX_HEADS * IDX_DIM].reshape(b, t, IDX_HEADS, IDX_DIM)
    k_idx = ix[..., IDX_HEADS * IDX_DIM:IDX_HEADS * IDX_DIM + IDX_DIM]
    w_idx = ix[..., IDX_HEADS * IDX_DIM + IDX_DIM:]
    o_c = dsa_attention(qc, kc, vc, q_idx, k_idx, w_idx, rel_bias[:, A_HEADS + B_HEADS:])
    o_c = o_c.reshape(b, t, C_OUT).astype(h.dtype)

    g = jax.nn.sigmoid(gates.reshape(b, t, 3, D_MODEL))
    y = (g[:, :, 0] * (o_a @ w_branch_a) + g[:, :, 1] * (o_b @ w_branch_b)
         + g[:, :, 2] * (o_c @ w_branch_c))
    return y @ w_out

def second_inputs(seed: int = 0) -> dict:
    key = jax.random.key(seed)
    ks = jax.random.split(key, 20)
    f32 = jnp.float32

    def dense(k, shape, fan_in):
        return jax.random.normal(k, shape, f32) * fan_in ** -0.5

    def gain(k, shape):
        return 1.0 + 0.05 * jax.random.normal(k, shape, f32)

    return {
        "x": jax.random.normal(ks[0], (BATCH, SEQ, D_MODEL), f32),
        "rel_bias": 0.5 * jax.random.normal(ks[1], (NUM_BUCKETS, BIAS_HEADS), f32),
        "ffn1_norm": gain(ks[2], (DEPTH, D_MODEL)),
        "ffn1_w_gate": dense(ks[3], (DEPTH, D_MODEL, D_FF), D_MODEL),
        "ffn1_w_up": dense(ks[4], (DEPTH, D_MODEL, D_FF), D_MODEL),
        "ffn1_w_down": dense(ks[5], (DEPTH, D_FF, D_MODEL), D_FF),
        "mix_norm": gain(ks[6], (DEPTH, D_MODEL)),
        "w_in": dense(ks[7], (DEPTH, D_MODEL, N_IN_2), D_MODEL),
        "qk_gain": gain(ks[8], (DEPTH, 3, 2, HEAD_DIM)),
        "diff_lambda": 0.1 * jax.random.normal(ks[9], (DEPTH, 4, HEAD_DIM), f32),
        "diff_out_norm": gain(ks[10], (DEPTH, B_V_DIM)),
        "w_branch_a": dense(ks[11], (DEPTH, A_OUT, D_MODEL), A_OUT),
        "w_branch_b": dense(ks[12], (DEPTH, B_OUT, D_MODEL), B_OUT),
        "w_branch_c": dense(ks[13], (DEPTH, C_OUT, D_MODEL), C_OUT),
        "w_out": dense(ks[14], (DEPTH, D_MODEL, D_MODEL), D_MODEL),
        "ffn2_norm": gain(ks[15], (DEPTH, D_MODEL)),
        "ffn2_w_gate": dense(ks[16], (DEPTH, D_MODEL, D_FF), D_MODEL),
        "ffn2_w_up": dense(ks[17], (DEPTH, D_MODEL, D_FF), D_MODEL),
        "ffn2_w_down": dense(ks[18], (DEPTH, D_FF, D_MODEL), D_FF),
    }

def second_block(x, rel_bias, ffn1_norm, ffn1_w_gate, ffn1_w_up, ffn1_w_down, mix_norm, w_in, qk_gain,
              diff_lambda, diff_out_norm, w_branch_a, w_branch_b, w_branch_c, w_out,
              ffn2_norm, ffn2_w_gate, ffn2_w_up, ffn2_w_down):
    for i in range(DEPTH):
        x = x + 0.5 * swiglu(rms_norm(x, ffn1_norm[i]), ffn1_w_gate[i], ffn1_w_up[i], ffn1_w_down[i])
        x = x + token_mixer(rms_norm(x, mix_norm[i]), w_in[i], qk_gain[i], diff_lambda[i], diff_out_norm[i],
                            w_branch_a[i], w_branch_b[i], w_branch_c[i], w_out[i], rel_bias, i)
        x = x + 0.5 * swiglu(rms_norm(x, ffn2_norm[i]), ffn2_w_gate[i], ffn2_w_up[i], ffn2_w_down[i])
    return x


def setup_inputs(seed=0):
    out = dict(first_inputs(seed))
    for name, value in second_inputs(seed + 1).items():
        if name != "x":
            out[name + "_2"] = value
    return out


def reference(
    x, c, ada_w, ada_b, norm_g, w_in, rwkv_mu, rwkv_w0, rwkv_w_up, rwkv_a0, rwkv_a_up,
    rwkv_g_up, rwkv_k_k, rwkv_k_a, rwkv_r_k, rwkv_ln_w, rwkv_ln_b, fox_b_f, nsa_pe_k, nsa_pe_v,
    nsa_ck_w1, nsa_ck_w2, nsa_cv_w1, nsa_cv_w2, rel_bias, w_out, ffn_up, ffn_conv_w, ffn_conv_b,
    ffn_down, rel_bias_2, ffn1_norm_2, ffn1_w_gate_2, ffn1_w_up_2, ffn1_w_down_2, mix_norm_2,
    w_in_2, qk_gain_2, diff_lambda_2, diff_out_norm_2, w_branch_a_2, w_branch_b_2, w_branch_c_2,
    w_out_2, ffn2_norm_2, ffn2_w_gate_2, ffn2_w_up_2, ffn2_w_down_2,
):
    x = first_block(
        x, c, ada_w, ada_b, norm_g, w_in, rwkv_mu, rwkv_w0, rwkv_w_up, rwkv_a0, rwkv_a_up,
        rwkv_g_up, rwkv_k_k, rwkv_k_a, rwkv_r_k, rwkv_ln_w, rwkv_ln_b, fox_b_f, nsa_pe_k,
        nsa_pe_v, nsa_ck_w1, nsa_ck_w2, nsa_cv_w1, nsa_cv_w2, rel_bias, w_out, ffn_up,
        ffn_conv_w, ffn_conv_b, ffn_down,
    )
    return second_block(
        x, rel_bias_2, ffn1_norm_2, ffn1_w_gate_2, ffn1_w_up_2, ffn1_w_down_2, mix_norm_2,
        w_in_2, qk_gain_2, diff_lambda_2, diff_out_norm_2, w_branch_a_2, w_branch_b_2,
        w_branch_c_2, w_out_2, ffn2_norm_2, ffn2_w_gate_2, ffn2_w_up_2, ffn2_w_down_2,
    )


_drawn_inputs = setup_inputs


def setup_inputs(seed=0):
    import zlib

    import numpy as np

    out = dict(_drawn_inputs(seed))
    spreads = {}
    factors = {'ffn1_norm_2': 4.98,
     'mix_norm_2': 2.767,
     'qk_gain_2': 3.731,
     'diff_lambda_2': 7.292,
     'diff_out_norm_2': 5.368,
     'ffn2_norm_2': 5.796}
    for name, (base, spread) in spreads.items():
        noise = np.random.default_rng([zlib.crc32(name.encode()), seed]).standard_normal(out[name].shape)
        drawn = base * np.exp(spread * noise) if base else spread * noise
        out[name] = jnp.asarray(drawn.astype(out[name].dtype))
    for name, factor in factors.items():
        out[name] = (out[name] * factor).astype(out[name].dtype)
    return out
```

```python
import math
from contextlib import ExitStack

import numpy as np

import concourse.bass as bass
from concourse import mybir

F32 = mybir.dt.float32
ACT = mybir.ActivationFunctionType
ALU = mybir.AluOpType
AX = mybir.AxisListType

P = 128
T = 512
TT = T // P
D = 1024
KD = D // P
HD = 64
DFF = 2816
KF = DFF // P
ATT_SCALE = HD ** -0.5
EPS = 1e-6
MASKED = -1e30
LOWEST = -1e20

C_RWKV, R_LOW = 256, 128
N_RWKV = 3 * C_RWKV + R_LOW
RW_TILES = N_RWKV // P
C_FOX, H_FOX = 384, 6
FOX_Q = N_RWKV
FOX_V = FOX_Q + 2 * C_FOX
FOX_F = FOX_V + C_FOX
C_NSA, H_NSA, C_KV = 384, 6, 128
NSA_Q = FOX_F + H_FOX
NSA_KC = NSA_Q + C_NSA
NSA_VS = NSA_KC + 3 * C_KV
NSA_KW = NSA_VS + C_KV
NSA_VW = NSA_KW + C_KV
NSA_GATE = NSA_VW + C_KV
L_CMP, D_CMP, CMP_HID = 32, 16, 128
N_CMP = T // D_CMP - L_CMP // D_CMP + 1
GN_EPS = 64e-5

A_HEADS, B_HEADS, C_HEADS, IDX_HEADS = 12, 4, 4, 8
A_SLOTS, A_GROUPS = 4, 3
QA, VA = 0, 2 * A_HEADS * HD
QB = VA + A_HEADS * HD
VB = QB + 4 * B_HEADS * HD
QC = VB + B_HEADS * 2 * HD
KC, VC = QC + C_HEADS * HD, QC + (C_HEADS + 1) * HD
QI = QC + (C_HEADS + 2) * HD
KI = QI + IDX_HEADS * HD
WI = KI + HD
GATES = WI + IDX_HEADS
TOPK = 128
LAM_INIT = 0.8 - 0.6 * math.exp(-0.3 * 0)

TABLE_LEN = 640
N_TABLES = H_NSA + A_HEADS + B_HEADS + C_HEADS + 1
TAB_NSA, TAB_A, TAB_B, TAB_C, TAB_FOX = 0, 6, 18, 22, 26



def square_constants():
    s, t = np.arange(P)[:, None], np.arange(P)[None, :]
    mats = [s == t, s // HD == t // HD, s < t, s <= t]
    for level in range(7):
        size = 2 << level
        mats.append((s // size == t // size) & (s % size < size // 2) & (t % size >= size // 2))
    return np.stack(mats, 1).astype(np.float32)


IDENT, HEADS, STRICT, INCL, LEVELS = 0, 1, 2, 3, 4


def distance_buckets():
    dist = T - 1 - np.arange(TABLE_LEN)

    def bucket(max_distance):
        n = np.maximum(dist, 0)
        large = 16 + (np.log(np.maximum(n, 1) / 16) / math.log(max_distance / 16) * 16 + 1e-9).astype(np.int64)
        return np.where(n < 16, n, np.minimum(large, 31))

    near, far = bucket(128), bucket(2048)
    kinds = [(near, dist >= 0), (far, (dist >= 0) & (dist <= 128)), (far, (dist >= 0) & (dist % 4 == 0)),
             (far, (dist >= 0) & (dist % 16 == 0)), (far, dist >= 0)]
    out = np.zeros((33, len(kinds), TABLE_LEN), np.float32)
    for n, (b, ok) in enumerate(kinds):
        out[np.where(ok, b, 32), n, np.arange(TABLE_LEN)] = 1.0
    return out


def head_rows():
    out = np.zeros((P, H_FOX // 2), np.float32)
    for p in range(H_FOX // 2):
        for a in range(2):
            out[[a * HD + 2 * p + a, a * HD + 32 + 2 * p + a], p] = 1.0
    return out


class Stage:

    def __init__(self, nc, name, old):
        self.nc, self.name, self.old = nc, name, old
        self.own = []

    def __enter__(self):
        self.ctx = ExitStack()
        return self

    def __exit__(self, *exc):
        self.ctx.close()
        self.old[:] = self.own

    def sb(self, name, shape, dt=F32):
        return self.ctx.enter_context(self.nc.sbuf_tensor(f"{self.name}_{name}", shape, dt))

    def ps(self, name, banks):
        return self.ctx.enter_context(self.nc.psum_tensor(f"{self.name}_{name}", [P, banks, T], F32))

    def sem(self, name):
        s = self.ctx.enter_context(self.nc.semaphore(f"{self.name}_{name}"))
        self.own.append(s)
        return s

    def block(self):
        block = self.ctx.enter_context(self.nc.Block())
        if self.old:
            @block.gpsimd
            def _(pool):
                for s in self.old:
                    pool.sem_clear(s)
        return block


class Count:

    def __init__(self, eng, sem):
        self.eng, self.sem, self.base, self.n = eng, sem, 0, 0

    def add(self, instruction):
        instruction.then_inc(self.sem, 1)
        self.n += 1

    def settle(self):
        self.eng.wait_ge(self.sem, self.base + self.n)

    def link(self, instruction):
        self.add(instruction)
        self.settle()

    def enter(self, base):
        self.base, self.n = base, 0


def flat(ap):
    return ap.rearrange("p a b -> p (a b)")


def tile_of(tensor, t):
    return flat(tensor[:, bass.ds(t, 1), :]) if not isinstance(t, int) else tensor[:, t, :]


def rounds(eng, tiles, unroll, body):
    whole = tiles // unroll
    if whole > 1:
        with eng.Fori(0, whole) as g:
            for j in range(unroll):
                body(g * unroll + j, j, g)
    else:
        whole = 0
    for t in range(whole * unroll, tiles):
        body(t, t % unroll, t // unroll)



def column_products(nc, old, name, weights, tiles, kt, rhs, store, ring=4):
    with Stage(nc, name, old) as s:
        slots = s.sb("slots", [P, ring, kt, P])
        psum = s.ps("psum", ring)
        loaded = [s.sem(f"loaded{j}") for j in range(ring)]
        done, free = s.sem("done"), s.sem("free")
        block = s.block()

        @block.sync
        def _(sp):
            def load(t, j, r):
                sp.wait_ge(free, t + 1)
                sp.dma_start(slots[:, j], weights(t)).then_inc(loaded[j], 16)
            rounds(sp, tiles, ring, load)

        @block.tensor
        def _(pe):
            def multiply(t, j, r):
                pe.wait_ge(loaded[j], r * 16 + 16)
                pe.wait_ge(free, t + 1)
                for k in range(kt):
                    mm = pe.matmul(psum[:, j], slots[:, j, k], rhs(k), start=k == 0, stop=k == kt - 1)
                mm.then_inc(done, 1)
            rounds(pe, tiles, ring, multiply)

        @block.scalar
        def _(act):
            act.sem_inc(free, ring)
            def take(t, j, r):
                act.wait_ge(done, t + 1)
                store(act, t, psum[:, j]).then_inc(free, 1)
            rounds(act, tiles, ring, take)


def mixed_products(nc, old, name, h, jobs, width):
    ring = 3
    with Stage(nc, name, old) as s:
        slots = s.sb("slots", [P, ring, KD, width])
        psum = s.ps("psum", 4)
        loaded = [s.sem(f"loaded{j}") for j in range(ring)]
        done, stored = s.sem("done"), s.sem("stored")
        outs = []
        for n, (_, outputs) in enumerate(jobs):
            for o in outputs:
                if o[0] == "columns":
                    _, lhs, m, dst, func = o
                    outs.append((n, lambda k, n=n, lhs=lhs: lhs(slots[:, n % ring], k), lambda k: h[:, k, :],
                                 m, T, dst, func))
                else:
                    _, w, dsts, func = o
                    for i in range(TT):
                        outs.append((n, lambda k, i=i: h[:, k, i * P:(i + 1) * P],
                                     lambda k, n=n, w=w: slots[:, n % ring, k, 0:w], P, w, dsts[i], func))
        last = [max(i for i, o in enumerate(outs) if o[0] == n) for n in range(len(jobs))]
        landed = [16 * sum(len(jobs[m][0]) for m in range(n % ring, n + 1, ring)) for n in range(len(jobs))]
        block = s.block()

        @block.sync
        def _(sp):
            for n, (loads, _) in enumerate(jobs):
                if n >= ring:
                    sp.wait_ge(done, last[n - ring] + 1)
                for cols, src in loads:
                    sp.dma_start(slots[:, n % ring, :, cols], src).then_inc(loaded[n % ring], 16)

        @block.tensor
        def _(pe):
            for i, (n, lhs, rhs, m, w, _, _) in enumerate(outs):
                pe.wait_ge(loaded[n % ring], landed[n])
                if i >= 4:
                    pe.wait_ge(stored, i - 3)
                for k in range(KD):
                    mm = pe.matmul(psum[0:m, i % 4, 0:w], lhs(k), rhs(k), start=k == 0, stop=k == KD - 1)
                mm.then_inc(done, 1)

        @block.scalar
        def _(act):
            for i, (_, _, _, m, w, dst, func) in enumerate(outs):
                act.wait_ge(done, i + 1)
                act.activation(dst, psum[0:m, i % 4, 0:w], func).then_inc(stored, 1)



def normalise(nc, old, name, src, dst, gain, shift, add_to=None):
    with Stage(nc, name, old) as s:
        squares = s.sb("squares", [P, 2, T])
        rstd = s.sb("rstd", [P, T])
        logs = s.sb("logs", [P, T])
        scaled = s.sb("scaled", [P, 2, T])
        ones = s.sb("ones", [P, P])
        eps = s.sb("eps", [P, 1])
        psum = s.ps("psum", 1)
        const, squared, summed, rooted = s.sem("const"), s.sem("squared"), s.sem("summed"), s.sem("rooted")
        used, scaled_s, shifted = s.sem("used"), s.sem("scaled"), s.sem("shifted")
        block = s.block()

        @block.scalar
        def _(act):
            for k in range(KD):
                if k >= 2:
                    act.wait_ge(used, k - 1)
                act.activation(squares[:, k % 2], src(k), ACT.Square).then_inc(squared, 1)
            act.wait_ge(summed, 1)
            act.wait_ge(const, 2)
            act.activation(logs[:], psum[:, 0], ACT.Ln, bias=eps[:, 0:1], scale=1.0 / D).then_inc(rooted, 1)
            act.wait_ge(rooted, 1)
            act.activation(rstd[:], logs[:], ACT.Exp, scale=-0.5).then_inc(rooted, 1)
            if shift is not None:
                for k in range(KD):
                    act.wait_ge(scaled_s, k + 1)
                    act.activation(dst(k), scaled[:, k % 2], ACT.Identity, bias=shift(k)).then_inc(shifted, 1)

        @block.tensor
        def _(pe):
            pe.wait_ge(const, 2)
            for k in range(KD):
                pe.wait_ge(squared, k + 1)
                mm = pe.matmul(psum[:, 0], ones[:], squares[:, k % 2], start=k == 0, stop=k == KD - 1)
                mm.then_inc(used if k < KD - 1 else summed, 1)

        @block.vector
        def _(dve):
            dve.memset(ones[:], 1.0).then_inc(const, 1)
            dve.memset(eps[:], EPS).then_inc(const, 1)
            dve.wait_ge(rooted, 2)
            for k in range(KD):
                if shift is not None:
                    if k >= 2:
                        dve.wait_ge(shifted, k - 1)
                    out = scaled[:, k % 2]
                elif add_to is not None:
                    out = scaled[:, k % 2]
                else:
                    out = dst(k)
                dve.scalar_tensor_tensor(out, src(k), gain(k), rstd[:], ALU.mult, ALU.mult)\
                   .then_inc(scaled_s, 1)
                if add_to is not None:
                    dve.wait_ge(scaled_s, k + 1)
                    dve.tensor_tensor(add_to(k), add_to(k), scaled[:, k % 2], ALU.add).then_inc(shifted, 1)



def load_parameters(nc, old, rows, packs, columns, square, cst_square, x, x_t, extra):
    with Stage(nc, "setup", old) as s:
        xin = s.sb("x", [P, TT, D])
        stage = s.sb("rows", [P, len(packs), P])
        psum = s.ps("psum", 8)
        const, params, x_in = s.sem("const"), s.sem("params"), s.sem("x_in")
        turned, stored = s.sem("turned"), s.sem("stored")
        block = s.block()

        @block.sync
        def _(sp):
            sp.dma_start(square[:], cst_square).then_inc(const, 16)
            for i in range(TT):
                sp.dma_start(xin[:, i], x[i * P:(i + 1) * P, :]).then_inc(x_in, 16)

        @block.scalar
        def _(act):
            for pack, row, n, cols, src in rows:
                act.dma_start(stage[row:row + n, pack, cols], src).then_inc(params, 16)
            for dst, src in extra:
                act.dma_start(dst, src).then_inc(params, 16)
            act.wait_ge(params, 16 * (len(rows) + len(extra)))

        @block.tensor
        def _(pe):
            ident = square[:, IDENT]
            pe.wait_ge(const, 16)
            pe.wait_ge(x_in, 16 * TT)
            for k in range(KD):
                for i in range(TT):
                    mm = pe.transpose(psum[:, k % 4, i * P:(i + 1) * P], xin[:, i, k * P:(k + 1) * P], ident)
                mm.then_inc(turned, 1)
                if k >= 3 and k < KD - 1:
                    pe.wait_ge(stored, k - 2)
            pe.wait_ge(params, 16 * (len(rows) + len(extra)))
            for n, used in enumerate(packs):
                mm = pe.transpose(psum[:, 4 + n // 4, (n % 4) * P:(n % 4) * P + used], stage[0:used, n],
                                  ident[0:used, 0:used])
            mm.then_inc(turned, 1)

        @block.vector
        def _(dve):
            for k in range(KD):
                dve.wait_ge(turned, k + 1)
                dve.tensor_copy(x_t[:, k], psum[:, k % 4]).then_inc(stored, 1)
            dve.wait_ge(turned, KD + 1)
            for n, used in enumerate(packs):
                dve.tensor_copy(columns[:, n, 0:used], psum[:, 4 + n // 4, (n % 4) * P:(n % 4) * P + used])\
                   .then_inc(stored, 1)


def modulation(nc, old, c_col, ada_w, ada_b_col, mod):
    tiles, per, ring = 6 * KD, 4, 3
    loads = tiles // per
    with Stage(nc, "mod", old) as s:
        slots = s.sb("slots", [P, ring, KD, per * P])
        silu = s.sb("silu", [P, KD])
        psum = s.ps("psum", 1)
        loaded = [s.sem(f"loaded{j}") for j in range(ring)]
        act_done, done = s.sem("silu_done"), s.sem("done")
        block = s.block()

        @block.sync
        def _(sp):
            def load(t, j, r):
                sp.wait_ge(done, t + 1)
                sp.dma_start(slots[:, j], ada_w[:, :, bass.ds(t * (per * P), per * P)]).then_inc(loaded[j], 16)
            rounds(sp, loads, ring, load)

        @block.scalar
        def _(act):
            act.activation(silu[:], c_col, ACT.Silu).then_inc(act_done, 1)

        @block.tensor
        def _(pe):
            pe.sem_inc(done, ring)
            pe.wait_ge(act_done, 1)
            def multiply(t, j, r):
                pe.wait_ge(loaded[j], r * 16 + 16)
                for m in range(per):
                    for k in range(KD):
                        mm = pe.matmul(psum[:, 0, bass.ds(t * per + m, 1)], slots[:, j, k, m * P:(m + 1) * P],
                                       silu[:, k:k + 1], start=k == 0, stop=k == KD - 1)
                mm.then_inc(done, 1)
            rounds(pe, loads, ring, multiply)

        @block.vector
        def _(dve):
            dve.wait_ge(done, loads + ring)
            dve.tensor_tensor(mod[:], psum[:, 0, 0:tiles], ada_b_col, ALU.add)


def block_one_gains(nc, old, mod, norm_g, gains):
    with Stage(nc, "gains", old) as s:
        done = s.sem("done")
        block = s.block()

        @block.vector
        def _(dve):
            for n, (scale, one) in enumerate([(1, True), (2, False), (4, True), (5, False)]):
                part = mod[:, scale * KD:(scale + 1) * KD]
                dve.scalar_tensor_tensor(gains[:, n * KD:(n + 1) * KD], part, 1.0 if one else 0.0,
                                         norm_g[:, n * KD:(n + 1) * KD], ALU.add, ALU.mult).then_inc(done, 1)



CHUNK = P
NCH = T // CHUNK


def rwkv_inputs(nc, old, rw, cols, w_up, square, r_in, a_in, k_in, b_in, v_in, gate, bonus, tot, mid):
    with Stage(nc, "rwkv_in", old) as s:
        mixed = s.sb("mixed", [P, RW_TILES, T])
        diff = s.sb("diff", [P, T])
        low = s.sb("low", [P, T])
        rate = s.sb("rate", [P, 2, T])
        ld = s.sb("ld", [P, 2, T])
        run = s.sb("run", [P, 2, T])
        kk = s.sb("kk", [P, 2, T])
        work = s.sb("work", [P, 2, T])
        root = s.sb("root", [P, 2, T])
        e_pos = s.sb("e_pos", [P, 2, T])
        e_before = s.sb("e_before", [P, 2, T])
        e_neg = s.sb("e_neg", [P, 2, T])
        ones = s.sb("ones", [P, T])
        psum = s.ps("psum", 8)
        v, a, low_done, up_done, sums_done = (s.sem(n) for n in ("dve", "act", "low", "up", "sums"))
        block = s.block()

        @block.vector
        def _(dve):
            c = Count(dve, v)
            for t in [6, 0, 1, 2, 3, 4, 5]:
                c.link(dve.tensor_tensor(diff[:], rw[:, t, 0:T], rw[:, t, 1:T + 1], ALU.subtract))
                c.link(dve.scalar_tensor_tensor(mixed[:, t], diff[:], cols["mu"][:, t:t + 1], rw[:, t, 1:T + 1],
                                                ALU.mult, ALU.add))
            c.add(dve.memset(ones[:], 1.0))
            for t in range(2):
                c.link(dve.tensor_scalar(kk[:, t], mixed[:, 2 + t], cols["k_k"][:, t:t + 1], None, ALU.mult))
                c.link(dve.tensor_tensor(work[:, t], kk[:, t], kk[:, t], ALU.mult))
            dve.wait_ge(a, 3 + 4)
            for t in range(2):
                c.link(dve.tensor_scalar(ld[:, t], ld[:, t], -math.exp(-0.5), None, ALU.mult))
                for n in range(NCH):
                    part = slice(n * CHUNK, (n + 1) * CHUNK)
                    c.add(dve.tensor_tensor_scan(run[:, t, part], ones[:, part], ld[:, t, part], 0.0,
                                                 ALU.mult, ALU.add))
            c.settle()
            for t in range(2):
                ends = run[:, t].rearrange("p (n w) -> p n w", w=CHUNK)[:, :, CHUNK - 1]
                c.add(dve.tensor_scalar(tot[:, t], ends, 1.0, None, ALU.mult))
                c.link(dve.tensor_scalar(mid[:, t], ends, 0.5, None, ALU.mult))
                c.link(dve.tensor_tensor(run[:, t].rearrange("p (n w) -> p n w", w=CHUNK),
                                         run[:, t].rearrange("p (n w) -> p n w", w=CHUNK),
                                         mid[:, t].unsqueeze(2).to_broadcast([P, NCH, CHUNK]), ALU.subtract))
                c.link(dve.tensor_tensor(ld[:, t], run[:, t], ld[:, t], ALU.subtract))
            dve.wait_ge(sums_done, 1)
            for t in range(2):
                c.link(dve.tensor_scalar(work[:, t], psum[:, 4 + t], 1e-24, None, ALU.max))
            dve.wait_ge(a, 7 + 2)
            for t in range(2):
                c.link(dve.reciprocal(work[:, t], root[:, t]))
                c.link(dve.tensor_tensor(kk[:, t], kk[:, t], work[:, t], ALU.mult))
            dve.wait_ge(a, 9 + 6)
            for t in range(2):
                c.add(dve.tensor_tensor(r_in[:, t], mixed[:, t], e_pos[:, t], ALU.mult))
                c.link(dve.scalar_tensor_tensor(a_in[:, t], kk[:, t], -1.0, e_before[:, t], ALU.mult, ALU.mult))
                c.link(dve.tensor_tensor(kk[:, t], kk[:, t], rate[:, t], ALU.mult))
                c.add(dve.tensor_tensor(b_in[:, t], kk[:, t], e_neg[:, t], ALU.mult))
                c.link(dve.tensor_scalar(rate[:, t], rate[:, t], 1.0, None, ALU.subtract))
                c.link(dve.tensor_scalar(rate[:, t], rate[:, t], cols["k_a"][:, t:t + 1], 1.0, ALU.mult, ALU.add))
                c.link(dve.tensor_tensor(rate[:, t], rate[:, t], mixed[:, 2 + t], ALU.mult))
                c.add(dve.tensor_tensor(k_in[:, t], rate[:, t], e_neg[:, t], ALU.mult))
                c.link(dve.scalar_tensor_tensor(work[:, t], mixed[:, t], cols["r_k"][:, t:t + 1], rate[:, t],
                                                ALU.mult, ALU.mult))
                c.add(dve.tensor_copy(v_in[:, t], mixed[:, 4 + t]))
            dve.wait_ge(sums_done, 2)
            for t in range(2):
                c.add(dve.tensor_tensor(bonus[:, t], psum[:, 6 + t], mixed[:, 4 + t], ALU.mult))

        @block.scalar
        def _(act):
            c = Count(act, a)
            act.wait_ge(v, 2)
            c.add(act.activation(low[0:32], mixed[0:32, 6], ACT.Tanh))
            c.add(act.activation(low[32:64], mixed[32:64, 6], ACT.Identity))
            c.add(act.activation(low[64:128], mixed[64:128, 6], ACT.Sigmoid))
            act.wait_ge(up_done, 1)
            for t in range(2):
                c.add(act.activation(ld[:, t], psum[:, t], ACT.Sigmoid, bias=cols["w0"][:, t:t + 1]))
                c.add(act.activation(rate[:, t], psum[:, 2 + t], ACT.Sigmoid, bias=cols["a0"][:, t:t + 1]))
            act.wait_ge(v, 39)
            for t in range(2):
                c.add(act.activation(root[:, t], work[:, t], ACT.Sqrt))
            for t in range(2):
                c.add(act.activation(e_pos[:, t], run[:, t], ACT.Exp))
                c.add(act.activation(e_before[:, t], ld[:, t], ACT.Exp))
                c.add(act.activation(e_neg[:, t], run[:, t], ACT.Exp, scale=-1.0))
            act.wait_ge(up_done, 2)
            for t in range(2):
                c.add(act.activation(gate[:, t], psum[:, t], ACT.Copy))

        @block.tensor
        def _(pe):
            pe.wait_ge(a, 3)
            for t in range(2):
                c = slice(t * P, (t + 1) * P)
                pe.matmul(psum[:, t], w_up[0:32, c], low[0:32], start=True, stop=True)
                mm = pe.matmul(psum[:, 2 + t], w_up[32:64, c], low[32:64], start=True, stop=True)
            mm.then_inc(up_done, 1)
            pe.wait_ge(v, 19)
            for t in range(2):
                mm = pe.matmul(psum[:, 4 + t], square[:, HEADS], work[:, t], start=True, stop=True)
            mm.then_inc(sums_done, 1)
            pe.wait_ge(a, 7)
            for t in range(2):
                mm = pe.matmul(psum[:, t], w_up[64:128, t * P:(t + 1) * P], low[64:128], start=True, stop=True)
            mm.then_inc(up_done, 1)
            pe.wait_ge(v, 63)
            for t in range(2):
                mm = pe.matmul(psum[:, 6 + t], square[:, HEADS], work[:, t], start=True, stop=True)
            mm.then_inc(sums_done, 1)


def rwkv_chunks(nc, old, square, r_in, a_in, k_in, b_in, v_in, tot, mid, y):
    H = 4
    with Stage(nc, "rwkv", old) as s:
        ab = s.sb("ab", [P, NCH, H * P])
        ak = s.sb("ak", [P, NCH, H * P])
        rb = s.sb("rb", [P, NCH, H * P])
        rk = s.sb("rk", [P, NCH, H * P])
        tok = s.sb("tok", [P, NCH, 3, 2 * P])
        inv = s.sb("inv", [P, NCH, H * P])
        inv_t = s.sb("inv_t", [P, NCH, H * P])
        quarter = s.sb("quarter", [P, NCH, H * P])
        half = s.sb("half", [P, 2, H * P])
        state = s.sb("state", [P, 2, HD])
        centred = s.sb("centred", [P, 2, HD])
        z = s.sb("z", [P, H, HD])
        u = s.sb("u", [P, H, HD])
        factors = s.sb("factors", [P, 2, 2, NCH])
        psum = s.ps("psum", 8)
        g_done, g_kept, t_done, t_kept = s.sem("gram"), s.sem("gram_kept"), s.sem("turned"), s.sem("turned_kept")
        q_ready, h_done, h_kept, x_done, x_kept = (s.sem(n) for n in
                                                   ("quarter", "half", "half_kept", "inv", "inv_kept"))
        fac, c_done, c_kept = s.sem("factors"), s.sem("chain"), s.sem("chain_kept")
        y_done, y_kept = s.sem("y"), s.sem("y_kept")
        block = s.block()
        ident = square[:, IDENT]

        def rows(h):
            return slice(HD * (h % 2), HD * (h % 2) + HD)

        def cols(n):
            return slice(n * CHUNK, (n + 1) * CHUNK)

        def bank4(ap, h):
            return ap[:, h * P:(h + 1) * P]

        grams = [(ab, b_in, a_in, STRICT), (ak, k_in, a_in, STRICT), (rb, b_in, r_in, INCL), (rk, k_in, r_in, INCL)]

        def second_half(pe, i):
            level, n = divmod(i, NCH)
            pe.wait_ge(h_kept, i + 1)
            if i >= 1:
                pe.wait_ge(x_kept, 2 * i)
            for h in range(H):
                mm = pe.matmul(bank4(psum[:, 2], h), bank4(inv_t[:, n], h), bank4(half[:, i % 2], h),
                               start=True, stop=True)
            for h in range(H):
                mm = pe.matmul(bank4(psum[:, 3], h), bank4(half[:, i % 2], h), bank4(inv_t[:, n], h),
                               start=True, stop=True)
            mm.then_inc(x_done, 1)

        @block.tensor
        def _(pe):
            g = 0
            for dst, left, right, _ in grams:
                for n in range(NCH):
                    if g >= 2:
                        pe.wait_ge(g_kept, g - 1)
                    for h in range(H):
                        mm = pe.matmul(bank4(psum[:, 2 * (g % 2) + h % 2], h // 2), left[rows(h), h // 2, cols(n)],
                                       right[rows(h), h // 2, cols(n)], start=True, stop=True)
                    mm.then_inc(g_done, 1)
                    g += 1
            for i, src in enumerate((b_in, k_in, v_in)):
                for n in range(NCH):
                    q = i * NCH + n
                    if q >= 2:
                        pe.wait_ge(t_kept, q - 1)
                    for t in range(2):
                        mm = pe.transpose(psum[:, 4 + q % 2, t * P:(t + 1) * P], src[:, t, cols(n)], ident)
                    mm.then_inc(t_done, 1)
            pe.wait_ge(g_kept, 16)
            i = 0
            for level in range(7):
                for n in range(NCH):
                    pe.wait_ge(q_ready, i + 1)
                    if i >= NCH:
                        pe.wait_ge(x_kept, 2 * (i - NCH) + 2)
                    if i >= 2:
                        pe.wait_ge(h_kept, i - 1)
                    for h in range(H):
                        mm = pe.matmul(bank4(psum[:, i % 2], h), bank4(quarter[:, n], h), bank4(inv[:, n], h),
                                       start=True, stop=True)
                    mm.then_inc(h_done, 1)
                    if i >= 1:
                        second_half(pe, i - 1)
                    i += 1
            second_half(pe, i - 1)
            m = 0
            for n in range(NCH):
                pe.wait_ge(c_kept, 3 * n + 1)
                if n == 0:
                    pe.wait_ge(t_kept, 3 * NCH)
                    pe.wait_ge(x_kept, 2 * 7 * NCH)
                for h in range(H):
                    o = psum[:, h % 2, (h // 2) * HD:(h // 2 + 1) * HD]
                    pe.matmul(o, a_in[rows(h), h // 2, cols(n)], centred[rows(h), h // 2], start=True, stop=False)
                    mm = pe.matmul(o, bank4(ak[:, n], h), tok[:, n, 2, h * HD:(h + 1) * HD],
                                   start=False, stop=True)
                mm.then_inc(c_done, 1)
                pe.wait_ge(c_kept, 3 * n + 2)
                for h in range(H):
                    mm = pe.matmul(psum[:, 2, h * HD:(h + 1) * HD], bank4(inv_t[:, n], h), z[:, h],
                                   start=True, stop=True)
                mm.then_inc(c_done, 1)
                pe.wait_ge(c_kept, 3 * n + 3)
                for h in range(H):
                    o = psum[rows(h), 3, (h // 2) * HD:(h // 2 + 1) * HD]
                    pe.matmul(o, tok[:, n, 0, h * HD:(h + 1) * HD], u[:, h], start=True, stop=False)
                    mm = pe.matmul(o, tok[:, n, 1, h * HD:(h + 1) * HD], tok[:, n, 2, h * HD:(h + 1) * HD],
                                   start=False, stop=True)
                mm.then_inc(c_done, 1)
                if n >= 1:
                    pe.wait_ge(y_kept, n)
                for h in range(H):
                    o = psum[rows(h), 4 + h // 2, 0:P]
                    pe.matmul(o, centred[rows(h), h // 2], r_in[rows(h), h // 2, cols(n)], start=True, stop=False)
                    pe.matmul(o, u[:, h], bank4(rb[:, n], h), start=False, stop=False)
                    mm = pe.matmul(o, tok[:, n, 2, h * HD:(h + 1) * HD], bank4(rk[:, n], h),
                                   start=False, stop=True)
                mm.then_inc(y_done, 1)

        @block.scalar
        def _(act):
            for q in range(3 * NCH):
                act.wait_ge(t_done, q + 1)
                act.activation(tok[:, q % NCH, q // NCH], psum[:, 4 + q % 2, 0:2 * P], ACT.Copy).then_inc(t_kept, 1)
            act.activation(factors[:, 0].rearrange("p t n -> p (t n)"), mid[:].rearrange("p t n -> p (t n)"),
                           ACT.Exp).then_inc(fac, 1)
            act.activation(factors[:, 1].rearrange("p t n -> p (t n)"), tot[:].rearrange("p t n -> p (t n)"),
                           ACT.Exp).then_inc(fac, 1)
            for i in range(7 * NCH):
                act.wait_ge(h_done, i + 1)
                if i >= 2:
                    act.wait_ge(x_done, i - 1)
                act.activation(half[:, i % 2], psum[:, i % 2], ACT.Copy).then_inc(h_kept, 1)
            for n in range(NCH):
                act.wait_ge(y_done, n + 1)
                for t in range(2):
                    last = act.activation(y[:, t, cols(n)], psum[:, 4 + t, 0:P], ACT.Copy)
                last.then_inc(y_kept, 1)

        @block.gpsimd
        def _(pool):
            for i in range(7 * NCH):
                level, n = divmod(i, NCH)
                pool.wait_ge(g_kept, n + 1)
                if level:
                    pool.wait_ge(h_done, i - NCH + 1)
                pool.tensor_tensor(quarter[:, n].rearrange("p (h t) -> p h t", h=H),
                                   ab[:, n].rearrange("p (h t) -> p h t", h=H),
                                   square[:, LEVELS + level].unsqueeze(1).to_broadcast([P, H, P]), ALU.mult)\
                    .then_inc(q_ready, 1)

        @block.vector
        def _(dve):
            g = 0
            for n in range(NCH):
                for x in (inv, inv_t):
                    dve.tensor_copy(x[:, n].rearrange("p (h t) -> p h t", h=H),
                                    ident.unsqueeze(1).to_broadcast([P, H, P]))
            for dst, _, _, mask in grams:
                for n in range(NCH):
                    dve.wait_ge(g_done, g + 1)
                    for odd in range(2):
                        last = dve.tensor_tensor(
                            dst[:, n].rearrange("p (q r t) -> p r q t", q=2, r=2)[:, odd],
                            psum[:, 2 * (g % 2) + odd, 0:2 * P].rearrange("p (q t) -> p q t", q=2),
                            square[:, mask].unsqueeze(1).to_broadcast([P, 2, P]), ALU.mult)
                    last.then_inc(g_kept, 1)
                    g += 1
            for i in range(7 * NCH):
                n = i % NCH
                dve.wait_ge(x_done, i + 1)
                dve.tensor_tensor(inv[:, n], inv[:, n], psum[:, 2], ALU.add).then_inc(x_kept, 1)
                dve.tensor_tensor(inv_t[:, n], inv_t[:, n], psum[:, 3], ALU.add).then_inc(x_kept, 1)
            c = Count(dve, c_kept)
            dve.memset(state[:], 0.0)
            c.link(dve.memset(centred[:], 0.0))
            dve.wait_ge(fac, 2)
            for n in range(NCH):
                dve.wait_ge(c_done, 3 * n + 1)
                for odd in range(2):
                    last = dve.tensor_copy(z[:].rearrange("p (q r) d -> p r q d", r=2)[:, odd],
                                           psum[:, odd, 0:2 * HD].rearrange("p (q d) -> p q d", q=2))
                c.add(last)
                dve.wait_ge(c_done, 3 * n + 2)
                c.add(dve.tensor_copy(u[:].rearrange("p h d -> p (h d)"), psum[:, 2, 0:H * HD]))
                dve.wait_ge(c_done, 3 * n + 3)
                if n == NCH - 1:
                    break
                for t in range(2):
                    dve.tensor_scalar(state[:, t], state[:, t], factors[:, 1, t, n:n + 1], None, ALU.mult)\
                       .then_inc(fac, 1)
                dve.wait_ge(fac, 2 + 4 * n + 2)
                for t in range(2):
                    dve.scalar_tensor_tensor(state[:, t], psum[:, 3, t * HD:(t + 1) * HD],
                                             factors[:, 0, t, n:n + 1], state[:, t], ALU.mult, ALU.add)\
                       .then_inc(fac, 1)
                dve.wait_ge(fac, 2 + 4 * n + 4)
                dve.wait_ge(y_done, n + 1)
                dve.tensor_scalar(centred[:, 0], state[:, 0], factors[:, 0, 0, n + 1:n + 2], None, ALU.mult)
                c.add(dve.tensor_scalar(centred[:, 1], state[:, 1], factors[:, 0, 1, n + 1:n + 2], None, ALU.mult))


def rwkv_output(nc, old, y, gate, bonus, cols, square, out):
    with Stage(nc, "rwkv_out", old) as s:
        work = s.sb("work", [P, 2, T])
        rstd = s.sb("rstd", [P, 2, T])
        eps = s.sb("eps", [P, 1])
        psum = s.ps("psum", 4)
        v, a, m = s.sem("dve"), s.sem("act"), s.sem("sums")
        block = s.block()

        @block.tensor
        def _(pe):
            for t in range(2):
                pe.matmul(psum[:, t], square[:, HEADS], y[:, t], start=True, stop=True).then_inc(m, 1)
            for t in range(2):
                pe.wait_ge(a, t + 1)
                pe.matmul(psum[:, 2 + t], square[:, HEADS], work[:, t], start=True, stop=True).then_inc(m, 1)

        @block.scalar
        def _(act):
            c = Count(act, a)
            for t in range(2):
                act.wait_ge(v, 2 + t)
                c.add(act.activation(work[:, t], y[:, t], ACT.Square))
            for t in range(2):
                act.wait_ge(m, 3 + t)
                c.link(act.activation(rstd[:, t], psum[:, 2 + t], ACT.Ln, bias=eps[:, 0:1], scale=1.0 / HD))
            for t in range(2):
                c.link(act.activation(rstd[:, t], rstd[:, t], ACT.Exp, scale=-0.5))

        @block.vector
        def _(dve):
            c = Count(dve, v)
            c.link(dve.memset(eps[:], GN_EPS))
            for t in range(2):
                dve.wait_ge(m, t + 1)
                c.link(dve.scalar_tensor_tensor(y[:, t], psum[:, t], -1.0 / HD, y[:, t], ALU.mult, ALU.add))
            dve.wait_ge(a, 6)
            for t in range(2):
                c.link(dve.scalar_tensor_tensor(y[:, t], y[:, t], cols["ln_w"][:, t:t + 1], rstd[:, t],
                                                ALU.mult, ALU.mult))
                c.link(dve.scalar_tensor_tensor(y[:, t], y[:, t], cols["ln_b"][:, t:t + 1], bonus[:, t],
                                                ALU.add, ALU.add))
                c.link(dve.tensor_tensor(out[:, t], y[:, t], gate[:, t], ALU.mult))



def distance_tables(nc, old, onehot, bias, scratch, tables):
    kinds = [0] * H_NSA + [1] * 4 + [2] * 4 + [3] * 4 + [4] * (B_HEADS + C_HEADS + 1)
    groups, start = [], 0
    for h in range(1, N_TABLES + 1):
        if h == N_TABLES or kinds[h] != kinds[start]:
            groups.append((start, h, kinds[start]))
            start = h
    half = TABLE_LEN // 2
    with Stage(nc, "tables", old) as s:
        hot = s.sb("hot", [33, 5, TABLE_LEN])
        rows = s.sb("rows", [32, len(groups), TABLE_LEN])
        psum = s.ps("psum", 4)
        loaded, done, kept, out = s.sem("loaded"), s.sem("done"), s.sem("kept"), s.sem("out")
        block = s.block()

        @block.sync
        def _(sp):
            sp.dma_start(hot[:], onehot).then_inc(loaded, 16)
            for g, (a, b, _) in enumerate(groups):
                sp.wait_ge(kept, 2 * g + 2)
                sp.dma_start(scratch[a:b, :], rows[0:b - a, g]).then_inc(out, 16)
            sp.wait_ge(out, 16 * len(groups))
            for a in range(0, N_TABLES, 9):
                rows_at = scratch[a:a + 9, :]
                sp.dma_start(tables[a:a + 9], bass.AP(rows_at.tensor, rows_at.offset + P - 1,
                                                      [[TABLE_LEN, 9], [-1, P], [1, T]])).then_inc(out, 16)
            sp.wait_ge(out, 16 * (len(groups) + 3))

        @block.tensor
        def _(pe):
            pe.wait_ge(loaded, 16)
            for g, (a, b, kind) in enumerate(groups):
                for c in range(2):
                    i = 2 * g + c
                    if i >= 4:
                        pe.wait_ge(kept, i - 3)
                    pe.matmul(psum[0:b - a, i % 4, 0:half], bias[:, a:b], hot[:, kind, c * half:(c + 1) * half],
                              start=True, stop=True).then_inc(done, 1)

        @block.vector
        def _(dve):
            for g, (a, b, _) in enumerate(groups):
                for c in range(2):
                    i = 2 * g + c
                    dve.wait_ge(done, i + 1)
                    dve.tensor_copy(rows[0:b - a, g, c * half:(c + 1) * half], psum[0:b - a, i % 4, 0:half])\
                       .then_inc(kept, 1)


def table_tile(tables, head):
    return tables[bass.ds(head, 1)].rearrange("a p t -> (a p) t") if not isinstance(head, int) else tables[head]


class Piece:

    def __init__(self, q, k, v, lo, keys, table, extra=None, plus=None, table_no=0):
        self.q, self.k, self.v, self.lo, self.keys, self.table = q, k, v, lo, keys, table
        self.extra, self.plus, self.table_no = extra, plus, table_no


def attention(nc, old, name, pairs, units, width, tables, staging, finish, fixed_tables=False):
    pieces = [(u, c, piece) for u, unit in enumerate(units) for c, piece in enumerate(unit)]
    n_pieces, n_units = len(pieces), len(units)
    assert n_pieces % 4 == 0 and n_units % 8 == 0
    last_of = [max(i for i, (u, _, _) in enumerate(pieces) if u == w) for w in range(n_units)]
    first_of = [min(i for i, (u, _, _) in enumerate(pieces) if u == w) for w in range(n_units)]
    with Stage(nc, name, old) as s:
        scores = s.sb("scores", [P, 4, T])
        turned = s.sb("turned", [P, 2, T])
        peak = s.sb("peak", [P, 8, 4])
        sums = s.sb("sums", [P, 8, 4])
        weight = s.sb("weight", [P, 8])
        spacer = s.sb("spacer", [1, 8])
        psum = s.ps("psum", 8)
        staged = s.sem("staged")
        tabled = [s.sem(f"tabled{n}") for n in range(len(tables))]
        scored, biased, peaked, exped = s.sem("scored"), s.sem("biased"), s.sem("peaked"), s.sem("exped")
        turn, copied, weighed, finished = s.sem("turn"), s.sem("copied"), s.sem("weighed"), s.sem("finished")
        small, done = s.sem("small"), s.sem("done")
        block = s.block()
        n_staged = staging(None, 0, None) if staging else 0

        def over_pairs(eng, body):
            if pairs == 1:
                body(0)
            else:
                with eng.Fori(0, pairs) as p:
                    body(p)

        @block.sync
        def _(sp):
            def load(p):
                for n, (dst, src, last_unit) in enumerate(tables):
                    sp.wait_ge(biased, p * n_pieces + last_of[last_unit] + 1)
                    sp.dma_start(dst, src(p)).then_inc(tabled[n], 16)
            over_pairs(sp, load)

        @block.gpsimd
        def _(pool):
            if not staging:
                return
            def stage(p):
                pool.wait_ge(biased, p * n_pieces + n_pieces)
                staging(pool, p, staged)
            over_pairs(pool, stage)

        @block.tensor
        def _(pe):
            pe.sem_inc(turn, 4)
            pe.sem_inc(weighed, 2)

            def body(p):
                pe.wait_ge(staged, p * n_staged + n_staged)
                for i in range(n_pieces + 3):
                    if i < n_pieces:
                        u, c, x = pieces[i]
                        pe.wait_ge(biased, p * n_pieces + n_pieces + i - 3)
                        cols = slice(x.lo * P, x.lo * P + x.keys)
                        mm = pe.matmul(psum[:, i % 4, 0:x.keys], x.q, x.k[:, cols], start=True,
                                       stop=x.extra is None)
                        if x.extra is not None:
                            mm = pe.matmul(psum[:, i % 4, 0:x.keys], x.extra[0], x.extra[1][:, cols],
                                           start=False, stop=True)
                        mm.then_inc(scored, 1)
                    if 2 <= i < n_pieces + 2:
                        t = i - 2
                        x = pieces[t][2]
                        pe.wait_ge(exped, p * n_pieces + t + 1)
                        pe.wait_ge(copied, p * n_pieces + t + 1)
                        for j in range(-(-x.keys // P)):
                            n = min(P, x.keys - j * P)
                            mm = pe.transpose(psum[0:n, 4 + t % 2, j * P:j * P + P],
                                              scores[:, t % 4, j * P:j * P + n], attention.ident)
                        mm.then_inc(turn, 1)
                    if i >= 3:
                        t = i - 3
                        u, c, x = pieces[t]
                        pe.wait_ge(copied, p * n_pieces + t + 3)
                        if c == 0:
                            pe.wait_ge(finished, p * n_units + u + 1)
                        blocks = -(-x.keys // P)
                        for j in range(blocks):
                            n = min(P, x.keys - j * P)
                            mm = pe.matmul(psum[:, 6 + u % 2, 0:width],
                                           turned[0:n, t % 2, j * P:j * P + P], x.v(x.lo + j, p),
                                           start=c == 0 and j == 0, stop=t == last_of[u] and j == blocks - 1)
                        mm.then_inc(weighed, 1)
            over_pairs(pe, body)

        @block.scalar
        def _(act):
            act.sem_inc(copied, 2)

            def body(p):
                for i in range(n_pieces + 2):
                    if i >= 2:
                        t = i - 2
                        x = pieces[t][2]
                        act.wait_ge(turn, p * n_pieces + t + 5)
                        act.wait_ge(weighed, p * n_pieces + t + 1)
                        n = min(P, x.keys)
                        w = -(-x.keys // P) * P
                        act.activation(turned[0:n, t % 2, 0:w], psum[0:n, 4 + t % 2, 0:w], ACT.Copy)\
                           .then_inc(copied, 1)
                    if i < n_pieces:
                        u, c, x = pieces[i]
                        act.wait_ge(peaked, p * n_units + u + 1)
                        b = scores[:, i % 4, 0:x.keys]
                        act.activation(b, b, ACT.Exp, bias=peak[:, u % 8, 3:4],
                                       accum_out=sums[:, u % 8, c:c + 1]).then_inc(exped, 1)
            over_pairs(act, body)

        @block.vector
        def _(dve):
            dve.sem_inc(biased, n_pieces)
            dve.sem_inc(finished, 2)
            small_c, done_c = Count(dve, small), Count(dve, done)

            def end(p, u, count):
                dve.wait_ge(weighed, p * n_pieces + last_of[u] + 3)
                total = sums[:, u % 8, 0:1]
                for c in range(1, len(units[u])):
                    count.link(dve.tensor_tensor(total, total, sums[:, u % 8, c:c + 1], ALU.add))
                count.link(dve.tensor_scalar(total, total, 1e-30, None, ALU.max))
                count.link(dve.reciprocal(weight[:, u % 8:u % 8 + 1], total))
                finish(dve, p, u, psum[:, 6 + u % 2, 0:width], weight[:, u % 8:u % 8 + 1], count,
                       finished)

            def body(p):
                small_c.enter(p * body.per)
                for i in range(n_pieces + 4):
                    if i < n_pieces:
                        u, c, x = pieces[i]
                        if tables:
                            dve.wait_ge(tabled[x.table_no], p * 16 + 16)
                        dve.wait_ge(scored, p * n_pieces + i + 1)
                        dve.wait_ge(turn, p * n_pieces + i + 1)
                        raw = psum[:, i % 4, 0:x.keys]
                        out = scores[:, i % 4, 0:x.keys]
                        if x.plus is not None:
                            small_c.link(dve.tensor_tensor(out, raw, x.plus, ALU.add))
                            raw = out
                        dve.memset(spacer[:, i % 8:i % 8 + 1], 0.0)
                        dve.tensor_tensor_reduce(out, raw, x.table, 1.0, LOWEST, ALU.add, ALU.max,
                                                 peak[:, u % 8, c:c + 1]).then_inc(biased, 1)
                        if i == last_of[u]:
                            dve.wait_ge(biased, p * n_pieces + n_pieces + i + 1)
                            for d in range(1, c + 1):
                                small_c.link(dve.tensor_tensor(peak[:, u % 8, 0:1], peak[:, u % 8, 0:1],
                                                               peak[:, u % 8, d:d + 1], ALU.max))
                            dve.tensor_scalar(peak[:, u % 8, 3:4], peak[:, u % 8, 0:1], -1.0, None, ALU.mult)\
                               .then_inc(peaked, 1)
                    if i >= 4 and pieces[i - 4][0] in range(n_units) and last_of[pieces[i - 4][0]] == i - 4:
                        end(p, pieces[i - 4][0], small_c)
                body.made = small_c.n
            body.per = sum(len(x) - 1 for x in units) * 2 + 2 * n_units + sum(x.plus is not None for _, _, x in pieces)\
                + n_units * finish.steps
            over_pairs(dve, body)
            assert body.made == body.per, (body.made, body.per)


def to_channels(nc, old, name, ident, tiles, scale=1.0):
    with Stage(nc, name, old) as s:
        psum = s.ps("psum", 2)
        done, kept = s.sem("done"), s.sem("kept")
        block = s.block()

        @block.tensor
        def _(pe):
            for n, (src, _) in enumerate(tiles):
                if n >= 2:
                    pe.wait_ge(kept, n - 1)
                for i in range(TT):
                    mm = pe.transpose(psum[:, n % 2, i * P:(i + 1) * P], src[:, i], ident)
                mm.then_inc(done, 1)

        @block.scalar
        def _(act):
            for n, (_, dst) in enumerate(tiles):
                act.wait_ge(done, n + 1)
                act.activation(dst, psum[:, n % 2], ACT.Copy, scale=scale).then_inc(kept, 1)


def fox_decay(nc, old, logit, b_f, heads, left, right):
    with Stage(nc, "fox_decay", old) as s:
        x = s.sb("x", [H_FOX, T])
        e = s.sb("e", [H_FOX, T])
        n = s.sb("n", [H_FOX, T])
        ones = s.sb("ones", [H_FOX, T])
        v, a = s.sem("dve"), s.sem("act")
        block = s.block()
        r = slice(0, H_FOX)

        @block.vector
        def _(dve):
            c = Count(dve, v)
            c.add(dve.memset(left[:], 1.0))
            c.add(dve.memset(right[:], 1.0))
            c.add(dve.memset(ones[:], 1.0))
            c.link(dve.tensor_scalar(x[:], logit[0:H_FOX], b_f, None, ALU.add))
            c.link(dve.scalar_tensor_tensor(e[:], x[:], -1.0, x[:], ALU.mult, ALU.min))
            c.link(dve.tensor_scalar(x[:], x[:], 0.0, None, ALU.min))
            dve.wait_ge(a, 2)
            c.link(dve.tensor_tensor(n[:], x[:], e[:], ALU.subtract))
            c.link(dve.tensor_tensor_scan(left[0:H_FOX], ones[:], n[:], 0.0, ALU.mult, ALU.add))
            c.add(dve.tensor_copy(left[HD:HD + H_FOX], left[0:H_FOX]))
            for base in (32, HD + 32):
                c.add(dve.tensor_scalar(right[base:base + H_FOX], left[0:H_FOX], -1.0, None, ALU.mult))

        @block.scalar
        def _(act):
            act.wait_ge(v, 6)
            act.activation(e[:], e[:], ACT.Exp).then_inc(a, 1)
            act.wait_ge(a, 1)
            act.activation(e[:], e[:], ACT.Ln, bias=1.0).then_inc(a, 1)


def fox_attention(nc, old, pj, fv, left, right, heads, scratch, out):
    ctx = ExitStack()
    with ctx:
        qs = ctx.enter_context(nc.sbuf_tensor("fox_qs", [P, T], F32))
        ks = ctx.enter_context(nc.sbuf_tensor("fox_ks", [P, T], F32))
        rh = ctx.enter_context(nc.sbuf_tensor("fox_rh", [P, T], F32))
        table = ctx.enter_context(nc.sbuf_tensor("fox_table", [P, T], F32))

        def staging(pool, p, sem):
            if pool is None:
                return 3
            pool.tensor_tensor(qs[:], flat(pj[:, bass.ds(RW_TILES + p, 1), 1:T + 1]), attention.scale, ALU.mult)\
                .then_inc(sem, 1)
            pool.tensor_copy(ks[:], flat(pj[:, bass.ds(RW_TILES + 3 + p, 1), 1:T + 1])).then_inc(sem, 1)
            pool.tensor_tensor(rh[:], right[:], heads[:, bass.ds(p, 1)].to_broadcast([P, T]), ALU.mult).then_inc(sem, 1)

        units = []
        where = []
        for a in range(2):
            for i in reversed(range(TT)):
                q = slice(i * P, (i + 1) * P)
                h = slice(a * HD, (a + 1) * HD)
                units.append([Piece(qs[h, q], ks[h], lambda j, p, a=a: flat(fv[:, j:j + 1, bass.ds(p * P + a * HD, HD)]), 0, (i + 1) * P,
                                    table[:, (TT - 1 - i) * P:], extra=(left[h, q], rh[h]))])
                where.append((a, i))

        def finish(dve, p, u, o, w, count, sem):
            a, i = where[u]
            dve.tensor_scalar(out[:, i, bass.ds(p * P + a * HD, HD)], o, w, None, ALU.mult).then_inc(sem, 1)
        finish.steps = 0
        attention(nc, old, "fox", 3, units, HD, [(table[:], lambda p: table_tile(scratch, TAB_FOX), 7)],
                  staging, finish)


def nsa_compress(nc, old, nk, pe_cols, w1s, w2, kcmp, vcmp):
    with Stage(nc, "compress", old) as s:
        w1 = s.sb("w1", [P, 2, L_CMP, CMP_HID])
        hid = s.sb("hid", [P, 4, 32])
        pos = s.sb("pos", [P, 2])
        x = s.sb("x", [P, 4, 32])
        w = s.sb("w", [P, 4, 32])
        psum = s.ps("psum", 5)
        loaded, done, v, a, kept = s.sem("loaded"), s.sem("done"), s.sem("dve"), s.sem("act"), s.sem("kept")
        block = s.block()

        @block.sync
        def _(sp):
            for n in range(2):
                for g in range(2):
                    sp.dma_start(w1[g * HD:(g + 1) * HD, n], w1s[n]).then_inc(loaded, 16)

        @block.tensor
        def _(pe):
            pe.wait_ge(loaded, 64)
            for n in range(2):
                for g in range(2):
                    rows = slice(g * HD, (g + 1) * HD)
                    for l in range(L_CMP):
                        tokens = nk[rows, n, l:l + D_CMP * (N_CMP - 1) + 1:D_CMP]
                        mm = pe.matmul(psum[:, 2 * n + g, 0:N_CMP], w1[rows, n, l], tokens,
                                       start=l == 0, stop=l == L_CMP - 1)
                for l in range(L_CMP):
                    mm = pe.matmul(psum[:, 4, n:n + 1], w1[0:HD, n, l], pe_cols[0:HD, n, l:l + 1],
                                   start=l == 0, stop=l == L_CMP - 1)
                mm.then_inc(done, 1)
            pe.wait_ge(v, 7)
            for g in range(2):
                pe.matmul(psum[g * HD:(g + 1) * HD, 0, 0:N_CMP], w2[:, 0], hid[:, g, 0:N_CMP],
                          start=True, stop=True)
                mm = pe.matmul(psum[0:N_CMP, 1 + g, 0:HD], hid[:, 2 + g, 0:N_CMP], w2[:, 1], start=True, stop=True)
            mm.then_inc(done, 1)

        @block.vector
        def _(dve):
            c = Count(dve, v)
            dve.wait_ge(done, 2)
            c.link(dve.tensor_copy(pos[:], psum[:, 4, 0:2]))
            for n in range(2):
                c.add(dve.tensor_scalar(x[:, 2 * n:2 * n + 2, 0:N_CMP], psum[:, 2 * n:2 * n + 2, 0:N_CMP],
                                        pos[:, n:n + 1], None, ALU.add))
            c.settle()
            xv, wv = x[:, :, 0:N_CMP], w[:, :, 0:N_CMP]
            c.link(dve.tensor_tensor(wv, xv, xv, ALU.mult))
            c.link(dve.tensor_scalar(wv, wv, 0.044715, 1.0, ALU.mult, ALU.add))
            c.link(dve.tensor_tensor(wv, wv, xv, ALU.mult))
            dve.wait_ge(a, 1)
            c.link(dve.tensor_tensor(hid[:, :, 0:N_CMP], wv, xv, ALU.mult))
            dve.wait_ge(done, 3)
            dve.tensor_copy(kcmp[:], psum[:, 0, 0:N_CMP])
            dve.tensor_copy(vcmp[:, 0], psum[0:N_CMP, 1, 0:HD])
            dve.tensor_copy(vcmp[:, 1], psum[0:N_CMP, 2, 0:HD]).then_inc(kept, 1)

        @block.scalar
        def _(act):
            act.wait_ge(v, 6)
            act.activation(w[:, :, 0:N_CMP], w[:, :, 0:N_CMP], ACT.Sigmoid, scale=2.0 * math.sqrt(2.0 / math.pi))\
               .then_inc(a, 1)


def nsa_attention(nc, old, nq, nk, nv, kcmp, vcmp, gates, scratch, out):
    with ExitStack() as ctx:
        qs = ctx.enter_context(nc.sbuf_tensor("nsa_qs", [P, T], F32))
        tables = ctx.enter_context(nc.sbuf_tensor("nsa_tables", [P, 2, T], F32))
        scaled = ctx.enter_context(nc.sbuf_tensor("nsa_scaled", [P, 4], F32))

        def staging(pool, p, sem):
            if pool is None:
                return 1
            pool.tensor_tensor(qs[:], tile_of(nq, p), attention.scale, ALU.mult).then_inc(sem, 1)

        units, where = [], []
        for a in range(2):
            h = slice(a * HD, (a + 1) * HD)
            for i in reversed(range(TT)):
                q = slice(i * P, (i + 1) * P)
                full = tables[:, a, (TT - 1 - i) * P:]
                n_c = 8 * i + 7
                first = (TT - 1 - i) * P + L_CMP - 1
                coarse = tables[:, a, first:first + D_CMP * (n_c - 1) + 1:D_CMP]
                units.append([Piece(qs[h, q], kcmp[h], lambda j, p, a=a, n=n_c: vcmp[0:n, a], 0, n_c, coarse, table_no=a)])
                units.append([Piece(qs[h, q], nk[h, 2], lambda j, p, h=h: nv[:, 0, j, h], 0, (i + 1) * P, full, table_no=a)])
                units.append([Piece(qs[h, q], nk[h, 3], lambda j, p, h=h: nv[:, 1, j, h], 0, (i + 1) * P, full, table_no=a)])
                where += [(a, i, b) for b in range(3)]

        def finish(dve, p, u, o, w, count, sem):
            a, i, b = where[u]
            dst = out[:, i, bass.ds(p * HD + a * 3 * HD, HD)]
            g = scaled[:, u % 4:u % 4 + 1]
            count.link(dve.tensor_tensor(g, w, flat(gates[:, i:i + 1, bass.ds(p * 3 + a * 9 + b, 1)]), ALU.mult))
            if b == 0:
                dve.tensor_scalar(dst, o, g, None, ALU.mult).then_inc(sem, 1)
            else:
                dve.wait_ge(sem, p * len(units) + u + 2)
                dve.scalar_tensor_tensor(dst, o, g, dst, ALU.mult, ALU.add).then_inc(sem, 1)
        finish.steps = 1
        attention(nc, old, "nsa", 3, units, HD,
                  [(tables[:, a], lambda p, a=a: table_tile(scratch, p + 3 * a), 12 * a + 11) for a in range(2)],
                  staging, finish)



def conv_hidden(nc, old, h, up, conv, hidden):
    ring = 4
    with Stage(nc, "conv_up", old) as s:
        slots = s.sb("slots", [P, ring, KD, 2, P])
        mixed = s.sb("mixed", [P, 2, 2, T])
        gate = s.sb("gate", [P, 2, T])
        psum = s.ps("psum", 8)
        loaded = [s.sem(f"loaded{j}") for j in range(ring)]
        done, based, first, convolved, gated, made = (s.sem(n) for n in
                                                      ("done", "based", "first", "convolved", "gated", "made"))
        block = s.block()
        halves = up.rearrange("k (w n) -> k w n", w=2).rearrange("(k p) w n -> p k w n", p=P)

        @block.sync
        def _(sp):
            def load(t, j, r):
                sp.wait_ge(made, t + 1)
                for w in range(2):
                    sp.dma_start(slots[:, j, :, w], halves[:, :, w, bass.ds(t * P, P)]).then_inc(loaded[j], 16)
            rounds(sp, KF, ring, load)

        @block.tensor
        def _(pe):
            def multiply(t, j, r):
                pe.wait_ge(loaded[j], r * 32 + 32)
                pe.wait_ge(made, t + 1)
                for w in range(2):
                    for k in range(KD):
                        mm = pe.matmul(psum[:, 2 * j + w], slots[:, j, k, w], h[:, k], start=k == 0,
                                       stop=k == KD - 1)
                    mm.then_inc(done, 1)
            rounds(pe, KF, ring, multiply)

        @block.scalar
        def _(act):
            def take(t, j, r):
                b = j % 2
                for w in range(2):
                    act.wait_ge(done, t * 2 + w + 1)
                    act.wait_ge(made, t + 3)
                    act.activation(mixed[:, b, w], psum[:, 2 * j + w], ACT.Identity,
                                   bias=conv(t, w, 3), scale=conv(t, w, 2)).then_inc(based, 1)
                act.wait_ge(convolved, t * 2 + 1)
                act.activation(gate[:, b], mixed[:, b, 0], ACT.Silu).then_inc(gated, 1)
            rounds(act, KF, ring, take)

        @block.vector
        def _(dve):
            dve.sem_inc(made, ring)

            def convolve(t, j, r):
                b = j % 2
                for w in range(2):
                    dve.wait_ge(based, t * 2 + w + 1)
                    m = mixed[:, b, w]
                    dve.scalar_tensor_tensor(m[:, 1:T], psum[:, 2 * j + w, 0:T - 1], conv(t, w, 1), m[:, 1:T],
                                             ALU.mult, ALU.add).then_inc(first, 1)
                    dve.wait_ge(first, t * 2 + w + 1)
                    dve.scalar_tensor_tensor(m[:, 2:T], psum[:, 2 * j + w, 0:T - 2], conv(t, w, 0), m[:, 2:T],
                                             ALU.mult, ALU.add).then_inc(convolved, 1)
                dve.wait_ge(convolved, t * 2 + 2)
                dve.wait_ge(gated, t + 1)
                dve.tensor_tensor(tile_of(hidden, t), gate[:, b], mixed[:, b, 1], ALU.mult).then_inc(made, 1)
            rounds(dve, KF, ring, convolve)


def glu_hidden(nc, old, name, h, w_gate, w_up, hidden):
    ring = 4
    with Stage(nc, name, old) as s:
        slots = s.sb("slots", [P, ring, KD, 2, P])
        gate = s.sb("gate", [P, 2, T])
        psum = s.ps("psum", 8)
        loaded = [s.sem(f"loaded{j}") for j in range(ring)]
        done, gated, made = s.sem("done"), s.sem("gated"), s.sem("made")
        block = s.block()
        sources = [w.rearrange("(k p) n -> p k n", p=P) for w in (w_gate, w_up)]

        @block.sync
        def _(sp):
            def load(t, j, r):
                sp.wait_ge(made, t + 1)
                for w in range(2):
                    sp.dma_start(slots[:, j, :, w], sources[w][:, :, bass.ds(t * P, P)]).then_inc(loaded[j], 16)
            rounds(sp, KF, ring, load)

        @block.tensor
        def _(pe):
            def multiply(t, j, r):
                pe.wait_ge(loaded[j], r * 32 + 32)
                pe.wait_ge(made, t + 1)
                for w in range(2):
                    for k in range(KD):
                        mm = pe.matmul(psum[:, 2 * j + w], slots[:, j, k, w], h[:, k], start=k == 0,
                                       stop=k == KD - 1)
                    mm.then_inc(done, 1)
            rounds(pe, KF, ring, multiply)

        @block.scalar
        def _(act):
            def take(t, j, r):
                act.wait_ge(done, t * 2 + 1)
                act.wait_ge(made, t + 3)
                act.activation(gate[:, j % 2], psum[:, 2 * j], ACT.Silu).then_inc(gated, 1)
            rounds(act, KF, ring, take)

        @block.vector
        def _(dve):
            dve.sem_inc(made, ring)

            def combine(t, j, r):
                dve.wait_ge(done, t * 2 + 2)
                dve.wait_ge(gated, t + 1)
                dve.tensor_tensor(tile_of(hidden, t), gate[:, j % 2], psum[:, 2 * j + 1], ALU.mult).then_inc(made, 1)
            rounds(dve, KF, ring, combine)



def view(w):
    return w.rearrange("(k p) n -> p k n", p=P)


def first_block(nc, old, keep, A, x_t, h, gains, mod, cols, square, scratch, heads, b_f):
    with ExitStack() as top:
        def sb(name, shape):
            return top.enter_context(nc.sbuf_tensor("one_" + name, shape, F32))

        y_t = sb("y_t", [P, KD, T])
        w_in = view(A["w_in"][0])
        normalise(nc, old, "norm0", lambda k: x_t[:, k], lambda k: h[:, k], lambda k: gains[:, k:k + 1],
                  lambda k: mod[:, k:k + 1])
        with ExitStack() as mix:
            def mb(name, shape):
                return mix.enter_context(nc.sbuf_tensor("mix_" + name, shape, F32))
            nq = mb("nq", [P, 3, T])
            nk = mb("nk", [P, 4, T])
            nv = mb("nv", [P, 2, TT, P])
            gates = mb("gates", [P, TT, 3 * H_NSA])
            fv = mb("fv", [P, TT, C_FOX])
            logit = mb("logit", [H_FOX, T])
            pj = mb("pj", [P, RW_TILES + 6, T + 1])

            with Stage(nc, "zero", old) as s:
                block = s.block()
                @block.vector
                def _(dve):
                    dve.memset(pj[:, :, 0:1], 0.0)

            def store(act, t, psum):
                dst = pj[:, t, 1:T + 1] if isinstance(t, int) else flat(pj[:, bass.ds(t, 1), 1:T + 1])
                return act.activation(dst, psum, ACT.Copy)
            column_products(nc, old, "in_a", lambda t: w_in[:, :, bass.ds(t * P, P)], RW_TILES + 6, KD,
                            lambda k: h[:, k], store)

            def cm(tiles, dst, m=P):
                return [("columns", lambda slot, k, c=c: slot[:, k, c * P:c * P + m], m, dst(c), ACT.Copy)
                        for c in range(tiles)]
            jobs = [
                ([(slice(0, C_FOX), w_in[:, :, FOX_V:FOX_V + C_FOX])],
                 [("tokens", C_FOX, [fv[:, i] for i in range(TT)], ACT.Copy)]),
                ([(slice(c * P + g * HD, c * P + (g + 1) * HD),
                   w_in[:, :, NSA_Q + (g * 3 + c) * HD:NSA_Q + (g * 3 + c + 1) * HD]) for c in range(3) for g in range(2)],
                 cm(3, lambda c: nq[:, c])),
                ([(slice(0, 3 * P), w_in[:, :, NSA_KC:NSA_KC + 3 * P])], cm(3, lambda c: nk[:, c])),
                ([(slice(0, P), w_in[:, :, NSA_KW:NSA_KW + P])], cm(1, lambda c: nk[:, 3])),
                ([(slice(0, P), w_in[:, :, NSA_VS:NSA_VS + P])],
                 [("tokens", P, [nv[:, 0, i] for i in range(TT)], ACT.Copy)]),
                ([(slice(0, P), w_in[:, :, NSA_VW:NSA_VW + P])],
                 [("tokens", P, [nv[:, 1, i] for i in range(TT)], ACT.Copy)]),
                ([(slice(0, H_FOX), w_in[:, :, FOX_F:FOX_F + H_FOX])],
                 cm(1, lambda c: logit[0:H_FOX], m=H_FOX)),
                ([(slice(0, 3 * H_NSA), w_in[:, :, NSA_GATE:NSA_GATE + 3 * H_NSA])],
                 [("tokens", 3 * H_NSA, [gates[:, i] for i in range(TT)], ACT.Sigmoid)]),
            ]
            mixed_products(nc, old, "in_b", h, jobs, 3 * P)

            with ExitStack() as ctx:
                def b(name, shape):
                    return ctx.enter_context(nc.sbuf_tensor("rw_" + name, shape, F32))
                gate, bonus, v_in = b("gate", [P, 2, T]), b("bonus", [P, 2, T]), b("v", [P, 2, T])
                yr = y_t[:, 0:2]
                r_in, a_in, k_in, b_in = (h[:, 2 * n:2 * n + 2] for n in range(4))
                tot, mid = b("tot", [P, 2, NCH]), b("mid", [P, 2, NCH])
                with nc.sbuf_tensor("rw_up", [P, C_RWKV], F32) as w_up:
                    with Stage(nc, "load_up", old) as s:
                        sem = s.sem("loaded")
                        block = s.block()
                        @block.sync
                        def _(sp):
                            sp.dma_start(w_up[0:32], A["rwkv_w_up"][0]).then_inc(sem, 16)
                            sp.dma_start(w_up[32:64], A["rwkv_a_up"][0]).then_inc(sem, 16)
                            sp.dma_start(w_up[64:128], A["rwkv_g_up"][0]).then_inc(sem, 16)
                            sp.wait_ge(sem, 48)
                    rwkv_inputs(nc, old, pj, cols, w_up, square, r_in, a_in, k_in, b_in, v_in, gate, bonus, tot, mid)
                rwkv_chunks(nc, old, square, r_in, a_in, k_in, b_in, v_in, tot, mid, yr)
                rwkv_output(nc, old, yr, gate, bonus, cols, square, y_t)

            with nc.sbuf_tensor("fox_tok", [P, TT, C_FOX], F32) as tok:
                with nc.sbuf_tensor("fox_left", [P, T], F32) as left, nc.sbuf_tensor("fox_right", [P, T], F32) as right:
                    fox_decay(nc, old, logit, b_f, heads, left, right)
                    fox_attention(nc, old, pj, fv, left, right, heads, scratch, tok)
                to_channels(nc, old, "fox_turn", square[:, IDENT],
                            [(tok[:, :, c * P:(c + 1) * P], y_t[:, 2 + c]) for c in range(3)])
            with nc.sbuf_tensor("nsa_tok", [P, TT, C_NSA], F32) as tok, nc.sbuf_tensor("nsa_kcmp", [P, N_CMP], F32) as kcmp, \
                    nc.sbuf_tensor("nsa_vcmp", [N_CMP, 2, HD], F32) as vcmp:
                with nc.sbuf_tensor("nsa_w2", [P, 2, HD], F32) as w2:
                    with Stage(nc, "load_w2", old) as s:
                        sem = s.sem("loaded")
                        block = s.block()
                        @block.sync
                        def _(sp):
                            for n, w in enumerate(("nsa_ck_w2", "nsa_cv_w2")):
                                sp.dma_start(w2[:, n], A[w][0]).then_inc(sem, 16)
                            sp.wait_ge(sem, 32)
                    nsa_compress(nc, old, nk, cols["pe"], [A[w][0].rearrange("(l d) c -> d l c", d=HD) for w in
                                                          ("nsa_ck_w1", "nsa_cv_w1")], w2, kcmp, vcmp)
                nsa_attention(nc, old, nq, nk, nv, kcmp, vcmp, gates, scratch, tok)
                to_channels(nc, old, "nsa_turn", square[:, IDENT],
                            [(tok[:, :, c * P:(c + 1) * P], y_t[:, 5 + c]) for c in range(3)])
        project_and_add(nc, old, "out1", A["w_out"][0], KD, lambda k: y_t[:, k], x_t, lambda k: gains[:, KD + k:KD + k + 1])
        normalise(nc, old, "norm2", lambda k: x_t[:, k], lambda k: h[:, k], lambda k: gains[:, 2 * KD + k:2 * KD + k + 1],
                  lambda k: mod[:, 3 * KD + k:3 * KD + k + 1])
    with nc.sbuf_tensor("hidden1", [P, KF, T], F32) as hidden:
        conv_hidden(nc, old, h, A["ffn_up"][0], cols["conv"], hidden)
        project_and_add(nc, old, "down1", A["ffn_down"][0], KF, lambda k: hidden[:, k], x_t,
                        lambda k: gains[:, 3 * KD + k:3 * KD + k + 1])


def project_and_add(nc, old, name, w, kt, rhs, x_t, gain):
    with nc.sbuf_tensor(name + "_y", [P, KD, T], F32) as y:
        def store(act, t, psum):
            return act.activation(tile_of(y, t), psum, ACT.Copy)
        wv = view(w)
        column_products(nc, old, name, lambda t: wv[:, :, bass.ds(t * P, P)], KD, kt, rhs, store)
        normalise(nc, old, name + "_norm", lambda k: y[:, k], None, gain, None, add_to=lambda k: x_t[:, k])



def head_norms(nc, old, tiles, gain, square):
    with Stage(nc, "head_norms", old) as s:
        squares = s.sb("squares", [P, 2, T])
        rstd = s.sb("rstd", [P, 2, T])
        eps = s.sb("eps", [P, 1])
        psum = s.ps("psum", 4)
        const, squared, summed, logged, rooted, done = (s.sem(n) for n in
                                                        ("const", "squared", "summed", "logged", "rooted", "done"))
        block = s.block()
        n_tiles = len(tiles)

        @block.scalar
        def _(act):
            act.wait_ge(const, 1)
            for n in range(n_tiles + 1):
                if n < n_tiles:
                    if n >= 2:
                        act.wait_ge(summed, n - 1)
                    act.activation(squares[:, n % 2], tiles[n], ACT.Square).then_inc(squared, 1)
                if n >= 1:
                    m = n - 1
                    act.wait_ge(summed, m + 1)
                    if m >= 2:
                        act.wait_ge(done, m - 1)
                    act.activation(rstd[:, m % 2], psum[:, m % 4], ACT.Ln, bias=eps[:, 0:1], scale=1.0 / HD)\
                       .then_inc(logged, 1)
                    act.wait_ge(logged, m + 1)
                    act.activation(rstd[:, m % 2], rstd[:, m % 2], ACT.Exp, scale=-0.5).then_inc(rooted, 1)

        @block.tensor
        def _(pe):
            for n in range(n_tiles):
                pe.wait_ge(squared, n + 1)
                if n >= 4:
                    pe.wait_ge(rooted, n - 3)
                pe.matmul(psum[:, n % 4], square[:, HEADS], squares[:, n % 2], start=True, stop=True)\
                  .then_inc(summed, 1)

        @block.vector
        def _(dve):
            dve.memset(eps[:], EPS).then_inc(const, 1)
            for n in range(n_tiles):
                dve.wait_ge(rooted, n + 1)
                dve.scalar_tensor_tensor(tiles[n], tiles[n], gain(n), rstd[:, n % 2], ALU.mult, ALU.mult)\
                   .then_inc(done, 1)


def dilated_attention(nc, old, qa, va, tables_dram, out):
    with ExitStack() as ctx:
        qs = ctx.enter_context(nc.sbuf_tensor("dil_qs", [P, 3, T], F32))
        ks = ctx.enter_context(nc.sbuf_tensor("dil_ks", [P, 3, T], F32))
        tables = ctx.enter_context(nc.sbuf_tensor("dil_tables", [P, 2, 3, T], F32))

        def staging(pool, p, sem):
            if pool is None:
                return 6
            for g in range(3):
                pool.tensor_tensor(qs[:, g], tile_of(qa, p + 2 * g), attention.scale, ALU.mult).then_inc(sem, 1)
                pool.tensor_copy(ks[:, g], tile_of(qa, p + 6 + 2 * g)).then_inc(sem, 1)

        units, where = [], []
        for a in range(2):
            h = slice(a * HD, (a + 1) * HD)
            for i in reversed(range(TT)):
                unit = []
                for g in range(3):
                    lo = max(0, i - 1) if g == 0 else 0
                    unit.append(Piece(
                        qs[h, g, i * P:(i + 1) * P], ks[h, g],
                        lambda j, p, a=a, g=g: flat(va[:, j:j + 1, bass.ds(p * P + (4 * g + a) * HD, HD)]),
                        lo, (i + 1 - lo) * P, tables[:, a, g, (TT - 1 - i + lo) * P:], table_no=3 * a + g))
                units.append(unit)
                where.append((a, i))

        def finish(dve, p, u, o, w, count, sem):
            a, i = where[u]
            dve.tensor_scalar(out[:, i, bass.ds(p * P + a * HD, HD)], o, w, None, ALU.mult).then_inc(sem, 1)
        finish.steps = 0
        attention(nc, old, "dil", 2, units, HD,
                  [(tables[:, a, g], lambda p, a=a, g=g: table_tile(tables_dram, p * 2 + (TAB_A + 4 * g + a)), 4 * a + 3)
                   for a in range(2) for g in range(3)], staging, finish)


def diff_attention(nc, old, qb, vb, minus_lam, tables_dram, out):
    with ExitStack() as ctx:
        qs = ctx.enter_context(nc.sbuf_tensor("diff_qs", [P, 2, T], F32))
        ks = ctx.enter_context(nc.sbuf_tensor("diff_ks", [P, 2, T], F32))
        tables = ctx.enter_context(nc.sbuf_tensor("diff_tables", [P, 2, T], F32))
        scaled = ctx.enter_context(nc.sbuf_tensor("diff_scaled", [P, 4], F32))

        def staging(pool, p, sem):
            if pool is None:
                return 4
            for m in range(2):
                pool.tensor_tensor(qs[:, m], tile_of(qb, p + 2 * m), attention.scale, ALU.mult).then_inc(sem, 1)
                pool.tensor_copy(ks[:, m], tile_of(qb, p + 4 + 2 * m)).then_inc(sem, 1)

        units, where = [], []
        for a in range(2):
            h = slice(a * HD, (a + 1) * HD)
            for i in reversed(range(TT)):
                for m in range(2):
                    units.append([Piece(
                        qs[h, m, i * P:(i + 1) * P], ks[h, m],
                        lambda j, p, a=a: flat(vb[:, j:j + 1, bass.ds(p * 2 * P + a * P, P)]),
                        0, (i + 1) * P, tables[:, a, (TT - 1 - i) * P:], table_no=a)])
                    where.append((a, i, m))

        def finish(dve, p, u, o, w, count, sem):
            a, i, m = where[u]
            dst = out[:, i, bass.ds(p * 2 * P + a * P, P)]
            g = scaled[:, u % 4:u % 4 + 1]
            count.link(dve.tensor_scalar(g, w, minus_lam if m else 1.0, None, ALU.mult))
            if m == 0:
                dve.tensor_scalar(dst, o, g, None, ALU.mult).then_inc(sem, 1)
            else:
                dve.wait_ge(sem, p * len(units) + u + 2)
                dve.scalar_tensor_tensor(dst, o, g, dst, ALU.mult, ALU.add).then_inc(sem, 1)
        finish.steps = 1
        attention(nc, old, "diff", 2, units, P,
                  [(tables[:, a], lambda p, a=a: table_tile(tables_dram, p * 2 + TAB_B + a), 8 * a + 7)
                   for a in range(2)], staging, finish)


def diff_factor(nc, old, lam_in, minus_lam):
    with Stage(nc, "lam", old) as s:
        prod = s.sb("prod", [P, 2, HD])
        sums = s.sb("sums", [P, 2])
        v, a = s.sem("dve"), s.sem("act")
        block = s.block()
        lv = lam_in[:].rearrange("p (m t d) -> p m t d", m=2, t=2)

        @block.vector
        def _(dve):
            c = Count(dve, v)
            c.link(dve.tensor_tensor(prod[:], lv[:, :, 0], lv[:, :, 1], ALU.mult))
            c.link(dve.tensor_reduce(sums[:], prod[:], AX.X, ALU.add))
            dve.wait_ge(a, 1)
            c.link(dve.tensor_tensor(minus_lam[:], sums[:, 1:2], sums[:, 0:1], ALU.subtract))
            c.link(dve.tensor_scalar(minus_lam[:], minus_lam[:], -LAM_INIT, None, ALU.add))

        @block.scalar
        def _(act):
            act.wait_ge(v, 2)
            act.activation(sums[:], sums[:], ACT.Exp).then_inc(a, 1)


def diff_norm(nc, old, tok):
    with Stage(nc, "diff_norm", old) as s:
        squares = s.sb("squares", [P, TT, B_HEADS, P])
        rstd = s.sb("rstd", [P, TT, B_HEADS])
        v, a = s.sem("dve"), s.sem("act")
        eps = s.sb("eps", [P, 1])
        block = s.block()
        view4 = tok[:].rearrange("p i (h d) -> p (i h) d", h=B_HEADS)
        sq = squares[:].rearrange("p i h d -> p (i h) d")
        r = rstd[:].rearrange("p i h -> p (i h)")

        @block.vector
        def _(dve):
            c = Count(dve, v)
            c.add(dve.memset(eps[:], EPS))
            dve.wait_ge(a, 1)
            c.link(dve.tensor_reduce(r, sq, AX.X, ALU.add))
            dve.wait_ge(a, 3)
            c.link(dve.tensor_tensor(view4, view4, r.unsqueeze(2).to_broadcast([P, TT * B_HEADS, P]), ALU.mult))
            c.link(dve.tensor_scalar(view4, view4, 1.0 - LAM_INIT, None, ALU.mult))

        @block.scalar
        def _(act):
            act.activation(sq, view4, ACT.Square).then_inc(a, 1)
            act.wait_ge(v, 2)
            act.activation(r, r, ACT.Ln, bias=eps[:, 0:1], scale=1.0 / P).then_inc(a, 1)
            act.wait_ge(a, 2)
            act.activation(r, r, ACT.Exp, scale=-0.5).then_inc(a, 1)


def select_keys(nc, old, qi, ki, w_idx, causal, penalty):
    rounds_of_8 = TOPK // 8
    with Stage(nc, "select", old) as s:
        relu = s.sb("relu", [P, 4, T])
        score = s.sb("score", [P, T])
        left = s.sb("left", [P, 2, T])
        top = s.sb("top", [P, 8])
        above = s.sb("above", [P, T])
        equal = s.sb("equal", [P, T])
        place = s.sb("place", [P, T])
        ones = s.sb("ones", [P, T])
        count_above = s.sb("count_above", [P, 1])
        weight = s.sb("weight", [P, TT, IDX_HEADS])
        psum = s.ps("psum", 4)
        done, act_done, summed, v = s.sem("done"), s.sem("relu"), s.sem("summed"), s.sem("dve")
        block = s.block()
        tiles = list(range(1, TT))

        @block.tensor
        def _(pe):
            for n, i in enumerate(tiles):
                for h in range(IDX_HEADS):
                    m = n * IDX_HEADS + h
                    if m >= 4:
                        pe.wait_ge(act_done, m - 3)
                    rows = slice(HD * (h % 2), HD * (h % 2) + HD)
                    pe.matmul(psum[:, m % 4, 0:(i + 1) * P], qi[rows, h // 2, i * P:(i + 1) * P],
                              ki[rows, 0:(i + 1) * P], start=True, stop=True).then_inc(done, 1)

        @block.scalar
        def _(act):
            for n, i in enumerate(tiles):
                for h in range(IDX_HEADS):
                    m = n * IDX_HEADS + h
                    act.wait_ge(done, m + 1)
                    if m >= 4:
                        act.wait_ge(summed, m - 3)
                    act.activation(relu[:, m % 4, 0:(i + 1) * P], psum[:, m % 4, 0:(i + 1) * P], ACT.Relu,
                                   scale=HD ** -0.5).then_inc(act_done, 1)

        @block.vector
        def _(dve):
            c = Count(dve, v)
            c.add(dve.memset(ones[:], 1.0))
            c.add(dve.memset(penalty[:, 0], 0.0))
            c.link(dve.tensor_scalar(weight[:], w_idx[:], IDX_HEADS ** -0.5, None, ALU.mult))
            for n, i in enumerate(tiles):
                keys = (i + 1) * P
                sc = score[:, 0:keys]
                for h in range(IDX_HEADS):
                    m = n * IDX_HEADS + h
                    dve.wait_ge(act_done, m + 1)
                    if h:
                        dve.wait_ge(summed, m)
                    base = sc if h else causal[:, (TT - 1 - i) * P:]
                    dve.scalar_tensor_tensor(sc, relu[:, m % 4, 0:keys], weight[:, i, h:h + 1], base,
                                             ALU.mult, ALU.add).then_inc(summed, 1)
                dve.wait_ge(summed, (n + 1) * IDX_HEADS)
                src = sc
                for r in range(rounds_of_8):
                    c.link(dve.max(top[:], src))
                    if r < rounds_of_8 - 1:
                        dst = left[:, r % 2, 0:keys]
                        c.link(dve.match_replace(dst, top[:], src, -3.0e38))
                        src = dst
                least = top[:, 7:8]
                c.link(dve.tensor_scalar(above[:, 0:keys], sc, least, 0.0, ALU.is_gt, ALU.add,
                                         accum_out=count_above[:]))
                c.link(dve.tensor_scalar(equal[:, 0:keys], sc, least, None, ALU.is_equal))
                c.link(dve.tensor_tensor_scan(place[:, 0:keys], ones[:, 0:keys], equal[:, 0:keys],
                                              count_above[:], ALU.mult, ALU.add))
                c.link(dve.scalar_tensor_tensor(equal[:, 0:keys], place[:, 0:keys], float(TOPK), equal[:, 0:keys],
                                                ALU.is_le, ALU.mult))
                c.link(dve.tensor_tensor(above[:, 0:keys], above[:, 0:keys], equal[:, 0:keys], ALU.add))
                c.link(dve.tensor_scalar(penalty[:, i, 0:keys], above[:, 0:keys], -MASKED, MASKED, ALU.mult, ALU.add))


def selected_attention(nc, old, qc, kc, vc, penalty, tables_dram, out):
    with ExitStack() as ctx:
        qs = ctx.enter_context(nc.sbuf_tensor("sel_qs", [P, T], F32))
        tables = ctx.enter_context(nc.sbuf_tensor("sel_tables", [P, 2, T], F32))

        def staging(pool, p, sem):
            if pool is None:
                return 1
            pool.tensor_tensor(qs[:], tile_of(qc, p), attention.scale, ALU.mult).then_inc(sem, 1)

        units, where = [], []
        for a in range(2):
            h = slice(a * HD, (a + 1) * HD)
            for i in reversed(range(TT)):
                units.append([Piece(qs[h, i * P:(i + 1) * P], kc[h], lambda j, p: vc[:, j], 0, (i + 1) * P,
                                    tables[:, a, (TT - 1 - i) * P:], plus=penalty[:, i, 0:(i + 1) * P], table_no=a)])
                where.append((a, i))

        def finish(dve, p, u, o, w, count, sem):
            a, i = where[u]
            dve.tensor_scalar(out[:, i, bass.ds(p * P + a * HD, HD)], o, w, None, ALU.mult).then_inc(sem, 1)
        finish.steps = 0
        attention(nc, old, "sel", 2, units, HD,
                  [(tables[:, a], lambda p, a=a: table_tile(tables_dram, p * 2 + TAB_C + a), 4 * a + 3)
                   for a in range(2)], staging, finish)


def gated_branches(nc, old, h, o_t, w_in, branches, y):
    ring = 2
    kts = [len(o) for o in o_t]
    first = [sum(kts[:b]) for b in range(3)]
    with Stage(nc, "branches", old) as s:
        gate_slots = s.sb("gate_slots", [P, ring, 3, KD, P])
        slots = s.sb("slots", [P, ring, sum(kts), P])
        gate = s.sb("gate", [P, 3, T])
        part = s.sb("part", [P, 4, T])
        psum = s.ps("psum", 6)
        loaded = [s.sem(f"loaded{j}") for j in range(ring)]
        gate_done, prod_done, gated, summed, added = (s.sem(n) for n in
                                                      ("gate_done", "prod_done", "gated", "summed", "added"))
        block = s.block()
        views = [view(w) for w in branches]

        @block.sync
        def _(sp):
            def load(t, j, r):
                sp.wait_ge(added, t * 3 + 3)
                for b in range(3):
                    sp.dma_start(gate_slots[:, j, b], w_in[:, :, bass.ds(t * P + (GATES + b * D), P)])\
                      .then_inc(loaded[j], 16)
                    sp.dma_start(slots[:, j, first[b]:first[b] + kts[b]], views[b][:, :, bass.ds(t * P, P)])\
                      .then_inc(loaded[j], 16)
            rounds(sp, KD, ring, load)

        @block.tensor
        def _(pe):
            def multiply(t, j, r):
                pe.wait_ge(loaded[j], r * 96 + 96)
                for b in range(3):
                    pe.wait_ge(added, t * 3 + (b + 4))
                    for k in range(KD):
                        mm = pe.matmul(psum[:, 2 * b], gate_slots[:, j, b, k], h[:, k], start=k == 0,
                                       stop=k == KD - 1)
                    mm.then_inc(gate_done, 1)
                    for k in range(kts[b]):
                        mm = pe.matmul(psum[:, 2 * b + 1], slots[:, j, first[b] + k], o_t[b][k], start=k == 0,
                                       stop=k == kts[b] - 1)
                    mm.then_inc(prod_done, 1)
            rounds(pe, KD, ring, multiply)

        @block.scalar
        def _(act):
            def take(t, j, r):
                for b in range(3):
                    act.wait_ge(gate_done, t * 3 + b + 1)
                    act.wait_ge(added, t * 3 + (b + 4))
                    act.activation(gate[:, b], psum[:, 2 * b], ACT.Sigmoid).then_inc(gated, 1)
            rounds(act, KD, ring, take)

        @block.vector
        def _(dve):
            dve.sem_inc(added, 6)

            def combine(t, j, r):
                for b in range(3):
                    dve.wait_ge(gated, t * 3 + b + 1)
                    dve.wait_ge(prod_done, t * 3 + b + 1)
                    if b == 0:
                        dve.tensor_tensor(part[:, 0], gate[:, b], psum[:, 2 * b + 1], ALU.mult).then_inc(added, 1)
                    else:
                        dve.tensor_tensor(part[:, b], gate[:, b], psum[:, 2 * b + 1], ALU.mult).then_inc(summed, 1)
                        dve.wait_ge(summed, t * 2 + b)
                        dve.wait_ge(added, t * 3 + (b + 6))
                        dst = part[:, 3] if b == 1 else tile_of(y, t)
                        dve.tensor_tensor(dst, part[:, 0 if b == 1 else 3], part[:, b], ALU.add).then_inc(added, 1)
            rounds(dve, KD, ring, combine)


def half_feed_forward(nc, old, name, A, x_t, h, norm, half):
    normalise(nc, old, name + "_n", lambda k: x_t[:, k], lambda k: h[:, k], lambda k: norm[:, k:k + 1], None)
    with nc.sbuf_tensor(name + "_hidden", [P, KF, T], F32) as hidden:
        glu_hidden(nc, old, name + "_up", h, A[name + "_w_gate_2"][0], A[name + "_w_up_2"][0], hidden)
        down = view(A[name + "_w_down_2"][0])
        project_and_sum(nc, old, name + "_down", down, KF, lambda k: hidden[:, k], x_t, half)


def project_and_sum(nc, old, name, w, kt, rhs, x_t, factor, ring=4):
    with Stage(nc, name, old) as s:
        slots = s.sb("slots", [P, ring, kt, P])
        psum = s.ps("psum", ring)
        loaded = [s.sem(f"loaded{j}") for j in range(ring)]
        done, free = s.sem("done"), s.sem("free")
        block = s.block()

        @block.sync
        def _(sp):
            def load(t, j, r):
                sp.wait_ge(free, t + 1)
                sp.dma_start(slots[:, j], w[:, :, bass.ds(t * P, P)]).then_inc(loaded[j], 16)
            rounds(sp, KD, ring, load)

        @block.tensor
        def _(pe):
            def multiply(t, j, r):
                pe.wait_ge(loaded[j], r * 16 + 16)
                pe.wait_ge(free, t + 1)
                for k in range(kt):
                    mm = pe.matmul(psum[:, j], slots[:, j, k], rhs(k), start=k == 0, stop=k == kt - 1)
                mm.then_inc(done, 1)
            rounds(pe, KD, ring, multiply)

        @block.vector
        def _(dve):
            dve.sem_inc(free, ring)

            def add(t, j, r):
                dve.wait_ge(done, t + 1)
                x = tile_of(x_t, t)
                dve.scalar_tensor_tensor(x, psum[:, j], factor, x, ALU.mult, ALU.add).then_inc(free, 1)
            rounds(dve, KD, ring, add)


def second_block(nc, old, A, x_t, h, cols, square, scratch, lam_in):
    half_feed_forward(nc, old, "ffn1", A, x_t, h, cols["ffn1_norm_2"], 0.5)
    normalise(nc, old, "mix_norm", lambda k: x_t[:, k], lambda k: h[:, k], lambda k: cols["mix_norm_2"][:, k:k + 1], None)
    w_in = view(A["w_in_2"][0])
    gain = cols["qk_gain"]
    with ExitStack() as top:
        def sb(name, shape):
            return top.enter_context(nc.sbuf_tensor("two_" + name, shape, F32))
        o_a, o_b, o_c = sb("o_a", [P, 2, T]), sb("o_b", [P, 4, T]), sb("o_c", [P, 2, T])
        with ExitStack() as mix:
            def mb(name, shape):
                return mix.enter_context(nc.sbuf_tensor("mix2_" + name, shape, F32))
            qa = mb("qa", [P, 12, T])
            va = mb("va", [P, TT, A_HEADS * HD])
            qb = mb("qb", [P, 8, T])
            vb = mb("vb", [P, TT, B_HEADS * P])
            qc, kc = mb("qc", [P, 3, T]), None
            kc = qc[:, 2]
            vc = mb("vc", [P, TT, HD])
            qi = mb("qi", [P, 5, T])
            ki = qi[:, 4]
            w_idx = mb("w_idx", [P, TT, IDX_HEADS])

            def copy_to(dst):
                return lambda act, t, psum: act.activation(tile_of(dst, t), psum, ACT.Copy)
            column_products(nc, old, "in_2a", lambda t: w_in[:, :, bass.ds(t * P + QA, P)], 12, KD, lambda k: h[:, k],
                            copy_to(qa))
            column_products(nc, old, "in_2b", lambda t: w_in[:, :, bass.ds(t * P + QB, P)], 8, KD, lambda k: h[:, k],
                            copy_to(qb))

            def cols_job(start, n, dst):
                return ([(slice(0, n * P), w_in[:, :, start:start + n * P])],
                        [("columns", lambda slot, k, c=c: slot[:, k, c * P:(c + 1) * P], P, dst(c), ACT.Copy)
                         for c in range(n)])

            def tok_job(start, w, dst):
                return ([(slice(0, w), w_in[:, :, start:start + w])],
                        [("tokens", w, [dst(i) for i in range(TT)], ACT.Copy)])

            def twice_job(start, dst):
                return ([(slice(a * HD, (a + 1) * HD), w_in[:, :, start:start + HD]) for a in range(2)],
                        [("columns", lambda slot, k: slot[:, k, 0:P], P, dst, ACT.Copy)])
            jobs = [tok_job(VA + c * 384, 384, lambda i, c=c: va[:, i, c * 384:(c + 1) * 384]) for c in range(2)]
            jobs += [tok_job(VB + c * 256, 256, lambda i, c=c: vb[:, i, c * 256:(c + 1) * 256]) for c in range(2)]
            jobs += [cols_job(QC, 2, lambda c: qc[:, c]), twice_job(KC, kc), tok_job(VC, HD, lambda i: vc[:, i]),
                     cols_job(QI, 2, lambda c: qi[:, c]), cols_job(QI + 2 * P, 2, lambda c: qi[:, 2 + c]),
                     twice_job(KI, ki), tok_job(WI, IDX_HEADS, lambda i: w_idx[:, i])]
            mixed_products(nc, old, "in_2c", h, jobs, 3 * P)
            tiles = [(qa[:, t], 0 if t < 6 else 1) for t in range(12)] + [(qb[:, t], 2 if t < 4 else 3) for t in range(8)]
            tiles += [(qc[:, t], 4 if t < 2 else 5) for t in range(3)]
            head_norms(nc, old, [t for t, _ in tiles], lambda n: gain[:, tiles[n][1]:tiles[n][1] + 1], square)

            def turn(name, tok, dst):
                to_channels(nc, old, name, square[:, IDENT],
                            [(tok[:, :, c * P:(c + 1) * P], dst[:, c]) for c in range(tok.shape[2] // P)])
            with nc.sbuf_tensor("dil_tok", [P, TT, 2 * P], F32) as tok:
                dilated_attention(nc, old, qa, va, scratch, tok)
                turn("dil_turn", tok, o_a)
            with nc.sbuf_tensor("diff_tok", [P, TT, 4 * P], F32) as tok, nc.sbuf_tensor("minus_lam", [P, 1], F32) as lam:
                diff_factor(nc, old, lam_in, lam)
                diff_attention(nc, old, qb, vb, lam[:], scratch, tok)
                diff_norm(nc, old, tok)
                to_channels(nc, old, "diff_turn", square[:, IDENT],
                            [(tok[:, :, c * P:(c + 1) * P], o_b[:, c]) for c in range(4)], scale=cols["diff_norm"][:, 0:1])
            with nc.sbuf_tensor("sel_tok", [P, TT, 2 * P], F32) as tok, \
                    nc.sbuf_tensor("penalty", [P, TT, T], F32) as penalty:
                with nc.sbuf_tensor("causal", [P, T], F32) as causal:
                    with Stage(nc, "load_causal", old) as s:
                        sem = s.sem("loaded")
                        block = s.block()
                        @block.sync
                        def _(sp):
                            sp.dma_start(causal[:], table_tile(scratch, TAB_FOX)).then_inc(sem, 16)
                            sp.wait_ge(sem, 16)
                    select_keys(nc, old, qi, ki, w_idx, causal, penalty)
                selected_attention(nc, old, qc, kc, vc, penalty, scratch, tok)
                turn("sel_turn", tok, o_c)
        with nc.sbuf_tensor("two_y", [P, KD, T], F32) as y:
            gated_branches(nc, old, h, [[o[:, k] for k in range(o.shape[1])] for o in (o_a, o_b, o_c)], w_in,
                           [A[f"w_branch_{b}_2"][0] for b in "abc"], y)
            project_and_sum(nc, old, "out2", view(A["w_out_2"][0]), KD, lambda k: y[:, k], x_t, 1.0)
    half_feed_forward(nc, old, "ffn2", A, x_t, h, cols["ffn2_norm_2"], 0.5)



def build(nc, A, C, out):
    scratch = nc.dram_tensor("distance_rows", (N_TABLES, TABLE_LEN), F32, kind="Internal").ap()
    tables = nc.dram_tensor("distance_tables", (N_TABLES, P, T), F32, kind="Internal").ap()
    old = []
    with ExitStack() as top:
        def sb(name, shape):
            return top.enter_context(nc.sbuf_tensor(name, shape, F32))

        x_t = sb("x_t", [P, KD, T])
        h = sb("h", [P, KD, T])
        square = sb("square", [P, LEVELS + 7, P])
        mod = sb("mod", [P, 6 * KD])
        gains = sb("gains", [P, 4 * KD])
        heads = sb("heads", [P, H_FOX // 2])
        b_f = sb("b_f", [H_FOX, 1])
        bias = sb("bias", [33, N_TABLES])
        lam_in = sb("lam_in", [P, 4 * HD])
        columns = sb("columns", [P, 5, P])
        att_scale = sb("att_scale", [P, 1])
        attention.ident = square[:, IDENT]
        attention.scale = att_scale[:].to_broadcast([P, T])

        rows, used, col = [], [0] * 5, {}

        def put(name, pack, n, src):
            rows.append((pack, used[pack], n, slice(0, P), src))
            col[name] = columns[:, pack, used[pack]:used[pack] + n]
            used[pack] += n

        def put_both(name, pack, n, src):
            for a in range(2):
                rows.append((pack, used[pack], n, slice(a * HD, (a + 1) * HD), src))
            col[name] = columns[:, pack, used[pack]:used[pack] + n]
            used[pack] += n

        def line(w):
            return w.rearrange("a (n p) -> (a n) p", p=P)
        put("norm_g", 0, 4 * KD, A["norm_g"][0].rearrange("a (n p) -> (a n) p", p=P))
        put("c", 0, KD, line(A["c"]))
        put("ada_b", 0, 6 * KD, line(A["ada_b"]))
        for n in ("ffn1_norm_2", "mix_norm_2", "ffn2_norm_2"):
            put(n, 0, KD, line(A[n]))
        cw = A["ffn_conv_w"][0].rearrange("a (n p) -> (a n) p", p=P)
        put("conv01", 1, 4 * KF, cw[0:4 * KF, :])
        put("conv2", 2, 2 * KF, cw[4 * KF:6 * KF, :])
        put("conv_b", 2, 2 * KF, line(A["ffn_conv_b"]))
        put("mu", 3, RW_TILES, line(A["rwkv_mu"]))
        for n in ("w0", "a0", "k_k", "k_a", "ln_w", "ln_b"):
            put(n, 3, 2, line(A["rwkv_" + n]))
        put("r_k", 3, 2, A["rwkv_r_k"][0].rearrange("(n a) d -> n (a d)", a=2))
        put("diff_norm", 3, 1, A["diff_out_norm_2"])
        put_both("qk_gain", 3, 6, A["qk_gain_2"][0].rearrange("a b d -> (a b) d"))
        put_both("pe_k", 4, L_CMP, A["nsa_pe_k"][0])
        put_both("pe_v", 4, L_CMP, A["nsa_pe_v"][0])
        extra = [
            (b_f[:], A["fox_b_f"].rearrange("a h -> h a")),
            (bias[0:32, 0:H_NSA], A["rel_bias"]),
            (bias[0:32, H_NSA:N_TABLES - 1], A["rel_bias_2"]),
            (lam_in[:], A["diff_lambda_2"].rearrange("a b d -> a (b d)")[0].partition_broadcast(P)),
            (heads[:], C["heads"]),
        ]
        with Stage(nc, "zero_bias", old) as s:
            block = s.block()
            @block.vector
            def _(dve):
                dve.memset(bias[0:32, N_TABLES - 1:N_TABLES], 0.0)
                dve.memset(bias[32:33], MASKED)
                dve.memset(att_scale[:], ATT_SCALE)
        load_parameters(nc, old, rows, used, columns, square, C["square"], A["x"][0], x_t, extra)
        distance_tables(nc, old, C["onehot"], bias, scratch, tables)
        cols = dict(col)
        cols["pe"] = columns[:, 4, 0:2 * L_CMP].rearrange("p (a l) -> p a l", a=2)

        def conv(t, w, tap_no):
            pack, start = {0: (1, 0), 1: (1, 2 * KF), 2: (2, 0), 3: (2, 2 * KF)}[tap_no]
            return columns[:, pack, bass.ds(t + (start + w * KF), 1)]
        cols["conv"] = conv
        modulation(nc, old, col["c"], view(A["ada_w"][0]), col["ada_b"], mod)
        block_one_gains(nc, old, mod, col["norm_g"], gains)
        first_block(nc, old, None, A, x_t, h, gains, mod, cols, square, tables, heads, b_f[:])
        second_block(nc, old, A, x_t, h, cols, square, tables, lam_in)

        with Stage(nc, "store", old) as s:
            tok = s.sb("tok", [P, TT, D])
            psum = s.ps("psum", 4)
            done, kept, stored = s.sem("done"), s.sem("kept"), s.sem("stored")
            block = s.block()

            @block.tensor
            def _(pe):
                for n in range(2 * TT):
                    i, half = divmod(n, 2)
                    if n >= 4:
                        pe.wait_ge(kept, n - 3)
                    for k in range(4):
                        mm = pe.transpose(psum[:, n % 4, k * P:(k + 1) * P],
                                          x_t[:, half * 4 + k, i * P:(i + 1) * P], square[:, IDENT])
                    mm.then_inc(done, 1)

            @block.vector
            def _(dve):
                for n in range(2 * TT):
                    i, half = divmod(n, 2)
                    dve.wait_ge(done, n + 1)
                    dve.tensor_copy(tok[:, i, half * T:(half + 1) * T], psum[:, n % 4]).then_inc(kept, 1)

            @block.sync
            def _(sp):
                for i in range(TT):
                    sp.wait_ge(kept, 2 * i + 2)
                    sp.dma_start(out[0, i * P:(i + 1) * P, :], tok[:, i]).then_inc(stored, 16)
                sp.wait_ge(stored, 16 * TT)


def kernel(**inputs):
    import concourse.bacc as _bacc
    from concourse.bass_utils import run_bass_kernel_spmd as _run

    nc = _bacc.Bacc("TRN2", target_bir_lowering=False, num_devices=1)
    arrays, A, C = {}, {}, {}
    constants = {"square": square_constants(), "onehot": distance_buckets(), "heads": head_rows()}
    for group, into in ((inputs, A), (constants, C)):
        for name, value in group.items():
            a = np.ascontiguousarray(value)
            arrays[f"in_{name}_dram"] = a
            into[name] = nc.dram_tensor(f"in_{name}_dram", a.shape, F32, kind="ExternalInput").ap()
    out = nc.dram_tensor("out_0_dram", (1, T, D), F32, kind="ExternalOutput").ap()
    build(nc, A, C, out)
    r = _run(nc, [arrays], core_ids=[0])
    return r.results[0]["out_0_dram"]
```

```python
import math
from contextlib import ExitStack

import numpy as np

import concourse.bass as bass
from concourse import mybir

F32 = mybir.dt.float32
F32R = mybir.dt.float32r
ACT = mybir.ActivationFunctionType
ALU = mybir.AluOpType
AX = mybir.AxisListType

P = 128
T = 512
TT = T // P
D = 1024
KD = D // P
HD = 64
DFF = 2816
KF = DFF // P
ATT_SCALE = HD ** -0.5
EPS = 1e-6
MASKED = -1e30
LOWEST = -1e20

C_RWKV, R_LOW = 256, 128
N_RWKV = 3 * C_RWKV + R_LOW
RW_TILES = N_RWKV // P
C_FOX, H_FOX = 384, 6
FOX_Q = N_RWKV
FOX_V = FOX_Q + 2 * C_FOX
FOX_F = FOX_V + C_FOX
C_NSA, H_NSA, C_KV = 384, 6, 128
NSA_Q = FOX_F + H_FOX
NSA_KC = NSA_Q + C_NSA
NSA_VS = NSA_KC + 3 * C_KV
NSA_KW = NSA_VS + C_KV
NSA_VW = NSA_KW + C_KV
NSA_GATE = NSA_VW + C_KV
L_CMP, D_CMP, CMP_HID = 32, 16, 128
N_CMP = T // D_CMP - L_CMP // D_CMP + 1
GN_EPS = 64e-5

A_HEADS, B_HEADS, C_HEADS, IDX_HEADS = 12, 4, 4, 8
A_SLOTS, A_GROUPS = 4, 3
QA, VA = 0, 2 * A_HEADS * HD
QB = VA + A_HEADS * HD
VB = QB + 4 * B_HEADS * HD
QC = VB + B_HEADS * 2 * HD
KC, VC = QC + C_HEADS * HD, QC + (C_HEADS + 1) * HD
QI = QC + (C_HEADS + 2) * HD
KI = QI + IDX_HEADS * HD
WI = KI + HD
GATES = WI + IDX_HEADS
TOPK = 128
LAM_INIT = 0.8 - 0.6 * math.exp(-0.3 * 0)

TABLE_LEN = 640
N_TABLES = H_NSA + A_HEADS + B_HEADS + C_HEADS + 1
TAB_NSA, TAB_A, TAB_B, TAB_C, TAB_FOX = 0, 6, 18, 22, 26



def square_constants():
    s, t = np.arange(P)[:, None], np.arange(P)[None, :]
    mats = [s == t, s // HD == t // HD, s < t, s <= t]
    for level in range(7):
        size = 2 << level
        mats.append((s // size == t // size) & (s % size < size // 2) & (t % size >= size // 2))
    return np.stack(mats, 1).astype(np.float32)


IDENT, HEADS, STRICT, INCL, LEVELS = 0, 1, 2, 3, 4


def distance_buckets():
    dist = T - 1 - np.arange(TABLE_LEN)

    def bucket(max_distance):
        n = np.maximum(dist, 0)
        large = 16 + (np.log(np.maximum(n, 1) / 16) / math.log(max_distance / 16) * 16 + 1e-9).astype(np.int64)
        return np.where(n < 16, n, np.minimum(large, 31))

    near, far = bucket(128), bucket(2048)
    kinds = [(near, dist >= 0), (far, (dist >= 0) & (dist <= 128)), (far, (dist >= 0) & (dist % 4 == 0)),
             (far, (dist >= 0) & (dist % 16 == 0)), (far, dist >= 0)]
    out = np.zeros((33, len(kinds), TABLE_LEN), np.float32)
    for n, (b, ok) in enumerate(kinds):
        out[np.where(ok, b, 32), n, np.arange(TABLE_LEN)] = 1.0
    return out


def head_rows():
    out = np.zeros((P, H_FOX // 2), np.float32)
    for p in range(H_FOX // 2):
        for a in range(2):
            out[[a * HD + 2 * p + a, a * HD + 32 + 2 * p + a], p] = 1.0
    return out


class Stage:

    def __init__(self, nc, name, old):
        self.nc, self.name, self.old = nc, name, old
        self.own = []

    def __enter__(self):
        self.ctx = ExitStack()
        return self

    def __exit__(self, *exc):
        self.ctx.close()
        self.old[:] = self.own

    def sb(self, name, shape, dt=F32):
        return self.ctx.enter_context(self.nc.sbuf_tensor(f"{self.name}_{name}", shape, dt))

    def ps(self, name, banks):
        return self.ctx.enter_context(self.nc.psum_tensor(f"{self.name}_{name}", [P, banks, T], F32))

    def sem(self, name):
        s = self.ctx.enter_context(self.nc.semaphore(f"{self.name}_{name}"))
        self.own.append(s)
        return s

    def block(self):
        block = self.ctx.enter_context(self.nc.Block())
        if self.old:
            @block.gpsimd
            def _(pool):
                for s in self.old:
                    pool.sem_clear(s)
        return block


class Count:

    def __init__(self, eng, sem):
        self.eng, self.sem, self.base, self.n = eng, sem, 0, 0

    def add(self, instruction):
        instruction.then_inc(self.sem, 1)
        self.n += 1

    def settle(self):
        self.eng.wait_ge(self.sem, self.base + self.n)

    def link(self, instruction):
        self.add(instruction)
        self.settle()

    def enter(self, base):
        self.base, self.n = base, 0


def flat(ap):
    return ap.rearrange("p a b -> p (a b)")


def tile_of(tensor, t):
    return flat(tensor[:, bass.ds(t, 1), :]) if not isinstance(t, int) else tensor[:, t, :]


def rounds(eng, tiles, unroll, body):
    whole = tiles // unroll
    if whole > 1:
        with eng.Fori(0, whole) as g:
            for j in range(unroll):
                body(g * unroll + j, j, g)
    else:
        whole = 0
    for t in range(whole * unroll, tiles):
        body(t, t % unroll, t // unroll)



RAW, PAIRS, LEAD = 4, 2, 2


def three_products(pe, out, weights, rhs, start, stop):
    (w_hi, w_lo), (r_hi, r_lo) = weights, rhs
    pe.matmul(out, w_hi, r_hi, start=start, stop=False)
    pe.matmul(out, w_hi, r_lo, start=False, stop=False)
    return pe.matmul(out, w_lo, r_hi, start=False, stop=stop)


def rounds_ahead(eng, units, start, finish):
    for u in range(LEAD):
        start(u, u, 0)

    def body(u, j, r):
        start(u + LEAD, (j + LEAD) % RAW, r + (j + LEAD) // RAW)
        finish(u, j, r)
    rounds(eng, units - LEAD, RAW, body)
    for u in range(units - LEAD, units):
        finish(u, u % RAW, u // RAW)


class Stream:

    def __init__(self, s, units, kt, source, rhs, per=1, outputs=None, banks=None):
        self.units, self.kt, self.source, self.rhs, self.per = units, kt, source, rhs, per
        self.banks, self.outputs = banks or RAW // per, outputs
        self.raw = s.sb("raw", [P, RAW, kt, P])
        self.hi = s.sb("w_hi", [P, PAIRS, kt, P], F32R)
        self.lo = s.sb("w_lo", [P, PAIRS, kt, P], F32R)
        self.psum = s.ps("psum", self.banks)
        self.loaded = [s.sem(f"loaded{j}") for j in range(RAW)]
        self.rounded, self.split, self.done, self.free = (s.sem(n) for n in ("rounded", "split", "done", "free"))

    def bank(self, j):
        return self.psum[:, j // self.per]

    def tile(self, j, r):
        return r * self.banks + j // self.per

    def sources(self, j, r):
        src = self.source(j, r)
        return src if isinstance(src, list) else [(slice(0, self.kt), src)]

    def load(self, sp):
        def body(u, j, r):
            sources = self.sources(j, r)
            sp.wait_ge(self.split, u + 1)
            for tiles, src in sources:
                sp.dma_start(self.raw[:, j, tiles], src).then_inc(self.loaded[j], 16)
        rounds(sp, self.units, RAW, body)

    def round_hi(self, act, u, j, r):
        n = 16 * len(self.sources(j, r))
        act.wait_ge(self.loaded[j], r * n + n)
        act.wait_ge(self.done, u + 1)
        act.activation(self.hi[:, j % PAIRS], self.raw[:, j], ACT.Copy).then_inc(self.rounded, 1)

    def split_lo(self, dve, u, j, r):
        dve.wait_ge(self.rounded, u + 1)
        dve.tensor_tensor(self.lo[:, j % PAIRS], self.raw[:, j], self.hi[:, j % PAIRS].bitcast(F32), ALU.subtract)\
           .then_inc(self.split, 1)

    def multiply(self, pe, banks_free=None):
        pe.sem_inc(self.done, PAIRS)

        def body(u, j, r):
            pe.wait_ge(self.split, u + (RAW + 1))
            opens, closes = j % self.per == 0, j % self.per == self.per - 1
            if banks_free is not None:
                banks_free(j, r)
            elif opens:
                pe.wait_ge(self.free, self.tile(j, r) + 1)
            for bank, first, end in self.outputs(j) if self.outputs else [(j // self.per, 0, self.kt)]:
                for k in range(first, end):
                    mm = three_products(pe, self.psum[:, bank], (self.hi[:, j % PAIRS, k], self.lo[:, j % PAIRS, k]),
                                        self.rhs(j, k), opens and k == first, closes and k == end - 1)
            mm.then_inc(self.done, 1)
        rounds(pe, self.units, RAW, body)

    def wait_products(self, eng, u):
        eng.wait_ge(self.done, u + (PAIRS + 1))


def nothing(u, j, r):
    pass


def column_products(nc, old, name, weights, tiles, rhs, store, chunks=1, by_vector=False):
    kt = weights(0, 0).shape[1]
    with Stage(nc, name, old) as s:
        st = Stream(s, tiles * chunks, kt, lambda j, r: weights(r * (RAW // chunks) + j // chunks, j % chunks),
                    lambda j, k: rhs((j % chunks) * kt + k), per=chunks)
        block = s.block()

        def take(eng):
            def body(u, j, r):
                if j % chunks == chunks - 1:
                    st.wait_products(eng, u)
                    store(eng, st.tile(j, r), st.bank(j)).then_inc(st.free, 1)
            return body

        @block.sync
        def _(sp):
            st.load(sp)

        @block.tensor
        def _(pe):
            st.multiply(pe)

        @block.scalar
        def _(act):
            rounds_ahead(act, st.units, lambda u, j, r: st.round_hi(act, u, j, r),
                         nothing if by_vector else take(act))

        @block.vector
        def _(dve):
            dve.sem_inc(st.split, RAW)
            dve.sem_inc(st.free, st.banks)
            rounds_ahead(dve, st.units, lambda u, j, r: st.split_lo(dve, u, j, r),
                         take(dve) if by_vector else nothing)


def mixed_products(nc, old, name, h, jobs, width):
    with Stage(nc, name, old) as s:
        raw = s.sb("raw", [P, 2, KD, width])
        hi = s.sb("w_hi", [P, 2, KD, width], F32R)
        lo = s.sb("w_lo", [P, 2, KD, width], F32R)
        psum = s.ps("psum", 4)
        loaded = [s.sem(f"loaded{j}") for j in range(2)]
        rounded, split, done, stored = s.sem("rounded"), s.sem("split"), s.sem("done"), s.sem("stored")
        outs = []
        for n, (_, _, outputs) in enumerate(jobs):
            for o in outputs:
                if o[0] == "columns":
                    outs.append((n, o[1], T, None, o[2], o[3]))
                else:
                    outs += [(n, 0, o[1], i, o[2][i], o[3]) for i in range(TT)]
        last = [max(i for i, o in enumerate(outs) if o[0] == n) for n in range(len(jobs))]
        landed = [16 * sum(len(jobs[m][0]) for m in range(n % 2, n + 1, 2)) for n in range(len(jobs))]
        block = s.block()

        @block.sync
        def _(sp):
            for n, (loads, _, _) in enumerate(jobs):
                if n >= 2:
                    sp.wait_ge(split, n - 1)
                for cols, src in loads:
                    sp.dma_start(raw[:, n % 2, :, cols], src).then_inc(loaded[n % 2], 16)

        @block.vector
        def _(dve):
            for n, (_, w, _) in enumerate(jobs):
                dve.wait_ge(rounded, n + 1)
                dve.tensor_tensor(lo[:, n % 2, :, 0:w], raw[:, n % 2, :, 0:w], hi[:, n % 2, :, 0:w].bitcast(F32),
                                  ALU.subtract).then_inc(split, 1)

        @block.tensor
        def _(pe):
            for i, (n, c, w, tokens, _, _) in enumerate(outs):
                pe.wait_ge(split, n + 1)
                if i >= 4:
                    pe.wait_ge(stored, i - 3)
                for k in range(KD):
                    if tokens is None:
                        left = [x[:, n % 2, k, c:c + P] for x in (hi, lo)]
                        right = [x[:, k, :] for x in h]
                    else:
                        left = [x[:, k, tokens * P:(tokens + 1) * P] for x in h]
                        right = [x[:, n % 2, k, 0:w] for x in (hi, lo)]
                    mm = three_products(pe, psum[:, i % 4, 0:w], left, right, k == 0, k == KD - 1)
                mm.then_inc(done, 1)

        @block.scalar
        def _(act):
            def round_job(n):
                act.wait_ge(loaded[n % 2], landed[n])
                if n >= 2:
                    act.wait_ge(done, last[n - 2] + 1)
                w = jobs[n][1]
                act.activation(hi[:, n % 2, :, 0:w], raw[:, n % 2, :, 0:w], ACT.Copy).then_inc(rounded, 1)
            round_job(0)
            round_job(1)
            for i, (n, _, w, _, dst, func) in enumerate(outs):
                act.wait_ge(done, i + 1)
                act.activation(dst, psum[0:dst.shape[0], i % 4, 0:w], func).then_inc(stored, 1)
                if i == last[n] and n + 2 < len(jobs):
                    round_job(n + 2)


def split_tiles(nc, old, name, src, pair):
    with Stage(nc, name, old) as s:
        rounded = s.sem("rounded")
        block = s.block()

        @block.scalar
        def _(act):
            for k in range(len(src)):
                act.activation(pair[0][:, k], src[k], ACT.Copy).then_inc(rounded, 1)

        @block.vector
        def _(dve):
            for k in range(0, len(src), 2):
                dve.wait_ge(rounded, k + 1)
                dve.tensor_tensor(pair[1][:, k], src[k], pair[0][:, k].bitcast(F32), ALU.subtract)

        @block.gpsimd
        def _(pool):
            for k in range(1, len(src), 2):
                pool.wait_ge(rounded, k + 1)
                pool.tensor_tensor(pair[1][:, k], src[k], pair[0][:, k].bitcast(F32), ALU.subtract)



def normalise(nc, old, name, src, gain, shift=None, pair=None, add_to=None):
    with Stage(nc, name, old) as s:
        squares = s.sb("squares", [P, 2, T])
        rstd = s.sb("rstd", [P, T])
        logs = s.sb("logs", [P, T])
        scaled = s.sb("scaled", [P, 4, T])
        ones = s.sb("ones", [P, P])
        eps = s.sb("eps", [P, 1])
        psum = s.ps("psum", 1)
        const, squared, summed, rooted = s.sem("const"), s.sem("squared"), s.sem("summed"), s.sem("rooted")
        used, scaled_s, ready = s.sem("used"), s.sem("scaled"), s.sem("ready")
        rounded, split = s.sem("rounded"), s.sem("split")
        block = s.block()

        @block.scalar
        def _(act):
            for k in range(0, KD, 2):
                if k >= 2:
                    act.wait_ge(used, k - 1)
                act.activation(squares[:, 0], src(k), ACT.Square).then_inc(squared, 1)
            act.wait_ge(summed, 1)
            act.wait_ge(const, 2)
            act.activation(logs[:], psum[:, 0], ACT.Ln, bias=eps[:, 0:1], scale=1.0 / D).then_inc(rooted, 1)
            act.wait_ge(rooted, 1)
            act.activation(rstd[:], logs[:], ACT.Exp, scale=-0.5).then_inc(rooted, 1)
            if pair is not None:
                for k in range(KD):
                    act.wait_ge(ready, k + 1)
                    act.activation(pair[0][:, k], scaled[:, k % 4], ACT.Copy).then_inc(rounded, 1)

        @block.gpsimd
        def _(pool):
            if pair is not None:
                for k in range(KD):
                    pool.wait_ge(rounded, k + 1)
                    pool.tensor_tensor(pair[1][:, k], scaled[:, k % 4], pair[0][:, k].bitcast(F32), ALU.subtract)\
                        .then_inc(split, 1)

        @block.tensor
        def _(pe):
            pe.wait_ge(const, 2)
            for k in range(KD):
                pe.wait_ge(squared if k % 2 == 0 else const, k // 2 + (1 if k % 2 == 0 else 3))
                mm = pe.matmul(psum[:, 0], ones[:], squares[:, k % 2], start=k == 0, stop=k == KD - 1)
                mm.then_inc(used if k < KD - 1 else summed, 1)

        @block.vector
        def _(dve):
            dve.memset(ones[:], 1.0).then_inc(const, 1)
            dve.memset(eps[:], EPS).then_inc(const, 1)
            for k in range(1, KD, 2):
                if k >= 3:
                    dve.wait_ge(used, k - 1)
                dve.tensor_tensor(squares[:, 1], src(k), src(k), ALU.mult).then_inc(const, 1)
            dve.wait_ge(rooted, 2)
            for k in range(KD):
                if pair is not None and k >= 4:
                    dve.wait_ge(split, k - 3)
                out = scaled[:, k % 4]
                plain = pair is not None and shift is None
                dve.scalar_tensor_tensor(out, src(k), gain(k), rstd[:], ALU.mult, ALU.mult)\
                   .then_inc(ready if plain else scaled_s, 1)
                if shift is not None:
                    dve.wait_ge(scaled_s, k + 1)
                    dve.tensor_scalar(out, out, shift(k), None, ALU.add).then_inc(ready, 1)
                if add_to is not None and k >= 1:
                    dve.wait_ge(scaled_s, k)
                    dve.tensor_tensor(add_to(k - 1), add_to(k - 1), scaled[:, (k - 1) % 4], ALU.add)
            if add_to is not None:
                dve.wait_ge(scaled_s, KD)
                dve.tensor_tensor(add_to(KD - 1), add_to(KD - 1), scaled[:, (KD - 1) % 4], ALU.add)



def load_parameters(nc, old, rows, packs, columns, square, cst_square, x, x_t, extra):
    with Stage(nc, "setup", old) as s:
        xin = s.sb("x", [P, TT, D])
        stage = s.sb("rows", [P, len(packs), P])
        psum = s.ps("psum", 8)
        const, params, x_in = s.sem("const"), s.sem("params"), s.sem("x_in")
        turned, stored = s.sem("turned"), s.sem("stored")
        block = s.block()

        @block.sync
        def _(sp):
            sp.dma_start(square[:], cst_square).then_inc(const, 16)
            for i in range(TT):
                sp.dma_start(xin[:, i], x[i * P:(i + 1) * P, :]).then_inc(x_in, 16)

        @block.scalar
        def _(act):
            for pack, row, n, cols, src in rows:
                act.dma_start(stage[row:row + n, pack, cols], src).then_inc(params, 16)
            for dst, src in extra:
                act.dma_start(dst, src).then_inc(params, 16)
            act.wait_ge(params, 16 * (len(rows) + len(extra)))

        @block.tensor
        def _(pe):
            ident = square[:, IDENT]
            pe.wait_ge(const, 16)
            pe.wait_ge(x_in, 16 * TT)
            for k in range(KD):
                for i in range(TT):
                    mm = pe.transpose(psum[:, k % 4, i * P:(i + 1) * P], xin[:, i, k * P:(k + 1) * P], ident)
                mm.then_inc(turned, 1)
                if k >= 3 and k < KD - 1:
                    pe.wait_ge(stored, k - 2)
            pe.wait_ge(params, 16 * (len(rows) + len(extra)))
            for n, used in enumerate(packs):
                mm = pe.transpose(psum[:, 4 + n // 4, (n % 4) * P:(n % 4) * P + used], stage[0:used, n],
                                  ident[0:used, 0:used])
            mm.then_inc(turned, 1)

        @block.vector
        def _(dve):
            for k in range(KD):
                dve.wait_ge(turned, k + 1)
                dve.tensor_copy(x_t[:, k], psum[:, k % 4]).then_inc(stored, 1)
            dve.wait_ge(turned, KD + 1)
            for n, used in enumerate(packs):
                dve.tensor_copy(columns[:, n, 0:used], psum[:, 4 + n // 4, (n % 4) * P:(n % 4) * P + used])\
                   .then_inc(stored, 1)


def modulation(nc, old, c_col, ada_w, ada_b_col, mod):
    tiles, per, ring = 6 * KD, 4, 3
    loads = tiles // per
    with Stage(nc, "mod", old) as s:
        slots = s.sb("slots", [P, ring, KD, per * P])
        silu = s.sb("silu", [P, KD])
        psum = s.ps("psum", 1)
        loaded = [s.sem(f"loaded{j}") for j in range(ring)]
        act_done, done = s.sem("silu_done"), s.sem("done")
        block = s.block()

        @block.sync
        def _(sp):
            def load(t, j, r):
                sp.wait_ge(done, t + 1)
                sp.dma_start(slots[:, j], ada_w[:, :, bass.ds(t * (per * P), per * P)]).then_inc(loaded[j], 16)
            rounds(sp, loads, ring, load)

        @block.scalar
        def _(act):
            act.activation(silu[:], c_col, ACT.Silu).then_inc(act_done, 1)

        @block.tensor
        def _(pe):
            pe.sem_inc(done, ring)
            pe.wait_ge(act_done, 1)
            def multiply(t, j, r):
                pe.wait_ge(loaded[j], r * 16 + 16)
                for m in range(per):
                    for k in range(KD):
                        mm = pe.matmul(psum[:, 0, bass.ds(t * per + m, 1)], slots[:, j, k, m * P:(m + 1) * P],
                                       silu[:, k:k + 1], start=k == 0, stop=k == KD - 1)
                mm.then_inc(done, 1)
            rounds(pe, loads, ring, multiply)

        @block.vector
        def _(dve):
            dve.wait_ge(done, loads + ring)
            dve.tensor_tensor(mod[:], psum[:, 0, 0:tiles], ada_b_col, ALU.add)


def block_one_gains(nc, old, mod, norm_g, gains):
    with Stage(nc, "gains", old) as s:
        done = s.sem("done")
        block = s.block()

        @block.vector
        def _(dve):
            for n, (scale, one) in enumerate([(1, True), (2, False), (4, True), (5, False)]):
                part = mod[:, scale * KD:(scale + 1) * KD]
                dve.scalar_tensor_tensor(gains[:, n * KD:(n + 1) * KD], part, 1.0 if one else 0.0,
                                         norm_g[:, n * KD:(n + 1) * KD], ALU.add, ALU.mult).then_inc(done, 1)



CHUNK = P
NCH = T // CHUNK


def rwkv_inputs(nc, old, rw, cols, w_up, square, r_in, a_in, k_in, b_in, v_in, gate, bonus, tot, mid):
    with Stage(nc, "rwkv_in", old) as s:
        mixed = s.sb("mixed", [P, RW_TILES, T])
        diff = s.sb("diff", [P, T])
        low = s.sb("low", [P, T])
        rate = s.sb("rate", [P, 2, T])
        ld = s.sb("ld", [P, 2, T])
        run = s.sb("run", [P, 2, T])
        kk = s.sb("kk", [P, 2, T])
        work = s.sb("work", [P, 2, T])
        root = s.sb("root", [P, 2, T])
        e_pos = s.sb("e_pos", [P, 2, T])
        e_before = s.sb("e_before", [P, 2, T])
        e_neg = s.sb("e_neg", [P, 2, T])
        ones = s.sb("ones", [P, T])
        psum = s.ps("psum", 8)
        v, a, low_done, up_done, sums_done = (s.sem(n) for n in ("dve", "act", "low", "up", "sums"))
        block = s.block()

        @block.vector
        def _(dve):
            c = Count(dve, v)
            for t in [6, 0, 1, 2, 3, 4, 5]:
                c.link(dve.tensor_tensor(diff[:], rw[:, t, 0:T], rw[:, t, 1:T + 1], ALU.subtract))
                c.link(dve.scalar_tensor_tensor(mixed[:, t], diff[:], cols["mu"][:, t:t + 1], rw[:, t, 1:T + 1],
                                                ALU.mult, ALU.add))
            c.add(dve.memset(ones[:], 1.0))
            for t in range(2):
                c.link(dve.tensor_scalar(kk[:, t], mixed[:, 2 + t], cols["k_k"][:, t:t + 1], None, ALU.mult))
                c.link(dve.tensor_tensor(work[:, t], kk[:, t], kk[:, t], ALU.mult))
            dve.wait_ge(a, 3 + 4)
            for t in range(2):
                c.link(dve.tensor_scalar(ld[:, t], ld[:, t], -math.exp(-0.5), None, ALU.mult))
                for n in range(NCH):
                    part = slice(n * CHUNK, (n + 1) * CHUNK)
                    c.add(dve.tensor_tensor_scan(run[:, t, part], ones[:, part], ld[:, t, part], 0.0,
                                                 ALU.mult, ALU.add))
            c.settle()
            for t in range(2):
                ends = run[:, t].rearrange("p (n w) -> p n w", w=CHUNK)[:, :, CHUNK - 1]
                c.add(dve.tensor_scalar(tot[:, t], ends, 1.0, None, ALU.mult))
                c.link(dve.tensor_scalar(mid[:, t], ends, 0.5, None, ALU.mult))
                c.link(dve.tensor_tensor(run[:, t].rearrange("p (n w) -> p n w", w=CHUNK),
                                         run[:, t].rearrange("p (n w) -> p n w", w=CHUNK),
                                         mid[:, t].unsqueeze(2).to_broadcast([P, NCH, CHUNK]), ALU.subtract))
                c.link(dve.tensor_tensor(ld[:, t], run[:, t], ld[:, t], ALU.subtract))
            dve.wait_ge(sums_done, 1)
            for t in range(2):
                c.link(dve.tensor_scalar(work[:, t], psum[:, 4 + t], 1e-24, None, ALU.max))
            dve.wait_ge(a, 7 + 2)
            for t in range(2):
                c.link(dve.reciprocal(work[:, t], root[:, t]))
                c.link(dve.tensor_tensor(kk[:, t], kk[:, t], work[:, t], ALU.mult))
            dve.wait_ge(a, 9 + 6)
            for t in range(2):
                c.add(dve.tensor_tensor(r_in[:, t], mixed[:, t], e_pos[:, t], ALU.mult))
                c.link(dve.scalar_tensor_tensor(a_in[:, t], kk[:, t], -1.0, e_before[:, t], ALU.mult, ALU.mult))
                c.link(dve.tensor_tensor(kk[:, t], kk[:, t], rate[:, t], ALU.mult))
                c.add(dve.tensor_tensor(b_in[:, t], kk[:, t], e_neg[:, t], ALU.mult))
                c.link(dve.tensor_scalar(rate[:, t], rate[:, t], 1.0, None, ALU.subtract))
                c.link(dve.tensor_scalar(rate[:, t], rate[:, t], cols["k_a"][:, t:t + 1], 1.0, ALU.mult, ALU.add))
                c.link(dve.tensor_tensor(rate[:, t], rate[:, t], mixed[:, 2 + t], ALU.mult))
                c.add(dve.tensor_tensor(k_in[:, t], rate[:, t], e_neg[:, t], ALU.mult))
                c.link(dve.scalar_tensor_tensor(work[:, t], mixed[:, t], cols["r_k"][:, t:t + 1], rate[:, t],
                                                ALU.mult, ALU.mult))
                c.add(dve.tensor_copy(v_in[:, t], mixed[:, 4 + t]))
            dve.wait_ge(sums_done, 2)
            for t in range(2):
                c.add(dve.tensor_tensor(bonus[:, t], psum[:, 6 + t], mixed[:, 4 + t], ALU.mult))

        @block.scalar
        def _(act):
            c = Count(act, a)
            act.wait_ge(v, 2)
            c.add(act.activation(low[0:32], mixed[0:32, 6], ACT.Tanh))
            c.add(act.activation(low[32:64], mixed[32:64, 6], ACT.Identity))
            c.add(act.activation(low[64:128], mixed[64:128, 6], ACT.Sigmoid))
            act.wait_ge(up_done, 1)
            for t in range(2):
                c.add(act.activation(ld[:, t], psum[:, t], ACT.Sigmoid, bias=cols["w0"][:, t:t + 1]))
                c.add(act.activation(rate[:, t], psum[:, 2 + t], ACT.Sigmoid, bias=cols["a0"][:, t:t + 1]))
            act.wait_ge(v, 39)
            for t in range(2):
                c.add(act.activation(root[:, t], work[:, t], ACT.Sqrt))
            for t in range(2):
                c.add(act.activation(e_pos[:, t], run[:, t], ACT.Exp))
                c.add(act.activation(e_before[:, t], ld[:, t], ACT.Exp))
                c.add(act.activation(e_neg[:, t], run[:, t], ACT.Exp, scale=-1.0))
            act.wait_ge(up_done, 2)
            for t in range(2):
                c.add(act.activation(gate[:, t], psum[:, t], ACT.Copy))

        @block.tensor
        def _(pe):
            pe.wait_ge(a, 3)
            for t in range(2):
                c = slice(t * P, (t + 1) * P)
                pe.matmul(psum[:, t], w_up[0:32, c], low[0:32], start=True, stop=True)
                mm = pe.matmul(psum[:, 2 + t], w_up[32:64, c], low[32:64], start=True, stop=True)
            mm.then_inc(up_done, 1)
            pe.wait_ge(v, 19)
            for t in range(2):
                mm = pe.matmul(psum[:, 4 + t], square[:, HEADS], work[:, t], start=True, stop=True)
            mm.then_inc(sums_done, 1)
            pe.wait_ge(a, 7)
            for t in range(2):
                mm = pe.matmul(psum[:, t], w_up[64:128, t * P:(t + 1) * P], low[64:128], start=True, stop=True)
            mm.then_inc(up_done, 1)
            pe.wait_ge(v, 63)
            for t in range(2):
                mm = pe.matmul(psum[:, 6 + t], square[:, HEADS], work[:, t], start=True, stop=True)
            mm.then_inc(sums_done, 1)


def rwkv_chunks(nc, old, square, r_in, a_in, k_in, b_in, v_in, tot, mid, y):
    H = 4
    with Stage(nc, "rwkv", old) as s:
        ab = s.sb("ab", [P, NCH, H * P])
        ak = s.sb("ak", [P, NCH, H * P])
        rb = s.sb("rb", [P, NCH, H * P])
        rk = s.sb("rk", [P, NCH, H * P])
        tok = s.sb("tok", [P, NCH, 3, 2 * P])
        inv = s.sb("inv", [P, NCH, H * P])
        inv_t = s.sb("inv_t", [P, NCH, H * P])
        quarter = s.sb("quarter", [P, NCH, H * P])
        half = s.sb("half", [P, 2, H * P])
        state = s.sb("state", [P, 2, HD])
        centred = s.sb("centred", [P, 2, HD])
        z = s.sb("z", [P, H, HD])
        u = s.sb("u", [P, H, HD])
        factors = s.sb("factors", [P, 2, 2, NCH])
        psum = s.ps("psum", 8)
        g_done, g_kept, t_done, t_kept = s.sem("gram"), s.sem("gram_kept"), s.sem("turned"), s.sem("turned_kept")
        q_ready, h_done, h_kept, x_done, x_kept = (s.sem(n) for n in
                                                   ("quarter", "half", "half_kept", "inv", "inv_kept"))
        fac, c_done, c_kept = s.sem("factors"), s.sem("chain"), s.sem("chain_kept")
        y_done, y_kept = s.sem("y"), s.sem("y_kept")
        block = s.block()
        ident = square[:, IDENT]

        def rows(h):
            return slice(HD * (h % 2), HD * (h % 2) + HD)

        def cols(n):
            return slice(n * CHUNK, (n + 1) * CHUNK)

        def bank4(ap, h):
            return ap[:, h * P:(h + 1) * P]

        grams = [(ab, b_in, a_in, STRICT), (ak, k_in, a_in, STRICT), (rb, b_in, r_in, INCL), (rk, k_in, r_in, INCL)]

        def second_half(pe, i):
            level, n = divmod(i, NCH)
            pe.wait_ge(h_kept, i + 1)
            if i >= 1:
                pe.wait_ge(x_kept, 2 * i)
            for h in range(H):
                mm = pe.matmul(bank4(psum[:, 2], h), bank4(inv_t[:, n], h), bank4(half[:, i % 2], h),
                               start=True, stop=True)
            for h in range(H):
                mm = pe.matmul(bank4(psum[:, 3], h), bank4(half[:, i % 2], h), bank4(inv_t[:, n], h),
                               start=True, stop=True)
            mm.then_inc(x_done, 1)

        @block.tensor
        def _(pe):
            g = 0
            for dst, left, right, _ in grams:
                for n in range(NCH):
                    if g >= 2:
                        pe.wait_ge(g_kept, g - 1)
                    for h in range(H):
                        mm = pe.matmul(bank4(psum[:, 2 * (g % 2) + h % 2], h // 2), left[rows(h), h // 2, cols(n)],
                                       right[rows(h), h // 2, cols(n)], start=True, stop=True)
                    mm.then_inc(g_done, 1)
                    g += 1
            for i, src in enumerate((b_in, k_in, v_in)):
                for n in range(NCH):
                    q = i * NCH + n
                    if q >= 2:
                        pe.wait_ge(t_kept, q - 1)
                    for t in range(2):
                        mm = pe.transpose(psum[:, 4 + q % 2, t * P:(t + 1) * P], src[:, t, cols(n)], ident)
                    mm.then_inc(t_done, 1)
            pe.wait_ge(g_kept, 16)
            i = 0
            for level in range(7):
                for n in range(NCH):
                    pe.wait_ge(q_ready, i + 1)
                    if i >= NCH:
                        pe.wait_ge(x_kept, 2 * (i - NCH) + 2)
                    if i >= 2:
                        pe.wait_ge(h_kept, i - 1)
                    for h in range(H):
                        mm = pe.matmul(bank4(psum[:, i % 2], h), bank4(quarter[:, n], h), bank4(inv[:, n], h),
                                       start=True, stop=True)
                    mm.then_inc(h_done, 1)
                    if i >= 1:
                        second_half(pe, i - 1)
                    i += 1
            second_half(pe, i - 1)
            m = 0
            for n in range(NCH):
                pe.wait_ge(c_kept, 3 * n + 1)
                if n == 0:
                    pe.wait_ge(t_kept, 3 * NCH)
                    pe.wait_ge(x_kept, 2 * 7 * NCH)
                for h in range(H):
                    o = psum[:, h % 2, (h // 2) * HD:(h // 2 + 1) * HD]
                    pe.matmul(o, a_in[rows(h), h // 2, cols(n)], centred[rows(h), h // 2], start=True, stop=False)
                    mm = pe.matmul(o, bank4(ak[:, n], h), tok[:, n, 2, h * HD:(h + 1) * HD],
                                   start=False, stop=True)
                mm.then_inc(c_done, 1)
                pe.wait_ge(c_kept, 3 * n + 2)
                for h in range(H):
                    mm = pe.matmul(psum[:, 2, h * HD:(h + 1) * HD], bank4(inv_t[:, n], h), z[:, h],
                                   start=True, stop=True)
                mm.then_inc(c_done, 1)
                pe.wait_ge(c_kept, 3 * n + 3)
                for h in range(H):
                    o = psum[rows(h), 3, (h // 2) * HD:(h // 2 + 1) * HD]
                    pe.matmul(o, tok[:, n, 0, h * HD:(h + 1) * HD], u[:, h], start=True, stop=False)
                    mm = pe.matmul(o, tok[:, n, 1, h * HD:(h + 1) * HD], tok[:, n, 2, h * HD:(h + 1) * HD],
                                   start=False, stop=True)
                mm.then_inc(c_done, 1)
                if n >= 1:
                    pe.wait_ge(y_kept, n)
                for h in range(H):
                    o = psum[rows(h), 4 + h // 2, 0:P]
                    pe.matmul(o, centred[rows(h), h // 2], r_in[rows(h), h // 2, cols(n)], start=True, stop=False)
                    pe.matmul(o, u[:, h], bank4(rb[:, n], h), start=False, stop=False)
                    mm = pe.matmul(o, tok[:, n, 2, h * HD:(h + 1) * HD], bank4(rk[:, n], h),
                                   start=False, stop=True)
                mm.then_inc(y_done, 1)

        @block.scalar
        def _(act):
            for q in range(3 * NCH):
                act.wait_ge(t_done, q + 1)
                act.activation(tok[:, q % NCH, q // NCH], psum[:, 4 + q % 2, 0:2 * P], ACT.Copy).then_inc(t_kept, 1)
            act.activation(factors[:, 0].rearrange("p t n -> p (t n)"), mid[:].rearrange("p t n -> p (t n)"),
                           ACT.Exp).then_inc(fac, 1)
            act.activation(factors[:, 1].rearrange("p t n -> p (t n)"), tot[:].rearrange("p t n -> p (t n)"),
                           ACT.Exp).then_inc(fac, 1)
            for i in range(7 * NCH):
                act.wait_ge(h_done, i + 1)
                if i >= 2:
                    act.wait_ge(x_done, i - 1)
                act.activation(half[:, i % 2], psum[:, i % 2], ACT.Copy).then_inc(h_kept, 1)
            for n in range(NCH):
                act.wait_ge(y_done, n + 1)
                for t in range(2):
                    last = act.activation(y[:, t, cols(n)], psum[:, 4 + t, 0:P], ACT.Copy)
                last.then_inc(y_kept, 1)

        @block.gpsimd
        def _(pool):
            for i in range(7 * NCH):
                level, n = divmod(i, NCH)
                pool.wait_ge(g_kept, n + 1)
                if level:
                    pool.wait_ge(h_done, i - NCH + 1)
                pool.tensor_tensor(quarter[:, n].rearrange("p (h t) -> p h t", h=H),
                                   ab[:, n].rearrange("p (h t) -> p h t", h=H),
                                   square[:, LEVELS + level].unsqueeze(1).to_broadcast([P, H, P]), ALU.mult)\
                    .then_inc(q_ready, 1)

        @block.vector
        def _(dve):
            g = 0
            for n in range(NCH):
                for x in (inv, inv_t):
                    dve.tensor_copy(x[:, n].rearrange("p (h t) -> p h t", h=H),
                                    ident.unsqueeze(1).to_broadcast([P, H, P]))
            for dst, _, _, mask in grams:
                for n in range(NCH):
                    dve.wait_ge(g_done, g + 1)
                    for odd in range(2):
                        last = dve.tensor_tensor(
                            dst[:, n].rearrange("p (q r t) -> p r q t", q=2, r=2)[:, odd],
                            psum[:, 2 * (g % 2) + odd, 0:2 * P].rearrange("p (q t) -> p q t", q=2),
                            square[:, mask].unsqueeze(1).to_broadcast([P, 2, P]), ALU.mult)
                    last.then_inc(g_kept, 1)
                    g += 1
            for i in range(7 * NCH):
                n = i % NCH
                dve.wait_ge(x_done, i + 1)
                dve.tensor_tensor(inv[:, n], inv[:, n], psum[:, 2], ALU.add).then_inc(x_kept, 1)
                dve.tensor_tensor(inv_t[:, n], inv_t[:, n], psum[:, 3], ALU.add).then_inc(x_kept, 1)
            c = Count(dve, c_kept)
            dve.memset(state[:], 0.0)
            c.link(dve.memset(centred[:], 0.0))
            dve.wait_ge(fac, 2)
            for n in range(NCH):
                dve.wait_ge(c_done, 3 * n + 1)
                for odd in range(2):
                    last = dve.tensor_copy(z[:].rearrange("p (q r) d -> p r q d", r=2)[:, odd],
                                           psum[:, odd, 0:2 * HD].rearrange("p (q d) -> p q d", q=2))
                c.add(last)
                dve.wait_ge(c_done, 3 * n + 2)
                c.add(dve.tensor_copy(u[:].rearrange("p h d -> p (h d)"), psum[:, 2, 0:H * HD]))
                dve.wait_ge(c_done, 3 * n + 3)
                if n == NCH - 1:
                    break
                for t in range(2):
                    dve.tensor_scalar(state[:, t], state[:, t], factors[:, 1, t, n:n + 1], None, ALU.mult)\
                       .then_inc(fac, 1)
                dve.wait_ge(fac, 2 + 4 * n + 2)
                for t in range(2):
                    dve.scalar_tensor_tensor(state[:, t], psum[:, 3, t * HD:(t + 1) * HD],
                                             factors[:, 0, t, n:n + 1], state[:, t], ALU.mult, ALU.add)\
                       .then_inc(fac, 1)
                dve.wait_ge(fac, 2 + 4 * n + 4)
                dve.wait_ge(y_done, n + 1)
                dve.tensor_scalar(centred[:, 0], state[:, 0], factors[:, 0, 0, n + 1:n + 2], None, ALU.mult)
                c.add(dve.tensor_scalar(centred[:, 1], state[:, 1], factors[:, 0, 1, n + 1:n + 2], None, ALU.mult))


def rwkv_output(nc, old, y, gate, bonus, cols, square, out):
    with Stage(nc, "rwkv_out", old) as s:
        work = s.sb("work", [P, 2, T])
        rstd = s.sb("rstd", [P, 2, T])
        eps = s.sb("eps", [P, 1])
        psum = s.ps("psum", 4)
        v, a, m = s.sem("dve"), s.sem("act"), s.sem("sums")
        block = s.block()

        @block.tensor
        def _(pe):
            for t in range(2):
                pe.matmul(psum[:, t], square[:, HEADS], y[:, t], start=True, stop=True).then_inc(m, 1)
            for t in range(2):
                pe.wait_ge(a, t + 1)
                pe.matmul(psum[:, 2 + t], square[:, HEADS], work[:, t], start=True, stop=True).then_inc(m, 1)

        @block.scalar
        def _(act):
            c = Count(act, a)
            for t in range(2):
                act.wait_ge(v, 2 + t)
                c.add(act.activation(work[:, t], y[:, t], ACT.Square))
            for t in range(2):
                act.wait_ge(m, 3 + t)
                c.link(act.activation(rstd[:, t], psum[:, 2 + t], ACT.Ln, bias=eps[:, 0:1], scale=1.0 / HD))
            for t in range(2):
                c.link(act.activation(rstd[:, t], rstd[:, t], ACT.Exp, scale=-0.5))

        @block.vector
        def _(dve):
            c = Count(dve, v)
            c.link(dve.memset(eps[:], GN_EPS))
            for t in range(2):
                dve.wait_ge(m, t + 1)
                c.link(dve.scalar_tensor_tensor(y[:, t], psum[:, t], -1.0 / HD, y[:, t], ALU.mult, ALU.add))
            dve.wait_ge(a, 6)
            for t in range(2):
                c.link(dve.scalar_tensor_tensor(y[:, t], y[:, t], cols["ln_w"][:, t:t + 1], rstd[:, t],
                                                ALU.mult, ALU.mult))
                c.link(dve.scalar_tensor_tensor(y[:, t], y[:, t], cols["ln_b"][:, t:t + 1], bonus[:, t],
                                                ALU.add, ALU.add))
                c.link(dve.tensor_tensor(out[:, t], y[:, t], gate[:, t], ALU.mult))



def distance_tables(nc, old, onehot, bias, scratch, tables):
    kinds = [0] * H_NSA + [1] * 4 + [2] * 4 + [3] * 4 + [4] * (B_HEADS + C_HEADS + 1)
    groups, start = [], 0
    for h in range(1, N_TABLES + 1):
        if h == N_TABLES or kinds[h] != kinds[start]:
            groups.append((start, h, kinds[start]))
            start = h
    half = TABLE_LEN // 2
    with Stage(nc, "tables", old) as s:
        hot = s.sb("hot", [33, 5, TABLE_LEN])
        rows = s.sb("rows", [32, len(groups), TABLE_LEN])
        psum = s.ps("psum", 4)
        loaded, done, kept, out = s.sem("loaded"), s.sem("done"), s.sem("kept"), s.sem("out")
        block = s.block()

        @block.sync
        def _(sp):
            sp.dma_start(hot[:], onehot).then_inc(loaded, 16)
            for g, (a, b, _) in enumerate(groups):
                sp.wait_ge(kept, 2 * g + 2)
                sp.dma_start(scratch[a:b, :], rows[0:b - a, g]).then_inc(out, 16)
            sp.wait_ge(out, 16 * len(groups))
            for a in range(0, N_TABLES, 9):
                rows_at = scratch[a:a + 9, :]
                sp.dma_start(tables[a:a + 9], bass.AP(rows_at.tensor, rows_at.offset + P - 1,
                                                      [[TABLE_LEN, 9], [-1, P], [1, T]])).then_inc(out, 16)
            sp.wait_ge(out, 16 * (len(groups) + 3))

        @block.tensor
        def _(pe):
            pe.wait_ge(loaded, 16)
            for g, (a, b, kind) in enumerate(groups):
                for c in range(2):
                    i = 2 * g + c
                    if i >= 4:
                        pe.wait_ge(kept, i - 3)
                    pe.matmul(psum[0:b - a, i % 4, 0:half], bias[:, a:b], hot[:, kind, c * half:(c + 1) * half],
                              start=True, stop=True).then_inc(done, 1)

        @block.vector
        def _(dve):
            for g, (a, b, _) in enumerate(groups):
                for c in range(2):
                    i = 2 * g + c
                    dve.wait_ge(done, i + 1)
                    dve.tensor_copy(rows[0:b - a, g, c * half:(c + 1) * half], psum[0:b - a, i % 4, 0:half])\
                       .then_inc(kept, 1)


def table_tile(tables, head):
    return tables[bass.ds(head, 1)].rearrange("a p t -> (a p) t") if not isinstance(head, int) else tables[head]


class Piece:

    def __init__(self, q, k, v, lo, keys, table, extra=None, plus=None, table_no=0):
        self.q, self.k, self.v, self.lo, self.keys, self.table = q, k, v, lo, keys, table
        self.extra, self.plus, self.table_no = extra, plus, table_no


def attention(nc, old, name, pairs, units, width, tables, staging, finish, fixed_tables=False):
    pieces = [(u, c, piece) for u, unit in enumerate(units) for c, piece in enumerate(unit)]
    n_pieces, n_units = len(pieces), len(units)
    assert n_pieces % 4 == 0 and n_units % 8 == 0
    last_of = [max(i for i, (u, _, _) in enumerate(pieces) if u == w) for w in range(n_units)]
    first_of = [min(i for i, (u, _, _) in enumerate(pieces) if u == w) for w in range(n_units)]
    with Stage(nc, name, old) as s:
        scores = s.sb("scores", [P, 4, T])
        turned = s.sb("turned", [P, 2, T])
        peak = s.sb("peak", [P, 8, 4])
        sums = s.sb("sums", [P, 8, 4])
        weight = s.sb("weight", [P, 8])
        spacer = s.sb("spacer", [1, 8])
        psum = s.ps("psum", 8)
        staged = s.sem("staged")
        tabled = [s.sem(f"tabled{n}") for n in range(len(tables))]
        scored, biased, peaked, exped = s.sem("scored"), s.sem("biased"), s.sem("peaked"), s.sem("exped")
        turn, copied, weighed, finished = s.sem("turn"), s.sem("copied"), s.sem("weighed"), s.sem("finished")
        small, done = s.sem("small"), s.sem("done")
        block = s.block()
        n_staged = staging(None, 0, None) if staging else 0

        def over_pairs(eng, body):
            if pairs == 1:
                body(0)
            else:
                with eng.Fori(0, pairs) as p:
                    body(p)

        @block.sync
        def _(sp):
            def load(p):
                for n, (dst, src, last_unit) in enumerate(tables):
                    sp.wait_ge(biased, p * n_pieces + last_of[last_unit] + 1)
                    sp.dma_start(dst, src(p)).then_inc(tabled[n], 16)
            over_pairs(sp, load)

        @block.gpsimd
        def _(pool):
            if not staging:
                return
            def stage(p):
                pool.wait_ge(biased, p * n_pieces + n_pieces)
                staging(pool, p, staged)
            over_pairs(pool, stage)

        @block.tensor
        def _(pe):
            pe.sem_inc(turn, 4)
            pe.sem_inc(weighed, 2)

            def body(p):
                pe.wait_ge(staged, p * n_staged + n_staged)
                for i in range(n_pieces + 3):
                    if i < n_pieces:
                        u, c, x = pieces[i]
                        pe.wait_ge(biased, p * n_pieces + n_pieces + i - 3)
                        cols = slice(x.lo * P, x.lo * P + x.keys)
                        mm = pe.matmul(psum[:, i % 4, 0:x.keys], x.q, x.k[:, cols], start=True,
                                       stop=x.extra is None)
                        if x.extra is not None:
                            mm = pe.matmul(psum[:, i % 4, 0:x.keys], x.extra[0], x.extra[1][:, cols],
                                           start=False, stop=True)
                        mm.then_inc(scored, 1)
                    if 2 <= i < n_pieces + 2:
                        t = i - 2
                        x = pieces[t][2]
                        pe.wait_ge(exped, p * n_pieces + t + 1)
                        pe.wait_ge(copied, p * n_pieces + t + 1)
                        for j in range(-(-x.keys // P)):
                            n = min(P, x.keys - j * P)
                            mm = pe.transpose(psum[0:n, 4 + t % 2, j * P:j * P + P],
                                              scores[:, t % 4, j * P:j * P + n], attention.ident)
                        mm.then_inc(turn, 1)
                    if i >= 3:
                        t = i - 3
                        u, c, x = pieces[t]
                        pe.wait_ge(copied, p * n_pieces + t + 3)
                        if c == 0:
                            pe.wait_ge(finished, p * n_units + u + 1)
                        blocks = -(-x.keys // P)
                        for j in range(blocks):
                            n = min(P, x.keys - j * P)
                            mm = pe.matmul(psum[:, 6 + u % 2, 0:width],
                                           turned[0:n, t % 2, j * P:j * P + P], x.v(x.lo + j, p),
                                           start=c == 0 and j == 0, stop=t == last_of[u] and j == blocks - 1)
                        mm.then_inc(weighed, 1)
            over_pairs(pe, body)

        @block.scalar
        def _(act):
            act.sem_inc(copied, 2)

            def body(p):
                for i in range(n_pieces + 2):
                    if i >= 2:
                        t = i - 2
                        x = pieces[t][2]
                        act.wait_ge(turn, p * n_pieces + t + 5)
                        act.wait_ge(weighed, p * n_pieces + t + 1)
                        n = min(P, x.keys)
                        w = -(-x.keys // P) * P
                        act.activation(turned[0:n, t % 2, 0:w], psum[0:n, 4 + t % 2, 0:w], ACT.Copy)\
                           .then_inc(copied, 1)
                    if i < n_pieces:
                        u, c, x = pieces[i]
                        act.wait_ge(peaked, p * n_units + u + 1)
                        b = scores[:, i % 4, 0:x.keys]
                        act.activation(b, b, ACT.Exp, bias=peak[:, u % 8, 3:4],
                                       accum_out=sums[:, u % 8, c:c + 1]).then_inc(exped, 1)
            over_pairs(act, body)

        @block.vector
        def _(dve):
            dve.sem_inc(biased, n_pieces)
            dve.sem_inc(finished, 2)
            small_c, done_c = Count(dve, small), Count(dve, done)

            def end(p, u, count):
                dve.wait_ge(weighed, p * n_pieces + last_of[u] + 3)
                total = sums[:, u % 8, 0:1]
                for c in range(1, len(units[u])):
                    count.link(dve.tensor_tensor(total, total, sums[:, u % 8, c:c + 1], ALU.add))
                count.link(dve.tensor_scalar(total, total, 1e-30, None, ALU.max))
                count.link(dve.reciprocal(weight[:, u % 8:u % 8 + 1], total))
                finish(dve, p, u, psum[:, 6 + u % 2, 0:width], weight[:, u % 8:u % 8 + 1], count,
                       finished)

            def body(p):
                small_c.enter(p * body.per)
                for i in range(n_pieces + 4):
                    if i < n_pieces:
                        u, c, x = pieces[i]
                        if tables:
                            dve.wait_ge(tabled[x.table_no], p * 16 + 16)
                        dve.wait_ge(scored, p * n_pieces + i + 1)
                        dve.wait_ge(turn, p * n_pieces + i + 1)
                        raw = psum[:, i % 4, 0:x.keys]
                        out = scores[:, i % 4, 0:x.keys]
                        if x.plus is not None:
                            small_c.link(dve.tensor_tensor(out, raw, x.plus, ALU.add))
                            raw = out
                        dve.memset(spacer[:, i % 8:i % 8 + 1], 0.0)
                        dve.tensor_tensor_reduce(out, raw, x.table, 1.0, LOWEST, ALU.add, ALU.max,
                                                 peak[:, u % 8, c:c + 1]).then_inc(biased, 1)
                        if i == last_of[u]:
                            dve.wait_ge(biased, p * n_pieces + n_pieces + i + 1)
                            for d in range(1, c + 1):
                                small_c.link(dve.tensor_tensor(peak[:, u % 8, 0:1], peak[:, u % 8, 0:1],
                                                               peak[:, u % 8, d:d + 1], ALU.max))
                            dve.tensor_scalar(peak[:, u % 8, 3:4], peak[:, u % 8, 0:1], -1.0, None, ALU.mult)\
                               .then_inc(peaked, 1)
                    if i >= 4 and pieces[i - 4][0] in range(n_units) and last_of[pieces[i - 4][0]] == i - 4:
                        end(p, pieces[i - 4][0], small_c)
                body.made = small_c.n
            body.per = sum(len(x) - 1 for x in units) * 2 + 2 * n_units + sum(x.plus is not None for _, _, x in pieces)\
                + n_units * finish.steps
            over_pairs(dve, body)
            assert body.made == body.per, (body.made, body.per)


def to_channels(nc, old, name, ident, tiles, scale=1.0):
    with Stage(nc, name, old) as s:
        psum = s.ps("psum", 2)
        done, kept = s.sem("done"), s.sem("kept")
        block = s.block()

        @block.tensor
        def _(pe):
            for n, (src, _) in enumerate(tiles):
                if n >= 2:
                    pe.wait_ge(kept, n - 1)
                for i in range(TT):
                    mm = pe.transpose(psum[:, n % 2, i * P:(i + 1) * P], src[:, i], ident)
                mm.then_inc(done, 1)

        @block.scalar
        def _(act):
            for n, (_, dst) in enumerate(tiles):
                act.wait_ge(done, n + 1)
                act.activation(dst, psum[:, n % 2], ACT.Copy, scale=scale).then_inc(kept, 1)


def fox_decay(nc, old, logit, b_f, heads, left, right):
    with Stage(nc, "fox_decay", old) as s:
        x = s.sb("x", [H_FOX, T])
        e = s.sb("e", [H_FOX, T])
        n = s.sb("n", [H_FOX, T])
        ones = s.sb("ones", [H_FOX, T])
        v, a = s.sem("dve"), s.sem("act")
        block = s.block()
        r = slice(0, H_FOX)

        @block.vector
        def _(dve):
            c = Count(dve, v)
            c.add(dve.memset(left[:], 1.0))
            c.add(dve.memset(right[:], 1.0))
            c.add(dve.memset(ones[:], 1.0))
            c.link(dve.tensor_scalar(x[:], logit[0:H_FOX], b_f, None, ALU.add))
            c.link(dve.scalar_tensor_tensor(e[:], x[:], -1.0, x[:], ALU.mult, ALU.min))
            c.link(dve.tensor_scalar(x[:], x[:], 0.0, None, ALU.min))
            dve.wait_ge(a, 2)
            c.link(dve.tensor_tensor(n[:], x[:], e[:], ALU.subtract))
            c.link(dve.tensor_tensor_scan(left[0:H_FOX], ones[:], n[:], 0.0, ALU.mult, ALU.add))
            c.add(dve.tensor_copy(left[HD:HD + H_FOX], left[0:H_FOX]))
            for base in (32, HD + 32):
                c.add(dve.tensor_scalar(right[base:base + H_FOX], left[0:H_FOX], -1.0, None, ALU.mult))

        @block.scalar
        def _(act):
            act.wait_ge(v, 6)
            act.activation(e[:], e[:], ACT.Exp).then_inc(a, 1)
            act.wait_ge(a, 1)
            act.activation(e[:], e[:], ACT.Ln, bias=1.0).then_inc(a, 1)


def fox_attention(nc, old, pj, fv, left, right, heads, scratch, out):
    ctx = ExitStack()
    with ctx:
        qs = ctx.enter_context(nc.sbuf_tensor("fox_qs", [P, T], F32))
        ks = ctx.enter_context(nc.sbuf_tensor("fox_ks", [P, T], F32))
        rh = ctx.enter_context(nc.sbuf_tensor("fox_rh", [P, T], F32))
        table = ctx.enter_context(nc.sbuf_tensor("fox_table", [P, T], F32))

        def staging(pool, p, sem):
            if pool is None:
                return 3
            pool.tensor_tensor(qs[:], flat(pj[:, bass.ds(RW_TILES + p, 1), 1:T + 1]), attention.scale, ALU.mult)\
                .then_inc(sem, 1)
            pool.tensor_copy(ks[:], flat(pj[:, bass.ds(RW_TILES + 3 + p, 1), 1:T + 1])).then_inc(sem, 1)
            pool.tensor_tensor(rh[:], right[:], heads[:, bass.ds(p, 1)].to_broadcast([P, T]), ALU.mult).then_inc(sem, 1)

        units = []
        where = []
        for a in range(2):
            for i in reversed(range(TT)):
                q = slice(i * P, (i + 1) * P)
                h = slice(a * HD, (a + 1) * HD)
                units.append([Piece(qs[h, q], ks[h], lambda j, p, a=a: flat(fv[:, j:j + 1, bass.ds(p * P + a * HD, HD)]), 0, (i + 1) * P,
                                    table[:, (TT - 1 - i) * P:], extra=(left[h, q], rh[h]))])
                where.append((a, i))

        def finish(dve, p, u, o, w, count, sem):
            a, i = where[u]
            dve.tensor_scalar(out[:, i, bass.ds(p * P + a * HD, HD)], o, w, None, ALU.mult).then_inc(sem, 1)
        finish.steps = 0
        attention(nc, old, "fox", 3, units, HD, [(table[:], lambda p: table_tile(scratch, TAB_FOX), 7)],
                  staging, finish)


def nsa_compress(nc, old, nk, pe_cols, w1s, w2, kcmp, vcmp):
    with Stage(nc, "compress", old) as s:
        w1 = s.sb("w1", [P, 2, L_CMP, CMP_HID])
        hid = s.sb("hid", [P, 4, 32])
        pos = s.sb("pos", [P, 2])
        x = s.sb("x", [P, 4, 32])
        w = s.sb("w", [P, 4, 32])
        psum = s.ps("psum", 5)
        loaded, done, v, a, kept = s.sem("loaded"), s.sem("done"), s.sem("dve"), s.sem("act"), s.sem("kept")
        block = s.block()

        @block.sync
        def _(sp):
            for n in range(2):
                for g in range(2):
                    sp.dma_start(w1[g * HD:(g + 1) * HD, n], w1s[n]).then_inc(loaded, 16)

        @block.tensor
        def _(pe):
            pe.wait_ge(loaded, 64)
            for n in range(2):
                for g in range(2):
                    rows = slice(g * HD, (g + 1) * HD)
                    for l in range(L_CMP):
                        tokens = nk[rows, n, l:l + D_CMP * (N_CMP - 1) + 1:D_CMP]
                        mm = pe.matmul(psum[:, 2 * n + g, 0:N_CMP], w1[rows, n, l], tokens,
                                       start=l == 0, stop=l == L_CMP - 1)
                for l in range(L_CMP):
                    mm = pe.matmul(psum[:, 4, n:n + 1], w1[0:HD, n, l], pe_cols[0:HD, n, l:l + 1],
                                   start=l == 0, stop=l == L_CMP - 1)
                mm.then_inc(done, 1)
            pe.wait_ge(v, 7)
            for g in range(2):
                pe.matmul(psum[g * HD:(g + 1) * HD, 0, 0:N_CMP], w2[:, 0], hid[:, g, 0:N_CMP],
                          start=True, stop=True)
                mm = pe.matmul(psum[0:N_CMP, 1 + g, 0:HD], hid[:, 2 + g, 0:N_CMP], w2[:, 1], start=True, stop=True)
            mm.then_inc(done, 1)

        @block.vector
        def _(dve):
            c = Count(dve, v)
            dve.wait_ge(done, 2)
            c.link(dve.tensor_copy(pos[:], psum[:, 4, 0:2]))
            for n in range(2):
                c.add(dve.tensor_scalar(x[:, 2 * n:2 * n + 2, 0:N_CMP], psum[:, 2 * n:2 * n + 2, 0:N_CMP],
                                        pos[:, n:n + 1], None, ALU.add))
            c.settle()
            xv, wv = x[:, :, 0:N_CMP], w[:, :, 0:N_CMP]
            c.link(dve.tensor_tensor(wv, xv, xv, ALU.mult))
            c.link(dve.tensor_scalar(wv, wv, 0.044715, 1.0, ALU.mult, ALU.add))
            c.link(dve.tensor_tensor(wv, wv, xv, ALU.mult))
            dve.wait_ge(a, 1)
            c.link(dve.tensor_tensor(hid[:, :, 0:N_CMP], wv, xv, ALU.mult))
            dve.wait_ge(done, 3)
            dve.tensor_copy(kcmp[:], psum[:, 0, 0:N_CMP])
            dve.tensor_copy(vcmp[:, 0], psum[0:N_CMP, 1, 0:HD])
            dve.tensor_copy(vcmp[:, 1], psum[0:N_CMP, 2, 0:HD]).then_inc(kept, 1)

        @block.scalar
        def _(act):
            act.wait_ge(v, 6)
            act.activation(w[:, :, 0:N_CMP], w[:, :, 0:N_CMP], ACT.Sigmoid, scale=2.0 * math.sqrt(2.0 / math.pi))\
               .then_inc(a, 1)


def nsa_attention(nc, old, nq, nk, nv, kcmp, vcmp, gates, scratch, out):
    with ExitStack() as ctx:
        qs = ctx.enter_context(nc.sbuf_tensor("nsa_qs", [P, T], F32))
        tables = ctx.enter_context(nc.sbuf_tensor("nsa_tables", [P, 2, T], F32))
        scaled = ctx.enter_context(nc.sbuf_tensor("nsa_scaled", [P, 4], F32))

        def staging(pool, p, sem):
            if pool is None:
                return 1
            pool.tensor_tensor(qs[:], tile_of(nq, p), attention.scale, ALU.mult).then_inc(sem, 1)

        units, where = [], []
        for a in range(2):
            h = slice(a * HD, (a + 1) * HD)
            for i in reversed(range(TT)):
                q = slice(i * P, (i + 1) * P)
                full = tables[:, a, (TT - 1 - i) * P:]
                n_c = 8 * i + 7
                first = (TT - 1 - i) * P + L_CMP - 1
                coarse = tables[:, a, first:first + D_CMP * (n_c - 1) + 1:D_CMP]
                units.append([Piece(qs[h, q], kcmp[h], lambda j, p, a=a, n=n_c: vcmp[0:n, a], 0, n_c, coarse, table_no=a)])
                units.append([Piece(qs[h, q], nk[h, 2], lambda j, p, h=h: nv[:, 0, j, h], 0, (i + 1) * P, full, table_no=a)])
                units.append([Piece(qs[h, q], nk[h, 3], lambda j, p, h=h: nv[:, 1, j, h], 0, (i + 1) * P, full, table_no=a)])
                where += [(a, i, b) for b in range(3)]

        def finish(dve, p, u, o, w, count, sem):
            a, i, b = where[u]
            dst = out[:, i, bass.ds(p * HD + a * 3 * HD, HD)]
            g = scaled[:, u % 4:u % 4 + 1]
            count.link(dve.tensor_tensor(g, w, flat(gates[:, i:i + 1, bass.ds(p * 3 + a * 9 + b, 1)]), ALU.mult))
            if b == 0:
                dve.tensor_scalar(dst, o, g, None, ALU.mult).then_inc(sem, 1)
            else:
                dve.wait_ge(sem, p * len(units) + u + 2)
                dve.scalar_tensor_tensor(dst, o, g, dst, ALU.mult, ALU.add).then_inc(sem, 1)
        finish.steps = 1
        attention(nc, old, "nsa", 3, units, HD,
                  [(tables[:, a], lambda p, a=a: table_tile(scratch, p + 3 * a), 12 * a + 11) for a in range(2)],
                  staging, finish)



def conv_hidden(nc, old, h, up, conv, hidden):
    halves = up.rearrange("k (w n) -> k w n", w=2).rearrange("(k p) w n -> p k w n", p=P)
    with Stage(nc, "conv_up", old) as s:
        st = Stream(s, 2 * KF, KD, lambda j, r: halves[:, :, j % 2, bass.ds((r * (RAW // 2) + j // 2) * P, P)],
                    lambda j, k: [x[:, k] for x in h])
        mixed = s.sb("mixed", [P, 2, 2, T])
        gate = s.sb("gate", [P, 2, T])
        product = s.sb("product", [P, 2, T])
        based, first, gated, made, hidden_hi = (s.sem(n) for n in ("based", "first", "gated", "made", "hidden_hi"))
        block = s.block()

        @block.sync
        def _(sp):
            st.load(sp)

        @block.tensor
        def _(pe):
            st.multiply(pe)

        @block.scalar
        def _(act):
            def take(u, j, r):
                w, b, t = j % 2, j // 2, r * (RAW // 2) + j // 2
                st.wait_products(act, u)
                if w == 0:
                    act.wait_ge(made, t + 1)
                act.activation(mixed[:, b, w], st.bank(j), ACT.Identity,
                               bias=conv(t, w, 3), scale=conv(t, w, 2)).then_inc(based, 1)
                if w == 1:
                    act.wait_ge(st.free, u + st.banks)
                    act.activation(gate[:, b], mixed[:, b, 0], ACT.Silu).then_inc(gated, 1)
                    act.wait_ge(made, t + 3)
                    act.activation(tile_of(hidden[0], t), product[:, b], ACT.Copy).then_inc(hidden_hi, 1)
            rounds_ahead(act, st.units, lambda u, j, r: st.round_hi(act, u, j, r), take)

        @block.vector
        def _(dve):
            dve.sem_inc(st.split, RAW)
            dve.sem_inc(st.free, st.banks)

            def convolve(u, j, r):
                w, b, t = j % 2, j // 2, r * (RAW // 2) + j // 2
                m = mixed[:, b, w]
                dve.wait_ge(based, u + 1)
                dve.scalar_tensor_tensor(m[:, 1:T], st.bank(j)[:, 0:T - 1], conv(t, w, 1), m[:, 1:T],
                                         ALU.mult, ALU.add).then_inc(first, 1)
                dve.wait_ge(first, u + 1)
                dve.scalar_tensor_tensor(m[:, 2:T], st.bank(j)[:, 0:T - 2], conv(t, w, 0), m[:, 2:T],
                                         ALU.mult, ALU.add).then_inc(st.free, 1)
            rounds_ahead(dve, st.units, lambda u, j, r: st.split_lo(dve, u, j, r), convolve)

        @block.gpsimd
        def _(pool):
            pool.sem_inc(made, 2)

            def combine(t, b, r):
                pool.wait_ge(st.free, t * 2 + (2 + st.banks))
                pool.wait_ge(gated, t + 1)
                pool.tensor_tensor(product[:, b], gate[:, b], mixed[:, b, 1], ALU.mult).then_inc(made, 1)
                pool.wait_ge(hidden_hi, t + 1)
                pool.tensor_tensor(tile_of(hidden[1], t), product[:, b], tile_of(hidden[0], t).bitcast(F32),
                                   ALU.subtract)
            rounds(pool, KF, 2, combine)


def glu_hidden(nc, old, name, h, w_gate, w_up, hidden):
    sources = [w.rearrange("(k p) n -> p k n", p=P) for w in (w_gate, w_up)]
    with Stage(nc, name, old) as s:
        st = Stream(s, 2 * KF, KD, lambda j, r: sources[j % 2][:, :, bass.ds((r * (RAW // 2) + j // 2) * P, P)],
                    lambda j, k: [x[:, k] for x in h])
        gate = s.sb("gate", [P, 2, T])
        product = s.sb("product", [P, 2, T])
        gated, hidden_hi, hidden_lo = s.sem("gated"), s.sem("hidden_hi"), s.sem("hidden_lo")
        block = s.block()

        @block.sync
        def _(sp):
            st.load(sp)

        @block.tensor
        def _(pe):
            st.multiply(pe)

        @block.scalar
        def _(act):
            def take(u, j, r):
                b, t = j // 2, r * (RAW // 2) + j // 2
                if j % 2 == 0:
                    st.wait_products(act, u)
                    act.activation(gate[:, b], st.bank(j), ACT.Silu).then_inc(gated, 1)
                else:
                    act.wait_ge(st.free, t * 2 + (2 + st.banks))
                    act.activation(tile_of(hidden[0], t), product[:, b], ACT.Copy).then_inc(hidden_hi, 1)
            rounds_ahead(act, st.units, lambda u, j, r: st.round_hi(act, u, j, r), take)

        @block.vector
        def _(dve):
            dve.sem_inc(st.split, RAW)
            dve.sem_inc(st.free, st.banks)

            def combine(u, j, r):
                if j % 2 == 1:
                    b, t = j // 2, r * (RAW // 2) + j // 2
                    st.wait_products(dve, u)
                    dve.wait_ge(gated, t + 1)
                    dve.wait_ge(hidden_lo, t + 1)
                    dve.tensor_tensor(product[:, b], gate[:, b], st.bank(j), ALU.mult).then_inc(st.free, 2)
            rounds_ahead(dve, st.units, lambda u, j, r: st.split_lo(dve, u, j, r), combine)

        @block.gpsimd
        def _(pool):
            pool.sem_inc(hidden_lo, 2)

            def lower(t, b, r):
                pool.wait_ge(hidden_hi, t + 1)
                pool.tensor_tensor(tile_of(hidden[1], t), product[:, b], tile_of(hidden[0], t).bitcast(F32),
                                   ALU.subtract).then_inc(hidden_lo, 1)
            rounds(pool, KF, 2, lower)



class Pair:

    def __init__(self, nc, name, n):
        self.nc, self.name, self.n = nc, name, n

    def __enter__(self):
        self.ctx = ExitStack()
        return [self.ctx.enter_context(self.nc.sbuf_tensor(f"{self.name}_{part}", [P, self.n, T], F32R))
                for part in ("hi", "lo")]

    def __exit__(self, *exc):
        self.ctx.close()


def tile(pair, k):
    return [x[:, k] for x in pair]


def view(w):
    return w.rearrange("(k p) n -> p k n", p=P)


def first_block(nc, old, A, x_t, gains, mod, cols, square, scratch, heads, b_f):
    with ExitStack() as top:
        def sb(name, shape):
            return top.enter_context(nc.sbuf_tensor("one_" + name, shape, F32))

        y_t = sb("y_t", [P, KD, T])
        w_in = view(A["w_in"][0])
        with ExitStack() as mix:
            def mb(name, shape):
                return mix.enter_context(nc.sbuf_tensor("mix_" + name, shape, F32))
            nq = mb("nq", [P, 3, T])
            nk = mb("nk", [P, 4, T])
            nv = mb("nv", [P, 2, TT, P])
            gates = mb("gates", [P, TT, 3 * H_NSA])
            fv = mb("fv", [P, TT, C_FOX])
            logit = mb("logit", [H_FOX, T])
            pj = mb("pj", [P, RW_TILES + 6, T + 1])

            with Stage(nc, "zero", old) as s:
                block = s.block()
                @block.vector
                def _(dve):
                    dve.memset(pj[:, :, 0:1], 0.0)

            def store(act, t, psum):
                dst = pj[:, t, 1:T + 1] if isinstance(t, int) else flat(pj[:, bass.ds(t, 1), 1:T + 1])
                return act.activation(dst, psum, ACT.Copy)

            def columns_job(loads, dsts):
                return (loads, len(dsts) * P, [("columns", c * P, dst, ACT.Copy) for c, dst in enumerate(dsts)])

            def tokens_job(start, w, dst, func=ACT.Copy):
                return ([(slice(0, w), w_in[:, :, start:start + w])], w,
                        [("tokens", w, [dst(i) for i in range(TT)], func)])

            def adjoining(start, n):
                return [(slice(0, n * P), w_in[:, :, start:start + n * P])]

            def heads_of_groups(c0, n):
                return [(slice((c - c0) * P + g * HD, (c - c0) * P + (g + 1) * HD),
                         w_in[:, :, NSA_Q + (g * 3 + c) * HD:NSA_Q + (g * 3 + c + 1) * HD])
                        for c in range(c0, c0 + n) for g in range(2)]
            jobs = [
                tokens_job(FOX_V, 2 * P, lambda i: fv[:, i, 0:2 * P]),
                tokens_job(FOX_V + 2 * P, P, lambda i: fv[:, i, 2 * P:3 * P]),
                columns_job(heads_of_groups(0, 2), [nq[:, 0], nq[:, 1]]),
                columns_job(heads_of_groups(2, 1), [nq[:, 2]]),
                columns_job(adjoining(NSA_KC, 2), [nk[:, 0], nk[:, 1]]),
                columns_job(adjoining(NSA_KC + 2 * P, 1), [nk[:, 2]]),
                columns_job(adjoining(NSA_KW, 1), [nk[:, 3]]),
                tokens_job(NSA_VS, P, lambda i: nv[:, 0, i]),
                tokens_job(NSA_VW, P, lambda i: nv[:, 1, i]),
                columns_job(adjoining(FOX_F, 1), [logit[0:H_FOX]]),
                tokens_job(NSA_GATE, 3 * H_NSA, lambda i: gates[:, i], ACT.Sigmoid),
            ]
            with Pair(nc, "h1", KD) as h:
                normalise(nc, old, "norm0", lambda k: x_t[:, k], lambda k: gains[:, k:k + 1],
                          shift=lambda k: mod[:, k:k + 1], pair=h)
                column_products(nc, old, "in_a", lambda t, c: w_in[:, :, bass.ds(t * P, P)], RW_TILES + 6,
                                lambda k: tile(h, k), store)
                mixed_products(nc, old, "in_b", h, jobs, 2 * P)

            with ExitStack() as ctx:
                def b(name, shape):
                    return ctx.enter_context(nc.sbuf_tensor("rw_" + name, shape, F32))
                gate, bonus, v_in = b("gate", [P, 2, T]), b("bonus", [P, 2, T]), b("v", [P, 2, T])
                yr = y_t[:, 0:2]
                r_in, a_in, k_in, b_in = (b(n, [P, 2, T]) for n in ("r", "a", "k", "b"))
                tot, mid = b("tot", [P, 2, NCH]), b("mid", [P, 2, NCH])
                with nc.sbuf_tensor("rw_up", [P, C_RWKV], F32) as w_up:
                    with Stage(nc, "load_up", old) as s:
                        sem = s.sem("loaded")
                        block = s.block()
                        @block.sync
                        def _(sp):
                            sp.dma_start(w_up[0:32], A["rwkv_w_up"][0]).then_inc(sem, 16)
                            sp.dma_start(w_up[32:64], A["rwkv_a_up"][0]).then_inc(sem, 16)
                            sp.dma_start(w_up[64:128], A["rwkv_g_up"][0]).then_inc(sem, 16)
                            sp.wait_ge(sem, 48)
                    rwkv_inputs(nc, old, pj, cols, w_up, square, r_in, a_in, k_in, b_in, v_in, gate, bonus, tot, mid)
                rwkv_chunks(nc, old, square, r_in, a_in, k_in, b_in, v_in, tot, mid, yr)
                rwkv_output(nc, old, yr, gate, bonus, cols, square, y_t)

            with nc.sbuf_tensor("fox_tok", [P, TT, C_FOX], F32) as tok:
                with nc.sbuf_tensor("fox_left", [P, T], F32) as left, nc.sbuf_tensor("fox_right", [P, T], F32) as right:
                    fox_decay(nc, old, logit, b_f, heads, left, right)
                    fox_attention(nc, old, pj, fv, left, right, heads, scratch, tok)
                to_channels(nc, old, "fox_turn", square[:, IDENT],
                            [(tok[:, :, c * P:(c + 1) * P], y_t[:, 2 + c]) for c in range(3)])
            with nc.sbuf_tensor("nsa_tok", [P, TT, C_NSA], F32) as tok, nc.sbuf_tensor("nsa_kcmp", [P, N_CMP], F32) as kcmp, \
                    nc.sbuf_tensor("nsa_vcmp", [N_CMP, 2, HD], F32) as vcmp:
                with nc.sbuf_tensor("nsa_w2", [P, 2, HD], F32) as w2:
                    with Stage(nc, "load_w2", old) as s:
                        sem = s.sem("loaded")
                        block = s.block()
                        @block.sync
                        def _(sp):
                            for n, w in enumerate(("nsa_ck_w2", "nsa_cv_w2")):
                                sp.dma_start(w2[:, n], A[w][0]).then_inc(sem, 16)
                            sp.wait_ge(sem, 32)
                    nsa_compress(nc, old, nk, cols["pe"], [A[w][0].rearrange("(l d) c -> d l c", d=HD) for w in
                                                          ("nsa_ck_w1", "nsa_cv_w1")], w2, kcmp, vcmp)
                nsa_attention(nc, old, nq, nk, nv, kcmp, vcmp, gates, scratch, tok)
                to_channels(nc, old, "nsa_turn", square[:, IDENT],
                            [(tok[:, :, c * P:(c + 1) * P], y_t[:, 5 + c]) for c in range(3)])
        with Pair(nc, "y1", KD) as y_pair:
            split_tiles(nc, old, "split1", [y_t[:, k] for k in range(KD)], y_pair)
            project_and_add(nc, old, "out1", A["w_out"][0], lambda k: tile(y_pair, k), x_t,
                            lambda k: gains[:, KD + k:KD + k + 1])
    with Pair(nc, "hidden1", KF) as hidden:
        with Pair(nc, "h2", KD) as h:
            normalise(nc, old, "norm2", lambda k: x_t[:, k], lambda k: gains[:, 2 * KD + k:2 * KD + k + 1],
                      shift=lambda k: mod[:, 3 * KD + k:3 * KD + k + 1], pair=h)
            conv_hidden(nc, old, h, A["ffn_up"][0], cols["conv"], hidden)
        project_and_add(nc, old, "down1", A["ffn_down"][0], lambda k: tile(hidden, k), x_t,
                        lambda k: gains[:, 3 * KD + k:3 * KD + k + 1], chunks=2)


def chunk_view(w, t, c, chunks):
    kt = w.shape[0] // P // chunks
    return view(w)[:, c * kt:(c + 1) * kt, bass.ds(t * P, P)]


def project_and_add(nc, old, name, w, rhs, x_t, gain, chunks=1):
    with nc.sbuf_tensor(name + "_y", [P, KD, T], F32) as y:
        column_products(nc, old, name, lambda t, c: chunk_view(w, t, c, chunks), KD, rhs,
                        lambda act, t, psum: act.activation(tile_of(y, t), psum, ACT.Copy), chunks)
        normalise(nc, old, name + "_norm", lambda k: y[:, k], gain, add_to=lambda k: x_t[:, k])





def head_norms(nc, old, tiles, gain, square):
    with Stage(nc, "head_norms", old) as s:
        squares = s.sb("squares", [P, 2, T])
        rstd = s.sb("rstd", [P, 2, T])
        eps = s.sb("eps", [P, 1])
        psum = s.ps("psum", 4)
        const, squared, summed, logged, rooted, done = (s.sem(n) for n in
                                                        ("const", "squared", "summed", "logged", "rooted", "done"))
        block = s.block()
        n_tiles = len(tiles)

        @block.scalar
        def _(act):
            act.wait_ge(const, 1)
            for n in range(n_tiles + 1):
                if n < n_tiles:
                    if n >= 2:
                        act.wait_ge(summed, n - 1)
                    act.activation(squares[:, n % 2], tiles[n], ACT.Square).then_inc(squared, 1)
                if n >= 1:
                    m = n - 1
                    act.wait_ge(summed, m + 1)
                    if m >= 2:
                        act.wait_ge(done, m - 1)
                    act.activation(rstd[:, m % 2], psum[:, m % 4], ACT.Ln, bias=eps[:, 0:1], scale=1.0 / HD)\
                       .then_inc(logged, 1)
                    act.wait_ge(logged, m + 1)
                    act.activation(rstd[:, m % 2], rstd[:, m % 2], ACT.Exp, scale=-0.5).then_inc(rooted, 1)

        @block.tensor
        def _(pe):
            for n in range(n_tiles):
                pe.wait_ge(squared, n + 1)
                if n >= 4:
                    pe.wait_ge(rooted, n - 3)
                pe.matmul(psum[:, n % 4], square[:, HEADS], squares[:, n % 2], start=True, stop=True)\
                  .then_inc(summed, 1)

        @block.vector
        def _(dve):
            dve.memset(eps[:], EPS).then_inc(const, 1)
            for n in range(n_tiles):
                dve.wait_ge(rooted, n + 1)
                dve.scalar_tensor_tensor(tiles[n], tiles[n], gain(n), rstd[:, n % 2], ALU.mult, ALU.mult)\
                   .then_inc(done, 1)


def dilated_attention(nc, old, qa, va, tables_dram, out):
    with ExitStack() as ctx:
        qs = ctx.enter_context(nc.sbuf_tensor("dil_qs", [P, 3, T], F32))
        ks = ctx.enter_context(nc.sbuf_tensor("dil_ks", [P, 3, T], F32))
        tables = ctx.enter_context(nc.sbuf_tensor("dil_tables", [P, 2, 3, T], F32))

        def staging(pool, p, sem):
            if pool is None:
                return 6
            for g in range(3):
                pool.tensor_tensor(qs[:, g], tile_of(qa, p + 2 * g), attention.scale, ALU.mult).then_inc(sem, 1)
                pool.tensor_copy(ks[:, g], tile_of(qa, p + 6 + 2 * g)).then_inc(sem, 1)

        units, where = [], []
        for a in range(2):
            h = slice(a * HD, (a + 1) * HD)
            for i in reversed(range(TT)):
                unit = []
                for g in range(3):
                    lo = max(0, i - 1) if g == 0 else 0
                    unit.append(Piece(
                        qs[h, g, i * P:(i + 1) * P], ks[h, g],
                        lambda j, p, a=a, g=g: flat(va[:, j:j + 1, bass.ds(p * P + (4 * g + a) * HD, HD)]),
                        lo, (i + 1 - lo) * P, tables[:, a, g, (TT - 1 - i + lo) * P:], table_no=3 * a + g))
                units.append(unit)
                where.append((a, i))

        def finish(dve, p, u, o, w, count, sem):
            a, i = where[u]
            dve.tensor_scalar(out[:, i, bass.ds(p * P + a * HD, HD)], o, w, None, ALU.mult).then_inc(sem, 1)
        finish.steps = 0
        attention(nc, old, "dil", 2, units, HD,
                  [(tables[:, a, g], lambda p, a=a, g=g: table_tile(tables_dram, p * 2 + (TAB_A + 4 * g + a)), 4 * a + 3)
                   for a in range(2) for g in range(3)], staging, finish)


def diff_attention(nc, old, qb, vb, minus_lam, tables_dram, out):
    with ExitStack() as ctx:
        qs = ctx.enter_context(nc.sbuf_tensor("diff_qs", [P, 2, T], F32))
        ks = ctx.enter_context(nc.sbuf_tensor("diff_ks", [P, 2, T], F32))
        tables = ctx.enter_context(nc.sbuf_tensor("diff_tables", [P, 2, T], F32))
        scaled = ctx.enter_context(nc.sbuf_tensor("diff_scaled", [P, 4], F32))

        def staging(pool, p, sem):
            if pool is None:
                return 4
            for m in range(2):
                pool.tensor_tensor(qs[:, m], tile_of(qb, p + 2 * m), attention.scale, ALU.mult).then_inc(sem, 1)
                pool.tensor_copy(ks[:, m], tile_of(qb, p + 4 + 2 * m)).then_inc(sem, 1)

        units, where = [], []
        for a in range(2):
            h = slice(a * HD, (a + 1) * HD)
            for i in reversed(range(TT)):
                for m in range(2):
                    units.append([Piece(
                        qs[h, m, i * P:(i + 1) * P], ks[h, m],
                        lambda j, p, a=a: flat(vb[:, j:j + 1, bass.ds(p * 2 * P + a * P, P)]),
                        0, (i + 1) * P, tables[:, a, (TT - 1 - i) * P:], table_no=a)])
                    where.append((a, i, m))

        def finish(dve, p, u, o, w, count, sem):
            a, i, m = where[u]
            dst = out[:, i, bass.ds(p * 2 * P + a * P, P)]
            g = scaled[:, u % 4:u % 4 + 1]
            count.link(dve.tensor_scalar(g, w, minus_lam if m else 1.0, None, ALU.mult))
            if m == 0:
                dve.tensor_scalar(dst, o, g, None, ALU.mult).then_inc(sem, 1)
            else:
                dve.wait_ge(sem, p * len(units) + u + 2)
                dve.scalar_tensor_tensor(dst, o, g, dst, ALU.mult, ALU.add).then_inc(sem, 1)
        finish.steps = 1
        attention(nc, old, "diff", 2, units, P,
                  [(tables[:, a], lambda p, a=a: table_tile(tables_dram, p * 2 + TAB_B + a), 8 * a + 7)
                   for a in range(2)], staging, finish)


def diff_factor(nc, old, lam_in, minus_lam):
    with Stage(nc, "lam", old) as s:
        prod = s.sb("prod", [P, 2, HD])
        sums = s.sb("sums", [P, 2])
        v, a = s.sem("dve"), s.sem("act")
        block = s.block()
        lv = lam_in[:].rearrange("p (m t d) -> p m t d", m=2, t=2)

        @block.vector
        def _(dve):
            c = Count(dve, v)
            c.link(dve.tensor_tensor(prod[:], lv[:, :, 0], lv[:, :, 1], ALU.mult))
            c.link(dve.tensor_reduce(sums[:], prod[:], AX.X, ALU.add))
            dve.wait_ge(a, 1)
            c.link(dve.tensor_tensor(minus_lam[:], sums[:, 1:2], sums[:, 0:1], ALU.subtract))
            c.link(dve.tensor_scalar(minus_lam[:], minus_lam[:], -LAM_INIT, None, ALU.add))

        @block.scalar
        def _(act):
            act.wait_ge(v, 2)
            act.activation(sums[:], sums[:], ACT.Exp).then_inc(a, 1)


def diff_norm(nc, old, tok):
    with Stage(nc, "diff_norm", old) as s:
        squares = s.sb("squares", [P, TT, B_HEADS, P])
        rstd = s.sb("rstd", [P, TT, B_HEADS])
        v, a = s.sem("dve"), s.sem("act")
        eps = s.sb("eps", [P, 1])
        block = s.block()
        view4 = tok[:].rearrange("p i (h d) -> p (i h) d", h=B_HEADS)
        sq = squares[:].rearrange("p i h d -> p (i h) d")
        r = rstd[:].rearrange("p i h -> p (i h)")

        @block.vector
        def _(dve):
            c = Count(dve, v)
            c.add(dve.memset(eps[:], EPS))
            dve.wait_ge(a, 1)
            c.link(dve.tensor_reduce(r, sq, AX.X, ALU.add))
            dve.wait_ge(a, 3)
            c.link(dve.tensor_tensor(view4, view4, r.unsqueeze(2).to_broadcast([P, TT * B_HEADS, P]), ALU.mult))
            c.link(dve.tensor_scalar(view4, view4, 1.0 - LAM_INIT, None, ALU.mult))

        @block.scalar
        def _(act):
            act.activation(sq, view4, ACT.Square).then_inc(a, 1)
            act.wait_ge(v, 2)
            act.activation(r, r, ACT.Ln, bias=eps[:, 0:1], scale=1.0 / P).then_inc(a, 1)
            act.wait_ge(a, 2)
            act.activation(r, r, ACT.Exp, scale=-0.5).then_inc(a, 1)


def select_keys(nc, old, qi, ki, w_idx, causal, penalty):
    rounds_of_8 = TOPK // 8
    with Stage(nc, "select", old) as s:
        relu = s.sb("relu", [P, 4, T])
        score = s.sb("score", [P, T])
        left = s.sb("left", [P, 2, T])
        top = s.sb("top", [P, 8])
        above = s.sb("above", [P, T])
        equal = s.sb("equal", [P, T])
        place = s.sb("place", [P, T])
        ones = s.sb("ones", [P, T])
        count_above = s.sb("count_above", [P, 1])
        weight = s.sb("weight", [P, TT, IDX_HEADS])
        psum = s.ps("psum", 4)
        done, act_done, summed, v = s.sem("done"), s.sem("relu"), s.sem("summed"), s.sem("dve")
        block = s.block()
        tiles = list(range(1, TT))

        @block.tensor
        def _(pe):
            for n, i in enumerate(tiles):
                for h in range(IDX_HEADS):
                    m = n * IDX_HEADS + h
                    if m >= 4:
                        pe.wait_ge(act_done, m - 3)
                    rows = slice(HD * (h % 2), HD * (h % 2) + HD)
                    pe.matmul(psum[:, m % 4, 0:(i + 1) * P], qi[rows, h // 2, i * P:(i + 1) * P],
                              ki[rows, 0:(i + 1) * P], start=True, stop=True).then_inc(done, 1)

        @block.scalar
        def _(act):
            for n, i in enumerate(tiles):
                for h in range(IDX_HEADS):
                    m = n * IDX_HEADS + h
                    act.wait_ge(done, m + 1)
                    if m >= 4:
                        act.wait_ge(summed, m - 3)
                    act.activation(relu[:, m % 4, 0:(i + 1) * P], psum[:, m % 4, 0:(i + 1) * P], ACT.Relu,
                                   scale=HD ** -0.5).then_inc(act_done, 1)

        @block.vector
        def _(dve):
            c = Count(dve, v)
            c.add(dve.memset(ones[:], 1.0))
            c.add(dve.memset(penalty[:, 0], 0.0))
            c.link(dve.tensor_scalar(weight[:], w_idx[:], IDX_HEADS ** -0.5, None, ALU.mult))
            for n, i in enumerate(tiles):
                keys = (i + 1) * P
                sc = score[:, 0:keys]
                for h in range(IDX_HEADS):
                    m = n * IDX_HEADS + h
                    dve.wait_ge(act_done, m + 1)
                    if h:
                        dve.wait_ge(summed, m)
                    base = sc if h else causal[:, (TT - 1 - i) * P:]
                    dve.scalar_tensor_tensor(sc, relu[:, m % 4, 0:keys], weight[:, i, h:h + 1], base,
                                             ALU.mult, ALU.add).then_inc(summed, 1)
                dve.wait_ge(summed, (n + 1) * IDX_HEADS)
                src = sc
                for r in range(rounds_of_8):
                    c.link(dve.max(top[:], src))
                    if r < rounds_of_8 - 1:
                        dst = left[:, r % 2, 0:keys]
                        c.link(dve.match_replace(dst, top[:], src, -3.0e38))
                        src = dst
                least = top[:, 7:8]
                c.link(dve.tensor_scalar(above[:, 0:keys], sc, least, 0.0, ALU.is_gt, ALU.add,
                                         accum_out=count_above[:]))
                c.link(dve.tensor_scalar(equal[:, 0:keys], sc, least, None, ALU.is_equal))
                c.link(dve.tensor_tensor_scan(place[:, 0:keys], ones[:, 0:keys], equal[:, 0:keys],
                                              count_above[:], ALU.mult, ALU.add))
                c.link(dve.scalar_tensor_tensor(equal[:, 0:keys], place[:, 0:keys], float(TOPK), equal[:, 0:keys],
                                                ALU.is_le, ALU.mult))
                c.link(dve.tensor_tensor(above[:, 0:keys], above[:, 0:keys], equal[:, 0:keys], ALU.add))
                c.link(dve.tensor_scalar(penalty[:, i, 0:keys], above[:, 0:keys], -MASKED, MASKED, ALU.mult, ALU.add))


def selected_attention(nc, old, qc, kc, vc, penalty, tables_dram, out):
    with ExitStack() as ctx:
        qs = ctx.enter_context(nc.sbuf_tensor("sel_qs", [P, T], F32))
        tables = ctx.enter_context(nc.sbuf_tensor("sel_tables", [P, 2, T], F32))

        def staging(pool, p, sem):
            if pool is None:
                return 1
            pool.tensor_tensor(qs[:], tile_of(qc, p), attention.scale, ALU.mult).then_inc(sem, 1)

        units, where = [], []
        for a in range(2):
            h = slice(a * HD, (a + 1) * HD)
            for i in reversed(range(TT)):
                units.append([Piece(qs[h, i * P:(i + 1) * P], kc[h], lambda j, p: vc[:, j], 0, (i + 1) * P,
                                    tables[:, a, (TT - 1 - i) * P:], plus=penalty[:, i, 0:(i + 1) * P], table_no=a)])
                where.append((a, i))

        def finish(dve, p, u, o, w, count, sem):
            a, i = where[u]
            dve.tensor_scalar(out[:, i, bass.ds(p * P + a * HD, HD)], o, w, None, ALU.mult).then_inc(sem, 1)
        finish.steps = 0
        attention(nc, old, "sel", 2, units, HD,
                  [(tables[:, a], lambda p, a=a: table_tile(tables_dram, p * 2 + TAB_C + a), 4 * a + 3)
                   for a in range(2)], staging, finish)


def gated_branches(nc, old, h, o, kts, w_in, branches, y):
    views = [view(w) for w in branches]
    first = [sum(kts[:b]) for b in range(3)]
    with Stage(nc, "branches", old) as s:
        st = Stream(s, RAW * KD, KD,
                    lambda j, r: w_in[:, :, GATES + j * D:][:, :, bass.ds((r * RAW) * (P // RAW), P)] if j < 3 else
                    [(slice(first[b], first[b] + kts[b]), views[b][:, :, bass.ds(r * P, P)]) for b in range(3)],
                    lambda j, k: tile(h if j < 3 else o, k),
                    outputs=lambda j: [(j, 0, KD)] if j < 3 else
                    [(3 + b, first[b], first[b] + kts[b]) for b in range(3)], banks=6)
        gate = s.sb("gate", [P, 3, T])
        part = s.sb("part", [P, 3, T])
        total = s.sb("total", [P, 2, T])
        added, total_hi, total_lo = s.sem("added"), s.sem("total_hi"), s.sem("total_lo")
        gates_read, products_read = s.sem("gates_read"), s.sem("products_read")
        block = s.block()

        @block.sync
        def _(sp):
            st.load(sp)

        @block.tensor
        def _(pe):
            def banks_free(j, r):
                if j == 0:
                    pe.wait_ge(gates_read, r * 3 + 3)
                if j == 3:
                    pe.wait_ge(products_read, r * 3 + 3)
            st.multiply(pe, banks_free)

        @block.scalar
        def _(act):
            act.sem_inc(gates_read, 3)

            def take(u, j, r):
                if j < 3:
                    st.wait_products(act, u)
                    if j == 0:
                        act.wait_ge(products_read, r * 3 + 3)
                    act.activation(gate[:, j], st.psum[:, j], ACT.Sigmoid).then_inc(gates_read, 1)
                else:
                    act.wait_ge(added, r * 2 + 2)
                    act.activation(tile_of(y[0], r), total[:, 1], ACT.Copy).then_inc(total_hi, 1)
            rounds_ahead(act, st.units, lambda u, j, r: st.round_hi(act, u, j, r), take)

        @block.vector
        def _(dve):
            dve.sem_inc(st.split, RAW)
            dve.sem_inc(products_read, 3)

            def combine(u, j, r):
                if j == 3:
                    st.wait_products(dve, u)
                    dve.wait_ge(gates_read, r * 3 + 6)
                    for b in range(3):
                        dve.tensor_tensor(part[:, b], gate[:, b], st.psum[:, 3 + b], ALU.mult)\
                           .then_inc(products_read, 1)
                    dve.wait_ge(products_read, r * 3 + 5)
                    dve.tensor_tensor(total[:, 0], part[:, 0], part[:, 1], ALU.add).then_inc(added, 1)
                    dve.wait_ge(products_read, r * 3 + 6)
                    dve.wait_ge(added, r * 2 + 1)
                    dve.wait_ge(total_lo, r + 1)
                    dve.tensor_tensor(total[:, 1], total[:, 0], part[:, 2], ALU.add).then_inc(added, 1)
            rounds_ahead(dve, st.units, lambda u, j, r: st.split_lo(dve, u, j, r), combine)

        @block.gpsimd
        def _(pool):
            pool.sem_inc(total_lo, 1)

            def lower(t, j, r):
                pool.wait_ge(total_hi, t + 1)
                pool.tensor_tensor(tile_of(y[1], t), total[:, 1], tile_of(y[0], t).bitcast(F32), ALU.subtract)\
                    .then_inc(total_lo, 1)
            rounds(pool, KD, 1, lower)


def half_feed_forward(nc, old, name, A, x_t, norm, half):
    with Pair(nc, name + "_hidden", KF) as hidden:
        with Pair(nc, name + "_h", KD) as h:
            normalise(nc, old, name + "_n", lambda k: x_t[:, k], lambda k: norm[:, k:k + 1], pair=h)
            glu_hidden(nc, old, name + "_up", h, A[name + "_w_gate_2"][0], A[name + "_w_up_2"][0], hidden)
        project_and_sum(nc, old, name + "_down", A[name + "_w_down_2"][0], lambda k: tile(hidden, k), x_t, half,
                        chunks=2)


def project_and_sum(nc, old, name, w, rhs, x_t, factor, chunks=1):
    def add(dve, t, psum):
        x = tile_of(x_t, t)
        return dve.scalar_tensor_tensor(x, psum, factor, x, ALU.mult, ALU.add)
    column_products(nc, old, name, lambda t, c: chunk_view(w, t, c, chunks), KD, rhs, add, chunks, by_vector=True)


def second_block(nc, old, A, x_t, cols, square, scratch, lam_in):
    half_feed_forward(nc, old, "ffn1", A, x_t, cols["ffn1_norm_2"], 0.5)

    def mix_norm(name, h):
        normalise(nc, old, name, lambda k: x_t[:, k], lambda k: cols["mix_norm_2"][:, k:k + 1], pair=h)
    w_in = view(A["w_in_2"][0])
    gain = cols["qk_gain"]
    with ExitStack() as top:
        def sb(name, shape):
            return top.enter_context(nc.sbuf_tensor("two_" + name, shape, F32))
        kts = [2, 4, 2]
        o = sb("o", [P, sum(kts), T])
        o_a, o_b, o_c = o[:, 0:2], o[:, 2:6], o[:, 6:8]
        with ExitStack() as mix:
            def mb(name, shape):
                return mix.enter_context(nc.sbuf_tensor("mix2_" + name, shape, F32))
            qa = mb("qa", [P, 12, T])
            va = mb("va", [P, TT, A_HEADS * HD])
            qb = mb("qb", [P, 8, T])
            vb = mb("vb", [P, TT, B_HEADS * P])
            qc, kc = mb("qc", [P, 3, T]), None
            kc = qc[:, 2]
            vc = mb("vc", [P, TT, HD])
            qi = mb("qi", [P, 5, T])
            ki = qi[:, 4]
            w_idx = mb("w_idx", [P, TT, IDX_HEADS])

            def copy_to(dst):
                return lambda act, t, psum: act.activation(tile_of(dst, t), psum, ACT.Copy)

            def cols_job(start, n, dst):
                return ([(slice(0, n * P), w_in[:, :, start:start + n * P])], n * P,
                        [("columns", c * P, dst(c), ACT.Copy) for c in range(n)])

            def tok_job(start, w, dst):
                return ([(slice(0, w), w_in[:, :, start:start + w])], w,
                        [("tokens", w, [dst(i) for i in range(TT)], ACT.Copy)])

            def twice_job(start, dst):
                return ([(slice(a * HD, (a + 1) * HD), w_in[:, :, start:start + HD]) for a in range(2)], P,
                        [("columns", 0, dst, ACT.Copy)])
            jobs = [tok_job(VA + c * 256, 256, lambda i, c=c: va[:, i, c * 256:(c + 1) * 256]) for c in range(3)]
            jobs += [tok_job(VB + c * 256, 256, lambda i, c=c: vb[:, i, c * 256:(c + 1) * 256]) for c in range(2)]
            jobs += [cols_job(QC, 2, lambda c: qc[:, c]), twice_job(KC, kc), tok_job(VC, HD, lambda i: vc[:, i]),
                     cols_job(QI, 2, lambda c: qi[:, c]), cols_job(QI + 2 * P, 2, lambda c: qi[:, 2 + c]),
                     twice_job(KI, ki), tok_job(WI, IDX_HEADS, lambda i: w_idx[:, i])]
            with Pair(nc, "h3", KD) as h:
                mix_norm("mix_norm", h)
                column_products(nc, old, "in_2a", lambda t, c: w_in[:, :, bass.ds(t * P + QA, P)], 12,
                                lambda k: tile(h, k), copy_to(qa))
                column_products(nc, old, "in_2b", lambda t, c: w_in[:, :, bass.ds(t * P + QB, P)], 8,
                                lambda k: tile(h, k), copy_to(qb))
                mixed_products(nc, old, "in_2c", h, jobs, 2 * P)
            tiles = [(qa[:, t], 0 if t < 6 else 1) for t in range(12)] + [(qb[:, t], 2 if t < 4 else 3) for t in range(8)]
            tiles += [(qc[:, t], 4 if t < 2 else 5) for t in range(3)]
            head_norms(nc, old, [t for t, _ in tiles], lambda n: gain[:, tiles[n][1]:tiles[n][1] + 1], square)

            def turn(name, tok, dst):
                to_channels(nc, old, name, square[:, IDENT],
                            [(tok[:, :, c * P:(c + 1) * P], dst[:, c]) for c in range(tok.shape[2] // P)])
            with nc.sbuf_tensor("dil_tok", [P, TT, 2 * P], F32) as tok:
                dilated_attention(nc, old, qa, va, scratch, tok)
                turn("dil_turn", tok, o_a)
            with nc.sbuf_tensor("diff_tok", [P, TT, 4 * P], F32) as tok, nc.sbuf_tensor("minus_lam", [P, 1], F32) as lam:
                diff_factor(nc, old, lam_in, lam)
                diff_attention(nc, old, qb, vb, lam[:], scratch, tok)
                diff_norm(nc, old, tok)
                to_channels(nc, old, "diff_turn", square[:, IDENT],
                            [(tok[:, :, c * P:(c + 1) * P], o_b[:, c]) for c in range(4)], scale=cols["diff_norm"][:, 0:1])
            with nc.sbuf_tensor("sel_tok", [P, TT, 2 * P], F32) as tok, \
                    nc.sbuf_tensor("penalty", [P, TT, T], F32) as penalty:
                with nc.sbuf_tensor("causal", [P, T], F32) as causal:
                    with Stage(nc, "load_causal", old) as s:
                        sem = s.sem("loaded")
                        block = s.block()
                        @block.sync
                        def _(sp):
                            sp.dma_start(causal[:], table_tile(scratch, TAB_FOX)).then_inc(sem, 16)
                            sp.wait_ge(sem, 16)
                    select_keys(nc, old, qi, ki, w_idx, causal, penalty)
                selected_attention(nc, old, qc, kc, vc, penalty, scratch, tok)
                turn("sel_turn", tok, o_c)
        with Pair(nc, "two_y", KD) as y:
            with Pair(nc, "h4", KD) as h, Pair(nc, "two_o", KD) as o_pair:
                mix_norm("mix_norm_again", h)
                split_tiles(nc, old, "split2", [o[:, k] for k in range(KD)], o_pair)
                gated_branches(nc, old, h, o_pair, kts, w_in, [A[f"w_branch_{b}_2"][0] for b in "abc"], y)
            project_and_sum(nc, old, "out2", A["w_out_2"][0], lambda k: tile(y, k), x_t, 1.0)
    half_feed_forward(nc, old, "ffn2", A, x_t, cols["ffn2_norm_2"], 0.5)



def build(nc, A, C, out):
    scratch = nc.dram_tensor("distance_rows", (N_TABLES, TABLE_LEN), F32, kind="Internal").ap()
    tables = nc.dram_tensor("distance_tables", (N_TABLES, P, T), F32, kind="Internal").ap()
    old = []
    with ExitStack() as top:
        def sb(name, shape):
            return top.enter_context(nc.sbuf_tensor(name, shape, F32))

        x_t = sb("x_t", [P, KD, T])
        square = sb("square", [P, LEVELS + 7, P])
        mod = sb("mod", [P, 6 * KD])
        gains = sb("gains", [P, 4 * KD])
        heads = sb("heads", [P, H_FOX // 2])
        b_f = sb("b_f", [H_FOX, 1])
        bias = sb("bias", [33, N_TABLES])
        lam_in = sb("lam_in", [P, 4 * HD])
        columns = sb("columns", [P, 5, P])
        att_scale = sb("att_scale", [P, 1])
        attention.ident = square[:, IDENT]
        attention.scale = att_scale[:].to_broadcast([P, T])

        rows, used, col = [], [0] * 5, {}

        def put(name, pack, n, src):
            rows.append((pack, used[pack], n, slice(0, P), src))
            col[name] = columns[:, pack, used[pack]:used[pack] + n]
            used[pack] += n

        def put_both(name, pack, n, src):
            for a in range(2):
                rows.append((pack, used[pack], n, slice(a * HD, (a + 1) * HD), src))
            col[name] = columns[:, pack, used[pack]:used[pack] + n]
            used[pack] += n

        def line(w):
            return w.rearrange("a (n p) -> (a n) p", p=P)
        put("norm_g", 0, 4 * KD, A["norm_g"][0].rearrange("a (n p) -> (a n) p", p=P))
        put("c", 0, KD, line(A["c"]))
        put("ada_b", 0, 6 * KD, line(A["ada_b"]))
        for n in ("ffn1_norm_2", "mix_norm_2", "ffn2_norm_2"):
            put(n, 0, KD, line(A[n]))
        cw = A["ffn_conv_w"][0].rearrange("a (n p) -> (a n) p", p=P)
        put("conv01", 1, 4 * KF, cw[0:4 * KF, :])
        put("conv2", 2, 2 * KF, cw[4 * KF:6 * KF, :])
        put("conv_b", 2, 2 * KF, line(A["ffn_conv_b"]))
        put("mu", 3, RW_TILES, line(A["rwkv_mu"]))
        for n in ("w0", "a0", "k_k", "k_a", "ln_w", "ln_b"):
            put(n, 3, 2, line(A["rwkv_" + n]))
        put("r_k", 3, 2, A["rwkv_r_k"][0].rearrange("(n a) d -> n (a d)", a=2))
        put("diff_norm", 3, 1, A["diff_out_norm_2"])
        put_both("qk_gain", 3, 6, A["qk_gain_2"][0].rearrange("a b d -> (a b) d"))
        put_both("pe_k", 4, L_CMP, A["nsa_pe_k"][0])
        put_both("pe_v", 4, L_CMP, A["nsa_pe_v"][0])
        extra = [
            (b_f[:], A["fox_b_f"].rearrange("a h -> h a")),
            (bias[0:32, 0:H_NSA], A["rel_bias"]),
            (bias[0:32, H_NSA:N_TABLES - 1], A["rel_bias_2"]),
            (lam_in[:], A["diff_lambda_2"].rearrange("a b d -> a (b d)")[0].partition_broadcast(P)),
            (heads[:], C["heads"]),
        ]
        with Stage(nc, "zero_bias", old) as s:
            block = s.block()
            @block.vector
            def _(dve):
                dve.memset(bias[0:32, N_TABLES - 1:N_TABLES], 0.0)
                dve.memset(bias[32:33], MASKED)
                dve.memset(att_scale[:], ATT_SCALE)
        load_parameters(nc, old, rows, used, columns, square, C["square"], A["x"][0], x_t, extra)
        distance_tables(nc, old, C["onehot"], bias, scratch, tables)
        cols = dict(col)
        cols["pe"] = columns[:, 4, 0:2 * L_CMP].rearrange("p (a l) -> p a l", a=2)

        def conv(t, w, tap_no):
            pack, start = {0: (1, 0), 1: (1, 2 * KF), 2: (2, 0), 3: (2, 2 * KF)}[tap_no]
            return columns[:, pack, bass.ds(t + (start + w * KF), 1)]
        cols["conv"] = conv
        modulation(nc, old, col["c"], view(A["ada_w"][0]), col["ada_b"], mod)
        block_one_gains(nc, old, mod, col["norm_g"], gains)
        first_block(nc, old, A, x_t, gains, mod, cols, square, tables, heads, b_f[:])
        second_block(nc, old, A, x_t, cols, square, tables, lam_in)

        with Stage(nc, "store", old) as s:
            tok = s.sb("tok", [P, TT, D])
            psum = s.ps("psum", 4)
            done, kept, stored = s.sem("done"), s.sem("kept"), s.sem("stored")
            block = s.block()

            @block.tensor
            def _(pe):
                for n in range(2 * TT):
                    i, half = divmod(n, 2)
                    if n >= 4:
                        pe.wait_ge(kept, n - 3)
                    for k in range(4):
                        mm = pe.transpose(psum[:, n % 4, k * P:(k + 1) * P],
                                          x_t[:, half * 4 + k, i * P:(i + 1) * P], square[:, IDENT])
                    mm.then_inc(done, 1)

            @block.vector
            def _(dve):
                for n in range(2 * TT):
                    i, half = divmod(n, 2)
                    dve.wait_ge(done, n + 1)
                    dve.tensor_copy(tok[:, i, half * T:(half + 1) * T], psum[:, n % 4]).then_inc(kept, 1)

            @block.sync
            def _(sp):
                for i in range(TT):
                    sp.wait_ge(kept, 2 * i + 2)
                    sp.dma_start(out[0, i * P:(i + 1) * P, :], tok[:, i]).then_inc(stored, 16)
                sp.wait_ge(stored, 16 * TT)


def kernel(**inputs):
    import concourse.bacc as _bacc
    from concourse.bass_utils import run_bass_kernel_spmd as _run

    nc = _bacc.Bacc("TRN2", target_bir_lowering=False, num_devices=1)
    arrays, A, C = {}, {}, {}
    constants = {"square": square_constants(), "onehot": distance_buckets(), "heads": head_rows()}
    for group, into in ((inputs, A), (constants, C)):
        for name, value in group.items():
            a = np.ascontiguousarray(value)
            arrays[f"in_{name}_dram"] = a
            into[name] = nc.dram_tensor(f"in_{name}_dram", a.shape, F32, kind="ExternalInput").ap()
    out = nc.dram_tensor("out_0_dram", (1, T, D), F32, kind="ExternalOutput").ap()
    build(nc, A, C, out)
    r = _run(nc, [arrays], core_ids=[0])
    return r.results[0]["out_0_dram"]
```

```python
import math
from contextlib import ExitStack

import numpy as np

import concourse.bass as bass
from concourse import mybir

F32 = mybir.dt.float32
F32R = mybir.dt.float32r
ACT = mybir.ActivationFunctionType
ALU = mybir.AluOpType
AX = mybir.AxisListType

P = 128
T = 512
TT = T // P
D = 1024
KD = D // P
HD = 64
DFF = 2816
KF = DFF // P
ATT_SCALE = HD ** -0.5
EPS = 1e-6
MASKED = -1e30
LOWEST = -1e20

C_RWKV, R_LOW = 256, 128
N_RWKV = 3 * C_RWKV + R_LOW
RW_TILES = N_RWKV // P
C_FOX, H_FOX = 384, 6
FOX_Q = N_RWKV
FOX_V = FOX_Q + 2 * C_FOX
FOX_F = FOX_V + C_FOX
C_NSA, H_NSA, C_KV = 384, 6, 128
NSA_Q = FOX_F + H_FOX
NSA_KC = NSA_Q + C_NSA
NSA_VS = NSA_KC + 3 * C_KV
NSA_KW = NSA_VS + C_KV
NSA_VW = NSA_KW + C_KV
NSA_GATE = NSA_VW + C_KV
L_CMP, D_CMP, CMP_HID = 32, 16, 128
N_CMP = T // D_CMP - L_CMP // D_CMP + 1
GN_EPS = 64e-5

A_HEADS, B_HEADS, C_HEADS, IDX_HEADS = 12, 4, 4, 8
A_SLOTS, A_GROUPS = 4, 3
QA, VA = 0, 2 * A_HEADS * HD
QB = VA + A_HEADS * HD
VB = QB + 4 * B_HEADS * HD
QC = VB + B_HEADS * 2 * HD
KC, VC = QC + C_HEADS * HD, QC + (C_HEADS + 1) * HD
QI = QC + (C_HEADS + 2) * HD
KI = QI + IDX_HEADS * HD
WI = KI + HD
GATES = WI + IDX_HEADS
TOPK = 128
LAM_INIT = 0.8 - 0.6 * math.exp(-0.3 * 0)

TABLE_LEN = 640
N_TABLES = H_NSA + A_HEADS + B_HEADS + C_HEADS + 1
TAB_NSA, TAB_A, TAB_B, TAB_C, TAB_FOX = 0, 6, 18, 22, 26
TABLE_STORES = 3



def square_constants():
    s, t = np.arange(P)[:, None], np.arange(P)[None, :]
    mats = [s == t, s // HD == t // HD, s < t, s <= t]
    for level in range(7):
        size = 2 << level
        mats.append((s // size == t // size) & (s % size < size // 2) & (t % size >= size // 2))
    return np.stack(mats, 1).astype(np.float32)


IDENT, HEADS, STRICT, INCL, LEVELS = 0, 1, 2, 3, 4


def distance_buckets():
    dist = T - 1 - np.arange(TABLE_LEN)

    def bucket(max_distance):
        n = np.maximum(dist, 0)
        large = 16 + (np.log(np.maximum(n, 1) / 16) / math.log(max_distance / 16) * 16 + 1e-9).astype(np.int64)
        return np.where(n < 16, n, np.minimum(large, 31))

    near, far = bucket(128), bucket(2048)
    kinds = [(near, dist >= 0), (far, (dist >= 0) & (dist <= 128)), (far, (dist >= 0) & (dist % 4 == 0)),
             (far, (dist >= 0) & (dist % 16 == 0)), (far, dist >= 0)]
    out = np.zeros((33, len(kinds), TABLE_LEN), np.float32)
    for n, (b, ok) in enumerate(kinds):
        out[np.where(ok, b, 32), n, np.arange(TABLE_LEN)] = 1.0
    return out


def head_rows():
    out = np.zeros((P, H_FOX // 2), np.float32)
    for p in range(H_FOX // 2):
        for a in range(2):
            out[[a * HD + 2 * p + a, a * HD + 32 + 2 * p + a], p] = 1.0
    return out


class Stage:

    def __init__(self, nc, name, old):
        self.nc, self.name, self.old = nc, name, old
        self.own = []

    def __enter__(self):
        self.ctx = ExitStack()
        return self

    def __exit__(self, *exc):
        self.ctx.close()
        self.old[:] = self.own

    def sb(self, name, shape, dt=F32):
        return self.ctx.enter_context(self.nc.sbuf_tensor(f"{self.name}_{name}", shape, dt))

    def ps(self, name, banks):
        return self.ctx.enter_context(self.nc.psum_tensor(f"{self.name}_{name}", [P, banks, T], F32))

    def sem(self, name):
        s = self.ctx.enter_context(self.nc.semaphore(f"{self.name}_{name}"))
        self.own.append(s)
        return s

    def block(self):
        block = self.ctx.enter_context(self.nc.Block())
        if self.old:
            @block.gpsimd
            def _(pool):
                for s in self.old:
                    pool.sem_clear(s)
        return block


class Count:

    def __init__(self, eng, sem):
        self.eng, self.sem, self.base, self.n = eng, sem, 0, 0

    def add(self, instruction):
        instruction.then_inc(self.sem, 1)
        self.n += 1

    def settle(self):
        self.eng.wait_ge(self.sem, self.base + self.n)

    def link(self, instruction):
        self.add(instruction)
        self.settle()

    def enter(self, base):
        self.base, self.n = base, 0


WARM, KEEP_WARM = 2, 5 * HD


def warm_up(pe, bank, square, n=WARM):
    for _ in range(n):
        pe.matmul(bank, square[:, 0], flat(square[:, 0:TT])[:, 0:bank.shape[1]], start=True, stop=True)


def flat(ap):
    return ap.rearrange("p a b -> p (a b)")


def tile_of(tensor, t):
    return flat(tensor[:, bass.ds(t, 1), :]) if not isinstance(t, int) else tensor[:, t, :]


def rounds(eng, tiles, unroll, body):
    whole = tiles // unroll
    if whole > 1:
        with eng.Fori(0, whole) as g:
            for j in range(unroll):
                body(g * unroll + j, j, g)
    else:
        whole = 0
    for t in range(whole * unroll, tiles):
        body(t, t % unroll, t // unroll)



RAW, PAIRS, LEAD = 4, 2, 2


def three_products(pe, out, weights, rhs, start, stop):
    (w_hi, w_lo), (r_hi, r_lo) = weights, rhs
    pe.matmul(out, w_hi, r_hi, start=start, stop=False)
    pe.matmul(out, w_hi, r_lo, start=False, stop=False)
    return pe.matmul(out, w_lo, r_hi, start=False, stop=stop)


def rounds_ahead(eng, units, start, finish):
    for u in range(LEAD):
        start(u, u, 0)

    def body(u, j, r):
        start(u + LEAD, (j + LEAD) % RAW, r + (j + LEAD) // RAW)
        finish(u, j, r)
    rounds(eng, units - LEAD, RAW, body)
    for u in range(units - LEAD, units):
        finish(u, u % RAW, u // RAW)


class Stream:

    def __init__(self, s, units, kt, source, rhs, per=1, outputs=None, banks=None, before=None):
        self.units, self.kt, self.source, self.rhs, self.per = units, kt, source, rhs, per
        self.banks, self.outputs = banks or RAW // per, outputs
        self.raw = s.sb("raw", [P, RAW, kt, P])
        self.loaded = [s.sem(f"loaded{j}") for j in range(RAW)]
        self.ahead = before is not None
        if before is not None:
            before(self.load_first)
        self.hi = s.sb("w_hi", [P, PAIRS, kt, P], F32R)
        self.lo = s.sb("w_lo", [P, PAIRS, kt, P], F32R)
        self.psum = s.ps("psum", self.banks)
        self.rounded, self.split, self.done, self.free = (s.sem(n) for n in ("rounded", "split", "done", "free"))

    def bank(self, j):
        return self.psum[:, j // self.per]

    def tile(self, j, r):
        return r * self.banks + j // self.per

    def sources(self, j, r):
        src = self.source(j, r)
        return src if isinstance(src, list) else [(slice(0, self.kt), src)]

    def load_unit(self, sp, j, r):
        for tiles, src in self.sources(j, r):
            sp.dma_start(self.raw[:, j, tiles], src).then_inc(self.loaded[j], 16)

    def load_first(self, sp):
        for j in range(RAW):
            self.load_unit(sp, j, 0)

    def load(self, sp):
        if not self.ahead:
            self.load_first(sp)

        def body(u, j, r):
            sp.wait_ge(self.split, u + 1)
            self.load_unit(sp, j, r + 1)
        rounds(sp, self.units - RAW, RAW, body)

    def round_hi(self, act, u, j, r):
        n = 16 * len(self.sources(j, r))
        act.wait_ge(self.loaded[j], r * n + n)
        act.wait_ge(self.done, u + 1)
        act.activation(self.hi[:, j % PAIRS], self.raw[:, j], ACT.Copy).then_inc(self.rounded, 1)

    def split_lo(self, dve, u, j, r):
        dve.wait_ge(self.rounded, u + 1)
        dve.tensor_tensor(self.lo[:, j % PAIRS], self.raw[:, j], self.hi[:, j % PAIRS].bitcast(F32), ALU.subtract)\
           .then_inc(self.split, 1)

    def multiply(self, pe, banks_free=None):
        pe.sem_inc(self.done, PAIRS)

        def body(u, j, r):
            pe.wait_ge(self.split, u + 1)
            opens, closes = j % self.per == 0, j % self.per == self.per - 1
            if banks_free is not None:
                banks_free(j, r)
            elif opens:
                pe.wait_ge(self.free, self.tile(j, r) + 1)
            for bank, first, end in self.outputs(j) if self.outputs else [(j // self.per, 0, self.kt)]:
                for k in range(first, end):
                    mm = three_products(pe, self.psum[:, bank], (self.hi[:, j % PAIRS, k], self.lo[:, j % PAIRS, k]),
                                        self.rhs(j, k), opens and k == first, closes and k == end - 1)
            mm.then_inc(self.done, 1)
        rounds(pe, self.units, RAW, body)

    def wait_products(self, eng, u):
        eng.wait_ge(self.done, u + (PAIRS + 1))


def nothing(u, j, r):
    pass


def column_products(nc, old, name, weights, tiles, rhs, store, chunks=1, by_vector=False, before=None,
                    load_next=None):
    kt = weights(0, 0).shape[1]
    with Stage(nc, name, old) as s:
        st = Stream(s, tiles * chunks, kt, lambda j, r: weights(r * (RAW // chunks) + j // chunks, j % chunks),
                    lambda j, k: rhs((j % chunks) * kt + k), per=chunks, before=before)
        block = s.block()

        def take(eng):
            def body(u, j, r):
                if j % chunks == chunks - 1:
                    st.wait_products(eng, u)
                    store(eng, st.tile(j, r), st.bank(j)).then_inc(st.free, 1)
            return body

        @block.sync
        def _(sp):
            st.load(sp)
            if load_next is not None:
                load_next(sp)

        @block.tensor
        def _(pe):
            st.multiply(pe)

        @block.scalar
        def _(act):
            rounds_ahead(act, st.units, lambda u, j, r: st.round_hi(act, u, j, r),
                         nothing if by_vector else take(act))

        @block.vector
        def _(dve):
            dve.sem_inc(st.free, st.banks)
            rounds_ahead(dve, st.units, lambda u, j, r: st.split_lo(dve, u, j, r),
                         take(dve) if by_vector else nothing)


def mixed_products(nc, old, name, h, jobs, width, before=None):
    with Stage(nc, name, old) as s:
        raw = s.sb("raw", [P, 2, KD, width])
        loaded = [s.sem(f"loaded{j}") for j in range(2)]

        def load_job(sp, n):
            for cols, src in jobs[n][0]:
                sp.dma_start(raw[:, n % 2, :, cols], src).then_inc(loaded[n % 2], 16)

        def load_first(sp):
            load_job(sp, 0)
            load_job(sp, 1)
        if before is not None:
            before(load_first)
        hi = s.sb("w_hi", [P, 2, KD, width], F32R)
        lo = s.sb("w_lo", [P, 2, KD, width], F32R)
        psum = s.ps("psum", 4)
        rounded, split, done, stored = s.sem("rounded"), s.sem("split"), s.sem("done"), s.sem("stored")
        outs = []
        for n, (_, w, outputs) in enumerate(jobs):
            for o in outputs:
                if o[0] == "columns":
                    outs.append((n, o[1], None, [(0, T, o[2], o[3])]))
                else:
                    outs += [(n, 0, i, [(a, b, dst[i], func) for a, b, dst, func in o[1]]) for i in range(TT)]
        last = [max(i for i, o in enumerate(outs) if o[0] == n) for n in range(len(jobs))]
        landed = [16 * sum(len(jobs[m][0]) for m in range(n % 2, n + 1, 2)) for n in range(len(jobs))]
        kept = [sum(len(o[3]) for o in outs[:i + 1]) for i in range(len(outs))]
        block = s.block()

        @block.sync
        def _(sp):
            if before is None:
                load_first(sp)
            for n in range(2, len(jobs)):
                sp.wait_ge(split, n - 1)
                load_job(sp, n)

        @block.vector
        def _(dve):
            for n, (_, w, _) in enumerate(jobs):
                dve.wait_ge(rounded, n + 1)
                dve.tensor_tensor(lo[:, n % 2, :, 0:w], raw[:, n % 2, :, 0:w], hi[:, n % 2, :, 0:w].bitcast(F32),
                                  ALU.subtract).then_inc(split, 1)

        @block.tensor
        def _(pe):
            for i, (n, c, tokens, _) in enumerate(outs):
                pe.wait_ge(split, n + 1)
                if i >= 4:
                    pe.wait_ge(stored, kept[i - 4])
                w = T if tokens is None else jobs[n][1]
                for k in range(KD):
                    if tokens is None:
                        left = [x[:, n % 2, k, c:c + P] for x in (hi, lo)]
                        right = [x[:, k, :] for x in h]
                    else:
                        left = [x[:, k, tokens * P:(tokens + 1) * P] for x in h]
                        right = [x[:, n % 2, k, 0:w] for x in (hi, lo)]
                    mm = three_products(pe, psum[:, i % 4, 0:w], left, right, k == 0, k == KD - 1)
                mm.then_inc(done, 1)

        @block.scalar
        def _(act):
            def round_job(n):
                act.wait_ge(loaded[n % 2], landed[n])
                if n >= 2:
                    act.wait_ge(done, last[n - 2] + 1)
                w = jobs[n][1]
                act.activation(hi[:, n % 2, :, 0:w], raw[:, n % 2, :, 0:w], ACT.Copy).then_inc(rounded, 1)
            round_job(0)
            round_job(1)
            for i, (n, _, _, parts) in enumerate(outs):
                act.wait_ge(done, i + 1)
                if i == last[n] and n + 2 < len(jobs):
                    round_job(n + 2)
                for a, b, dst, func in parts:
                    func, scale = func if isinstance(func, tuple) else (func, 1.0)
                    act.activation(dst, psum[0:dst.shape[0], i % 4, a:b], func, scale=scale).then_inc(stored, 1)


def split_tiles(nc, old, name, src, pair, load_next):
    with Stage(nc, name, old) as s:
        block = s.block()

        @block.sync
        def _(sp):
            load_next(sp)
        split_beside(s, block, src, pair)


def split_beside(s, block, src, pair):
    rounded = s.sem("tiles_rounded")

    @block.scalar
    def _(act):
        for k in range(len(src)):
            act.activation(pair[0][:, k], src[k], ACT.Copy).then_inc(rounded, 1)

    @block.vector
    def _(dve):
        for k in range(0, len(src), 2):
            dve.wait_ge(rounded, k + 1)
            dve.tensor_tensor(pair[1][:, k], src[k], pair[0][:, k].bitcast(F32), ALU.subtract)

    @block.gpsimd
    def _(pool):
        for k in range(1, len(src), 2):
            pool.wait_ge(rounded, k + 1)
            pool.tensor_tensor(pair[1][:, k], src[k], pair[0][:, k].bitcast(F32), ALU.subtract)



def normalise(nc, old, name, src, gain, shift=None, pair=None, add_to=None, load_next=None,
              rstd=None, rooted_before=False, beside=None):
    with Stage(nc, name, old) as s:
        squares = s.sb("squares", [P, 2, T])
        if rstd is None:
            rstd = s.sb("rstd", [P, T])
        logs = s.sb("logs", [P, T])
        scaled = s.sb("scaled", [P, 4, T])
        ones = s.sb("ones", [P, P])
        eps = s.sb("eps", [P, 1])
        psum = s.ps("psum", 1)
        const, squared, summed, rooted = s.sem("const"), s.sem("squared"), s.sem("summed"), s.sem("rooted")
        used, scaled_s, ready = s.sem("used"), s.sem("scaled"), s.sem("ready")
        rounded, even_split, odd_split = s.sem("rounded"), s.sem("even_split"), s.sem("odd_split")
        block = s.block()

        @block.sync
        def _(sp):
            if load_next is not None:
                load_next(sp)

        def roots(act):
            for k in range(0, KD, 2):
                if k >= 2:
                    act.wait_ge(used, k - 1)
                act.activation(squares[:, 0], src(k), ACT.Square).then_inc(squared, 1)
            act.wait_ge(summed, 1)
            act.wait_ge(const, 2)
            act.activation(logs[:], psum[:, 0], ACT.Ln, bias=eps[:, 0:1], scale=1.0 / D).then_inc(rooted, 1)
            act.wait_ge(rooted, 1)
            act.activation(rstd[:], logs[:], ACT.Exp, scale=-0.5).then_inc(rooted, 1)

        def odd_squares(dve):
            dve.memset(ones[:], 1.0).then_inc(const, 1)
            dve.memset(eps[:], EPS).then_inc(const, 1)
            for k in range(1, KD, 2):
                if k >= 3:
                    dve.wait_ge(used, k - 1)
                dve.tensor_tensor(squares[:, 1], src(k), src(k), ALU.mult).then_inc(const, 1)
            dve.wait_ge(rooted, 2)

        @block.scalar
        def _(act):
            if not rooted_before:
                roots(act)
            if pair is not None:
                for k in range(KD):
                    act.wait_ge(ready, k + 1)
                    act.activation(pair[0][:, k], scaled[:, k % 4], ACT.Copy).then_inc(rounded, 1)

        @block.gpsimd
        def _(pool):
            if pair is not None:
                for k in range(0, KD, 2):
                    pool.wait_ge(rounded, k + 1)
                    pool.tensor_tensor(pair[1][:, k], scaled[:, k % 4], pair[0][:, k].bitcast(F32), ALU.subtract)\
                        .then_inc(even_split, 1)

        @block.tensor
        def _(pe):
            if rooted_before:
                return
            pe.wait_ge(const, 2)
            for k in range(KD):
                pe.wait_ge(squared if k % 2 == 0 else const, k // 2 + (1 if k % 2 == 0 else 3))
                mm = pe.matmul(psum[:, 0], ones[:], squares[:, k % 2], start=k == 0, stop=k == KD - 1)
                mm.then_inc(used if k < KD - 1 else summed, 1)

        @block.vector
        def _(dve):
            if not rooted_before:
                odd_squares(dve)

            def lower_odd(k):
                dve.wait_ge(rounded, k + 1)
                dve.tensor_tensor(pair[1][:, k], scaled[:, k % 4], pair[0][:, k].bitcast(F32), ALU.subtract)\
                   .then_inc(odd_split, 1)
            for k in range(KD):
                if pair is not None and k >= 4:
                    dve.wait_ge(even_split if k % 2 == 0 else odd_split, k // 2 - 1)
                out = scaled[:, k % 4]
                plain = pair is not None and shift is None
                dve.scalar_tensor_tensor(out, src(k), gain(k), rstd[:], ALU.mult, ALU.mult)\
                   .then_inc(ready if plain else scaled_s, 1)
                if shift is not None:
                    dve.wait_ge(scaled_s, k + 1)
                    dve.tensor_scalar(out, out, shift(k), None, ALU.add).then_inc(ready, 1)
                if pair is not None and k >= 2 and k % 2 == 0:
                    lower_odd(k - 1)
                if add_to is not None and k >= 1:
                    dve.wait_ge(scaled_s, k)
                    dve.tensor_tensor(add_to(k - 1), add_to(k - 1), scaled[:, (k - 1) % 4], ALU.add)
            if pair is not None:
                lower_odd(KD - 1)
            if add_to is not None:
                dve.wait_ge(scaled_s, KD)
                dve.tensor_tensor(add_to(KD - 1), add_to(KD - 1), scaled[:, (KD - 1) % 4], ALU.add)
        if beside is not None:
            beside(s, block)



EARLY = 2 * KD
MOD_LOAD = 4

def load_parameters(nc, old, rows, packs, columns, square, cst_square, x, x_t, extra, load_next):
    with Stage(nc, "setup", old) as s:
        xin = s.sb("x", [P, TT, D])
        stage = s.sb("rows", [P, len(packs), P])
        psum = s.ps("psum", 8)
        const, params, x_in = s.sem("const"), s.sem("params"), s.sem("x_in")
        turned, stored = s.sem("turned"), s.sem("stored")
        block = s.block()

        @block.sync
        def _(sp):
            sp.dma_start(square[:], cst_square).then_inc(const, 16)
            for i in range(TT):
                sp.dma_start(xin[:, i], x[i * P:(i + 1) * P, :]).then_inc(x_in, 16)
            sp.wait_ge(params, 16 * (len(rows) + len(extra)))
            load_next(sp)

        @block.scalar
        def _(act):
            for pack, row, n, cols, src in rows:
                act.dma_start(stage[row:row + n, pack, cols], src).then_inc(params, 16)
            for dst, src in extra:
                act.dma_start(dst, src).then_inc(params, 16)
            act.wait_ge(params, 16 * (len(rows) + len(extra)))

        @block.tensor
        def _(pe):
            ident = square[:, IDENT]
            pe.wait_ge(const, 16)
            pe.wait_ge(x_in, 16 * TT)
            for k in range(KD):
                for i in range(TT):
                    mm = pe.transpose(psum[:, k % 4, i * P:(i + 1) * P], xin[:, i, k * P:(k + 1) * P], ident)
                mm.then_inc(turned, 1)
                if k >= 3 and k < KD - 1:
                    pe.wait_ge(stored, k - 2)
            pe.wait_ge(params, 16 * (len(rows) + len(extra)))
            for n, used in enumerate(packs):
                mm = pe.transpose(psum[:, 4 + n // 4, (n % 4) * P:(n % 4) * P + used], stage[0:used, n],
                                  ident[0:used, 0:used])
            mm.then_inc(turned, 1)

        @block.vector
        def _(dve):
            for k in range(KD):
                dve.wait_ge(turned, k + 1)
                dve.tensor_copy(x_t[:, k], psum[:, k % 4]).then_inc(stored, 1)
            dve.wait_ge(turned, KD + 1)
            for n, used in enumerate(packs):
                dve.tensor_copy(columns[:, n, 0:used], psum[:, 4 + n // 4, (n % 4) * P:(n % 4) * P + used])\
                   .then_inc(stored, 1)


def modulation(nc, old, c_col, silu, ada_w, ada_b_col, mod, before, beside):
    loads = EARLY // MOD_LOAD
    with Stage(nc, "mod", old) as s:
        slots = s.sb("slots", [P, loads, KD, MOD_LOAD * P])
        loaded = [s.sem(f"loaded{t}") for t in range(loads)]

        def load(sp, ts):
            for t in ts:
                sp.dma_start(slots[:, t], ada_w[:, :, t * MOD_LOAD * P:(t + 1) * MOD_LOAD * P]).then_inc(loaded[t], 16)
        before(lambda sp: load(sp, range(1)))
        total = s.sb("total", [P, loads, MOD_LOAD * P])
        ones = s.sb("ones", [P, 1])
        psum = s.ps("psum", 1)
        ready, done, added = s.sem("ready"), s.sem("done"), s.sem("added")
        block = s.block()

        @block.sync
        def _(sp):
            load(sp, range(1, loads))

        @block.scalar
        def _(act):
            act.activation(silu[:], c_col, ACT.Silu).then_inc(ready, 1)
        beside(s, block)

        @block.tensor
        def _(pe):
            for t in range(loads):
                pe.wait_ge(added, (t + 1) * KD)
                for m in range(MOD_LOAD):
                    n = t * MOD_LOAD + m
                    mm = pe.matmul(psum[:, 0, n:n + 1], total[:, t, m * P:(m + 1) * P], ones[:], start=True, stop=True)
            mm.then_inc(done, 1)

        @block.vector
        def _(dve):
            dve.memset(ones[:], 1.0).then_inc(ready, 1)
            dve.wait_ge(ready, 2)
            for t in range(loads):
                dve.wait_ge(loaded[t], 16)
                for k in range(KD):
                    if k == 0:
                        dve.tensor_scalar(total[:, t], slots[:, t, 0], silu[:, 0:1], None, ALU.mult).then_inc(added, 1)
                    else:
                        dve.wait_ge(added, t * KD + k)
                        dve.scalar_tensor_tensor(total[:, t], slots[:, t, k], silu[:, k:k + 1], total[:, t],
                                                 ALU.mult, ALU.add).then_inc(added, 1)
            dve.wait_ge(done, 1)
            dve.tensor_tensor(mod[:, 0:EARLY], psum[:, 0, 0:EARLY], ada_b_col[:, 0:EARLY], ALU.add)


class LateModulation:

    RING = 2

    def __init__(self, silu, ada_w, ada_b_col, mod):
        self.silu, self.ada_w, self.ada_b_col, self.mod = silu, ada_w, ada_b_col, mod
        self.loads = (6 * KD - EARLY) // MOD_LOAD
        self.steps = self.loads * KD

    def place(self, s):
        self.slots = s.sb("mod_slots", [P, self.RING, KD, MOD_LOAD * P])
        self.total = s.sb("mod_total", [P, self.loads, MOD_LOAD * P])
        self.ones = s.sb("mod_ones", [P, 1])
        self.loaded = [s.sem(f"mod_loaded{j}") for j in range(self.RING)]
        self.added, self.ready, self.done = s.sem("mod_added"), s.sem("mod_ready"), s.sem("mod_done")

    def add(self, dve, step):
        t, k = divmod(step, KD)
        j, total = t % self.RING, self.total[:, t]
        if k == 0:
            dve.wait_ge(self.loaded[j], 16 * (t // self.RING + 1))
            dve.tensor_scalar(total, self.slots[:, j, 0], self.silu[:, 0:1], None, ALU.mult).then_inc(self.added, 1)
        else:
            dve.wait_ge(self.added, step)
            dve.scalar_tensor_tensor(total, self.slots[:, j, k], self.silu[:, k:k + 1], total, ALU.mult, ALU.add)\
               .then_inc(self.added, 1)

    def rest(self, block, psum, psum_free, freed):
        @block.sync
        def _(sp):
            for t in range(self.loads):
                if t >= self.RING:
                    sp.wait_ge(self.added, (t - self.RING + 1) * KD)
                first = (EARLY + t * MOD_LOAD) * P
                sp.dma_start(self.slots[:, t % self.RING], self.ada_w[:, :, first:first + MOD_LOAD * P])\
                  .then_inc(self.loaded[t % self.RING], 16)

        @block.gpsimd
        def _(pool):
            pool.memset(self.ones[:], 1.0).then_inc(self.ready, 1)

        @block.tensor
        def _(pe):
            pe.wait_ge(psum_free, freed)
            pe.wait_ge(self.ready, 1)
            pe.wait_ge(self.added, self.steps)
            for n in range(self.loads * MOD_LOAD):
                t, m = divmod(n, MOD_LOAD)
                mm = pe.matmul(psum[:, n:n + 1], self.total[:, t, m * P:(m + 1) * P], self.ones[:],
                               start=True, stop=True)
            mm.then_inc(self.done, 1)

        @block.vector
        def _(dve):
            dve.wait_ge(self.done, 1)
            dve.tensor_tensor(self.mod[:, EARLY:], psum[:, 0:6 * KD - EARLY], self.ada_b_col[:, EARLY:], ALU.add)


def early_gains(nc, old, mod, norm_g, gains, qk_gain, store_scale):
    with Stage(nc, "gains", old) as s:
        done = s.sem("done")
        block = s.block()

        @block.vector
        def _(dve):
            queries = qk_gain[:, 0:6:2]
            dve.tensor_scalar(queries, queries, ATT_SCALE, None, ALU.mult)
            dve.memset(store_scale[:], 1.0).then_inc(done, 1)
            dve.wait_ge(done, 1)
            dve.memset(store_scale[:, RW_TILES:RW_TILES + 3], ATT_SCALE)
            dve.scalar_tensor_tensor(gains[:, 0:KD], mod[:, KD:2 * KD], 1.0, norm_g[:, 0:KD], ALU.add, ALU.mult)


def late_gains(nc, old, mod, norm_g, gains):
    with Stage(nc, "late_gains", old) as s:
        block = s.block()

        @block.vector
        def _(dve):
            for n, (scale, one) in ((1, (2, 0.0)), (2, (4, 1.0)), (3, (5, 0.0))):
                dve.scalar_tensor_tensor(gains[:, n * KD:(n + 1) * KD], mod[:, scale * KD:(scale + 1) * KD], one,
                                         norm_g[:, n * KD:(n + 1) * KD], ALU.add, ALU.mult)



CHUNK = P
NCH = T // CHUNK


def rwkv_inputs(nc, old, rw, cols, ups, square, r_in, a_in, k_in, b_in, v_in, gate, bonus, tot, mid):
    with Stage(nc, "rwkv_in", old) as s:
        mixed = s.sb("mixed", [P, RW_TILES, T])
        diff = s.sb("diff", [P, T])
        diff_v = s.sb("diff_v", [P, T])
        w_up = s.sb("w_up", [P, C_RWKV])
        low = s.sb("low", [P, T])
        rate = s.sb("rate", [P, 2, T])
        ld = s.sb("ld", [P, 2, T])
        run = s.sb("run", [P, 2, T])
        kk = s.sb("kk", [P, 2, T])
        work = s.sb("work", [P, 2, T])
        root = s.sb("root", [P, 2, T])
        e_pos = s.sb("e_pos", [P, 2, T])
        e_before = s.sb("e_before", [P, 2, T])
        e_neg = s.sb("e_neg", [P, 2, T])
        ones = s.sb("ones", [P, T])
        psum = s.ps("psum", 8)
        v, a, up_done, sums_done = (s.sem(n) for n in ("dve", "act", "up", "sums"))
        up_in, shifted = s.sem("up_in"), s.sem("shifted")
        block = s.block()

        @block.sync
        def _(sp):
            row = 0
            for src in ups:
                sp.dma_start(w_up[row:row + src.shape[0]], src).then_inc(up_in, 16)
                row += src.shape[0]

        @block.gpsimd
        def _(pool):
            c = Count(pool, shifted)
            for t in (4, 5):
                c.link(pool.tensor_tensor(diff_v[:], rw[:, t, 0:T], rw[:, t, 1:T + 1], ALU.subtract))
                c.link(pool.tensor_tensor(diff_v[:], diff_v[:], cols["mu"][:, t:t + 1].to_broadcast([P, T]), ALU.mult))
                c.link(pool.tensor_tensor(mixed[:, t], diff_v[:], rw[:, t, 1:T + 1], ALU.add))
            for t in range(2):
                pool.tensor_copy(v_in[:, t], mixed[:, 4 + t])
            pool.wait_ge(v, 10)
            pool.wait_ge(a, 15)
            for t in range(2):
                pool.tensor_tensor(r_in[:, t], mixed[:, t], e_pos[:, t], ALU.mult)

        @block.vector
        def _(dve):
            c = Count(dve, v)
            for t in [6, 0, 1, 2, 3]:
                c.link(dve.tensor_tensor(diff[:], rw[:, t, 0:T], rw[:, t, 1:T + 1], ALU.subtract))
                c.link(dve.scalar_tensor_tensor(mixed[:, t], diff[:], cols["mu"][:, t:t + 1], rw[:, t, 1:T + 1],
                                                ALU.mult, ALU.add))
            c.add(dve.memset(ones[:], 1.0))
            for t in range(2):
                c.link(dve.tensor_scalar(kk[:, t], mixed[:, 2 + t], cols["k_k"][:, t:t + 1], None, ALU.mult))
                c.link(dve.tensor_tensor(work[:, t], kk[:, t], kk[:, t], ALU.mult))
            dve.wait_ge(a, 3 + 4)
            for t in range(2):
                c.link(dve.tensor_scalar(ld[:, t], ld[:, t], -math.exp(-0.5), None, ALU.mult))
                for n in range(NCH):
                    part = slice(n * CHUNK, (n + 1) * CHUNK)
                    c.add(dve.tensor_tensor_scan(run[:, t, part], ones[:, part], ld[:, t, part], 0.0,
                                                 ALU.mult, ALU.add))
            c.settle()
            for t in range(2):
                ends = run[:, t].rearrange("p (n w) -> p n w", w=CHUNK)[:, :, CHUNK - 1]
                c.add(dve.tensor_scalar(tot[:, t], ends, 1.0, None, ALU.mult))
                c.link(dve.tensor_scalar(mid[:, t], ends, 0.5, None, ALU.mult))
                c.link(dve.tensor_tensor(run[:, t].rearrange("p (n w) -> p n w", w=CHUNK),
                                         run[:, t].rearrange("p (n w) -> p n w", w=CHUNK),
                                         mid[:, t].unsqueeze(2).to_broadcast([P, NCH, CHUNK]), ALU.subtract))
                c.link(dve.tensor_tensor(ld[:, t], run[:, t], ld[:, t], ALU.subtract))
            dve.wait_ge(sums_done, 1)
            for t in range(2):
                c.link(dve.tensor_scalar(work[:, t], psum[:, 4 + t], 1e-24, None, ALU.max))
            dve.wait_ge(a, 7 + 2)
            for t in range(2):
                c.link(dve.reciprocal(work[:, t], root[:, t]))
                c.link(dve.tensor_tensor(kk[:, t], kk[:, t], work[:, t], ALU.mult))
            dve.wait_ge(a, 9 + 6)
            for t in range(2):
                c.link(dve.scalar_tensor_tensor(a_in[:, t], kk[:, t], -1.0, e_before[:, t], ALU.mult, ALU.mult))
                c.link(dve.tensor_tensor(kk[:, t], kk[:, t], rate[:, t], ALU.mult))
                c.add(dve.tensor_tensor(b_in[:, t], kk[:, t], e_neg[:, t], ALU.mult))
                c.link(dve.tensor_scalar(rate[:, t], rate[:, t], 1.0, None, ALU.subtract))
                c.link(dve.tensor_scalar(rate[:, t], rate[:, t], cols["k_a"][:, t:t + 1], 1.0, ALU.mult, ALU.add))
                c.link(dve.tensor_tensor(rate[:, t], rate[:, t], mixed[:, 2 + t], ALU.mult))
                c.add(dve.tensor_tensor(k_in[:, t], rate[:, t], e_neg[:, t], ALU.mult))
                c.link(dve.scalar_tensor_tensor(work[:, t], mixed[:, t], cols["r_k"][:, t:t + 1], rate[:, t],
                                                ALU.mult, ALU.mult))
            dve.wait_ge(shifted, 6)
            dve.wait_ge(sums_done, 2)
            for t in range(2):
                c.add(dve.tensor_tensor(bonus[:, t], psum[:, 6 + t], mixed[:, 4 + t], ALU.mult))

        @block.scalar
        def _(act):
            c = Count(act, a)
            act.wait_ge(v, 2)
            c.add(act.activation(low[0:32], mixed[0:32, 6], ACT.Tanh))
            c.add(act.activation(low[32:64], mixed[32:64, 6], ACT.Identity))
            c.add(act.activation(low[64:128], mixed[64:128, 6], ACT.Sigmoid))
            act.wait_ge(up_done, 1)
            for t in range(2):
                c.add(act.activation(ld[:, t], psum[:, t], ACT.Sigmoid, bias=cols["w0"][:, t:t + 1]))
                c.add(act.activation(rate[:, t], psum[:, 2 + t], ACT.Sigmoid, bias=cols["a0"][:, t:t + 1]))
            act.wait_ge(v, 35)
            for t in range(2):
                c.add(act.activation(root[:, t], work[:, t], ACT.Sqrt))
            for t in range(2):
                c.add(act.activation(e_pos[:, t], run[:, t], ACT.Exp))
                c.add(act.activation(e_before[:, t], ld[:, t], ACT.Exp))
                c.add(act.activation(e_neg[:, t], run[:, t], ACT.Exp, scale=-1.0))
            act.wait_ge(up_done, 2)
            for t in range(2):
                c.add(act.activation(gate[:, t], psum[:, t], ACT.Copy))

        @block.tensor
        def _(pe):
            pe.wait_ge(up_in, 48)
            pe.wait_ge(a, 3)
            for t in range(2):
                c = slice(t * P, (t + 1) * P)
                pe.matmul(psum[:, t], w_up[0:32, c], low[0:32], start=True, stop=True)
                mm = pe.matmul(psum[:, 2 + t], w_up[32:64, c], low[32:64], start=True, stop=True)
            mm.then_inc(up_done, 1)
            pe.wait_ge(v, 15)
            for t in range(2):
                mm = pe.matmul(psum[:, 4 + t], square[:, HEADS], work[:, t], start=True, stop=True)
            mm.then_inc(sums_done, 1)
            pe.wait_ge(a, 7)
            for t in range(2):
                mm = pe.matmul(psum[:, t], w_up[64:128, t * P:(t + 1) * P], low[64:128], start=True, stop=True)
            mm.then_inc(up_done, 1)
            pe.wait_ge(v, 55)
            for t in range(2):
                mm = pe.matmul(psum[:, 6 + t], square[:, HEADS], work[:, t], start=True, stop=True)
            mm.then_inc(sums_done, 1)


def rwkv_chunks(nc, old, square, r_in, a_in, k_in, b_in, v_in, tot, mid, y):
    H = 4
    with Stage(nc, "rwkv", old) as s:
        ab = s.sb("ab", [P, NCH, H * P])
        ak = s.sb("ak", [P, NCH, H * P])
        rb = s.sb("rb", [P, NCH, H * P])
        rk = s.sb("rk", [P, NCH, H * P])
        tok = s.sb("tok", [P, NCH, 3, 2 * P])
        inv = s.sb("inv", [P, NCH, H * P])
        inv_t = s.sb("inv_t", [P, NCH, H * P])
        quarter = s.sb("quarter", [P, NCH, H * P])
        half = s.sb("half", [P, 2, H * P])
        state = s.sb("state", [P, 2, HD])
        centred = s.sb("centred", [P, 2, HD])
        z = s.sb("z", [P, H, HD])
        u = s.sb("u", [P, H, HD])
        factors = s.sb("factors", [P, 2, 2, NCH])
        psum = s.ps("psum", 8)
        g_done, g_kept, t_done, t_kept = s.sem("gram"), s.sem("gram_kept"), s.sem("turned"), s.sem("turned_kept")
        q_ready, h_done, h_kept, x_done, x_kept = (s.sem(n) for n in
                                                   ("quarter", "half", "half_kept", "inv", "inv_kept"))
        fac, c_done, c_kept = s.sem("factors"), s.sem("chain"), s.sem("chain_kept")
        y_done, y_kept = s.sem("y"), s.sem("y_kept")
        block = s.block()
        ident = square[:, IDENT]

        def rows(h):
            return slice(HD * (h % 2), HD * (h % 2) + HD)

        def cols(n):
            return slice(n * CHUNK, (n + 1) * CHUNK)

        def bank4(ap, h):
            return ap[:, h * P:(h + 1) * P]

        grams = [(ab, b_in, a_in, STRICT), (ak, k_in, a_in, STRICT), (rb, b_in, r_in, INCL), (rk, k_in, r_in, INCL)]

        def second_half(pe, i):
            level, n = divmod(i, NCH)
            pe.wait_ge(h_kept, i - NCH + 1)
            pe.wait_ge(x_kept, 2 * i if level < 6 else 12 * NCH + n)
            for h in range(H) if level < 6 else ():
                mm = pe.matmul(bank4(psum[:, 2], h), bank4(inv_t[:, n], h), bank4(half[:, i % 2], h),
                               start=True, stop=True)
            for h in range(H):
                mm = pe.matmul(bank4(psum[:, 3], h), bank4(half[:, i % 2], h), bank4(inv_t[:, n], h),
                               start=True, stop=True)
            mm.then_inc(x_done, 1)

        @block.tensor
        def _(pe):
            warm_up(pe, psum[:, 0], square)
            g = 0
            for dst, left, right, _ in grams:
                for n in range(NCH):
                    if g >= 2:
                        pe.wait_ge(g_kept, g - 1)
                    for h in range(H):
                        mm = pe.matmul(bank4(psum[:, 2 * (g % 2) + h % 2], h // 2), left[rows(h), h // 2, cols(n)],
                                       right[rows(h), h // 2, cols(n)], start=True, stop=True)
                    mm.then_inc(g_done, 1)
                    g += 1
            for i, src in enumerate((b_in, k_in, v_in)):
                for n in range(NCH):
                    q = i * NCH + n
                    if q >= 2:
                        pe.wait_ge(t_kept, q - 1)
                    for t in range(2):
                        mm = pe.transpose(psum[:, 4 + q % 2, t * P:(t + 1) * P], src[:, t, cols(n)], ident)
                    mm.then_inc(t_done, 1)
            pe.wait_ge(g_kept, 16)
            for n in range(NCH):
                pe.wait_ge(q_ready, n + 1)
                if n >= 1:
                    pe.wait_ge(x_kept, 2 * n)
                for h in range(H):
                    mm = pe.transpose(bank4(psum[:, 2], h), bank4(quarter[:, n], h), ident)
                mm.then_inc(x_done, 1)
            i = NCH
            for level in range(1, 7):
                for n in range(NCH):
                    pe.wait_ge(q_ready, i + 1)
                    pe.wait_ge(x_kept, 2 * (i - NCH) + 2)
                    if i >= NCH + 2:
                        pe.wait_ge(h_kept, i - NCH - 1)
                    for h in range(H):
                        mm = pe.matmul(bank4(psum[:, i % 2], h), bank4(quarter[:, n], h), bank4(inv[:, n], h),
                                       start=True, stop=True)
                    mm.then_inc(h_done, 1)
                    if i >= NCH + 1:
                        second_half(pe, i - 1)
                    i += 1
            second_half(pe, i - 1)
            m = 0
            for n in range(NCH):
                pe.wait_ge(c_kept, 3 * n + 1)
                if n == 0:
                    pe.wait_ge(t_kept, 3 * NCH)
                    pe.wait_ge(x_kept, 13 * NCH)
                for h in range(H):
                    o = psum[:, h % 2, (h // 2) * HD:(h // 2 + 1) * HD]
                    pe.matmul(o, a_in[rows(h), h // 2, cols(n)], centred[rows(h), h // 2], start=True, stop=False)
                    mm = pe.matmul(o, bank4(ak[:, n], h), tok[:, n, 2, h * HD:(h + 1) * HD],
                                   start=False, stop=True)
                mm.then_inc(c_done, 1)
                pe.wait_ge(c_kept, 3 * n + 2)
                for h in range(H):
                    mm = pe.matmul(psum[:, 2, h * HD:(h + 1) * HD], bank4(inv_t[:, n], h), z[:, h],
                                   start=True, stop=True)
                mm.then_inc(c_done, 1)
                pe.wait_ge(c_kept, 3 * n + 3)
                for h in range(H):
                    o = psum[rows(h), 3, (h // 2) * HD:(h // 2 + 1) * HD]
                    pe.matmul(o, tok[:, n, 0, h * HD:(h + 1) * HD], u[:, h], start=True, stop=False)
                    mm = pe.matmul(o, tok[:, n, 1, h * HD:(h + 1) * HD], tok[:, n, 2, h * HD:(h + 1) * HD],
                                   start=False, stop=True)
                mm.then_inc(c_done, 1)
                if n >= 1:
                    pe.wait_ge(y_kept, n)
                for h in range(H):
                    o = psum[rows(h), 4 + h // 2, 0:P]
                    pe.matmul(o, centred[rows(h), h // 2], r_in[rows(h), h // 2, cols(n)], start=True, stop=False)
                    pe.matmul(o, u[:, h], bank4(rb[:, n], h), start=False, stop=False)
                    mm = pe.matmul(o, tok[:, n, 2, h * HD:(h + 1) * HD], bank4(rk[:, n], h),
                                   start=False, stop=True)
                mm.then_inc(y_done, 1)

        @block.scalar
        def _(act):
            for q in range(3 * NCH):
                act.wait_ge(t_done, q + 1)
                act.activation(tok[:, q % NCH, q // NCH], psum[:, 4 + q % 2, 0:2 * P], ACT.Copy).then_inc(t_kept, 1)
            act.activation(factors[:, 0].rearrange("p t n -> p (t n)"), mid[:].rearrange("p t n -> p (t n)"),
                           ACT.Exp).then_inc(fac, 1)
            act.activation(factors[:, 1].rearrange("p t n -> p (t n)"), tot[:].rearrange("p t n -> p (t n)"),
                           ACT.Exp).then_inc(fac, 1)
            for i in range(NCH, 7 * NCH):
                act.wait_ge(h_done, i - NCH + 1)
                if i >= NCH + 2:
                    act.wait_ge(x_done, i - 1)
                act.activation(half[:, i % 2], psum[:, i % 2], ACT.Copy).then_inc(h_kept, 1)
            for n in range(NCH):
                act.wait_ge(y_done, n + 1)
                for t in range(2):
                    last = act.activation(y[:, t, cols(n)], psum[:, 4 + t, 0:P], ACT.Copy)
                last.then_inc(y_kept, 1)

        @block.gpsimd
        def _(pool):
            for i in range(7 * NCH):
                level, n = divmod(i, NCH)
                pool.wait_ge(g_kept, n + 1)
                if level == 1:
                    pool.wait_ge(x_kept, 2 * n + 2)
                if level > 1:
                    pool.wait_ge(h_done, i - 2 * NCH + 1)
                pool.tensor_tensor(quarter[:, n].rearrange("p (h t) -> p h t", h=H),
                                   ab[:, n].rearrange("p (h t) -> p h t", h=H),
                                   square[:, LEVELS + level].unsqueeze(1).to_broadcast([P, H, P]), ALU.mult)\
                    .then_inc(q_ready, 1)

        @block.vector
        def _(dve):
            g = 0
            for n in range(NCH):
                for x in (inv, inv_t):
                    dve.tensor_copy(x[:, n].rearrange("p (h t) -> p h t", h=H),
                                    ident.unsqueeze(1).to_broadcast([P, H, P]))
            for dst, _, _, mask in grams:
                for n in range(NCH):
                    dve.wait_ge(g_done, g + 1)
                    for odd in range(2):
                        last = dve.tensor_tensor(
                            dst[:, n].rearrange("p (q r t) -> p r q t", q=2, r=2)[:, odd],
                            psum[:, 2 * (g % 2) + odd, 0:2 * P].rearrange("p (q t) -> p q t", q=2),
                            square[:, mask].unsqueeze(1).to_broadcast([P, 2, P]), ALU.mult)
                    last.then_inc(g_kept, 1)
                    g += 1
            for i in range(7 * NCH):
                level, n = divmod(i, NCH)
                dve.wait_ge(x_done, i + 1)
                if level < 6:
                    dve.tensor_tensor(inv[:, n], inv[:, n], psum[:, 2], ALU.add).then_inc(x_kept, 1)
                dve.tensor_tensor(inv_t[:, n], inv_t[:, n], quarter[:, n] if level == 0 else psum[:, 3], ALU.add)\
                   .then_inc(x_kept, 1)
            c = Count(dve, c_kept)
            dve.memset(state[:], 0.0)
            c.link(dve.memset(centred[:], 0.0))
            dve.wait_ge(fac, 2)
            for n in range(NCH):
                dve.wait_ge(c_done, 3 * n + 1)
                for odd in range(2):
                    last = dve.tensor_copy(z[:].rearrange("p (q r) d -> p r q d", r=2)[:, odd],
                                           psum[:, odd, 0:2 * HD].rearrange("p (q d) -> p q d", q=2))
                c.add(last)
                dve.wait_ge(c_done, 3 * n + 2)
                c.add(dve.tensor_copy(u[:].rearrange("p h d -> p (h d)"), psum[:, 2, 0:H * HD]))
                dve.wait_ge(c_done, 3 * n + 3)
                if n == NCH - 1:
                    break
                for t in range(2):
                    dve.tensor_scalar(state[:, t], state[:, t], factors[:, 1, t, n:n + 1], None, ALU.mult)\
                       .then_inc(fac, 1)
                dve.wait_ge(fac, 2 + 4 * n + 2)
                for t in range(2):
                    dve.scalar_tensor_tensor(state[:, t], psum[:, 3, t * HD:(t + 1) * HD],
                                             factors[:, 0, t, n:n + 1], state[:, t], ALU.mult, ALU.add)\
                       .then_inc(fac, 1)
                dve.wait_ge(fac, 2 + 4 * n + 4)
                dve.wait_ge(y_done, n + 1)
                dve.tensor_scalar(centred[:, 0], state[:, 0], factors[:, 0, 0, n + 1:n + 2], None, ALU.mult)
                c.add(dve.tensor_scalar(centred[:, 1], state[:, 1], factors[:, 0, 1, n + 1:n + 2], None, ALU.mult))


def rwkv_output(nc, old, y, gate, bonus, cols, square, out):
    with Stage(nc, "rwkv_out", old) as s:
        work = s.sb("work", [P, 2, T])
        rstd = s.sb("rstd", [P, 2, T])
        eps = s.sb("eps", [P, 1])
        psum = s.ps("psum", 4)
        v, a, m = s.sem("dve"), s.sem("act"), s.sem("sums")
        block = s.block()

        @block.tensor
        def _(pe):
            for t in range(2):
                pe.matmul(psum[:, t], square[:, HEADS], y[:, t], start=True, stop=True).then_inc(m, 1)
            for t in range(2):
                pe.wait_ge(a, t + 1)
                pe.matmul(psum[:, 2 + t], square[:, HEADS], work[:, t], start=True, stop=True).then_inc(m, 1)

        @block.scalar
        def _(act):
            c = Count(act, a)
            for t in range(2):
                act.wait_ge(v, 2 + t)
                c.add(act.activation(work[:, t], y[:, t], ACT.Square))
            for t in range(2):
                act.wait_ge(m, 3 + t)
                c.link(act.activation(rstd[:, t], psum[:, 2 + t], ACT.Ln, bias=eps[:, 0:1], scale=1.0 / HD))
            for t in range(2):
                c.link(act.activation(rstd[:, t], rstd[:, t], ACT.Exp, scale=-0.5))

        @block.vector
        def _(dve):
            c = Count(dve, v)
            c.link(dve.memset(eps[:], GN_EPS))
            for t in range(2):
                dve.wait_ge(m, t + 1)
                c.link(dve.scalar_tensor_tensor(y[:, t], psum[:, t], -1.0 / HD, y[:, t], ALU.mult, ALU.add))
            dve.wait_ge(a, 6)
            for t in range(2):
                c.link(dve.scalar_tensor_tensor(y[:, t], y[:, t], cols["ln_w"][:, t:t + 1], rstd[:, t],
                                                ALU.mult, ALU.mult))
                c.link(dve.scalar_tensor_tensor(y[:, t], y[:, t], cols["ln_b"][:, t:t + 1], bonus[:, t],
                                                ALU.add, ALU.add))
                c.link(dve.tensor_tensor(out[:, t], y[:, t], gate[:, t], ALU.mult))



def distance_tables(s, block, onehot, bias, scratch, tables, tables_out):
    kinds = [0] * H_NSA + [1] * 4 + [2] * 4 + [3] * 4 + [4] * (B_HEADS + C_HEADS + 1)
    groups, start = [], 0
    for h in range(1, N_TABLES + 1):
        if h == N_TABLES or kinds[h] != kinds[start]:
            groups.append((start, h, kinds[start]))
            start = h
    half = TABLE_LEN // 2
    hot = s.sb("hot", [33, 5, TABLE_LEN])
    rows = s.sb("rows", [32, len(groups), TABLE_LEN])
    psum = s.ps("rows_psum", 4)
    loaded, done, kept, out = s.sem("hot_in"), s.sem("rows_done"), s.sem("rows_kept"), s.sem("rows_out")

    @block.scalar
    def _(act):
        act.dma_start(hot[:], onehot).then_inc(loaded, 16)
        for g, (a, b, _) in enumerate(groups):
            for c in range(2):
                i = 2 * g + c
                act.wait_ge(done, i + 1)
                act.activation(rows[0:b - a, g, c * half:(c + 1) * half], psum[0:b - a, i % 4, 0:half], ACT.Copy)\
                   .then_inc(kept, 1)
            act.wait_ge(kept, 2 * g + 2)
            act.dma_start(scratch[a:b, :], rows[0:b - a, g]).then_inc(out, 16)
        act.wait_ge(out, 16 * len(groups))
        for a in range(0, N_TABLES, N_TABLES // TABLE_STORES):
            rows_at = scratch[a:a + N_TABLES // TABLE_STORES, :]
            act.dma_start(tables[a:a + N_TABLES // TABLE_STORES], bass.AP(rows_at.tensor, rows_at.offset + P - 1,
                                                   [[TABLE_LEN, N_TABLES // TABLE_STORES], [-1, P], [1, T]])).then_inc(tables_out, 16)

    @block.tensor
    def _(pe):
        pe.wait_ge(loaded, 16)
        for g, (a, b, kind) in enumerate(groups):
            for c in range(2):
                i = 2 * g + c
                if i >= 4:
                    pe.wait_ge(kept, i - 3)
                pe.matmul(psum[0:b - a, i % 4, 0:half], bias[:, a:b], hot[:, kind, c * half:(c + 1) * half],
                          start=True, stop=True).then_inc(done, 1)


SCORES, LAG, AHEAD = 8, 4, 2


class Piece:

    def __init__(self, q, k, v, lo, keys, table, extra=None, plus=None, table_no=0):
        self.q, self.k, self.v, self.lo, self.keys, self.table = q, k, v, lo, keys, table
        self.extra, self.plus, self.table_no = extra, plus, table_no


def attention(nc, old, name, units, width, tables, finish, prepare=None, beside=None, tables_out=None,
              keep_warm=0):
    pieces = [(u, c, piece) for u, unit in enumerate(units) for c, piece in enumerate(unit)]
    n_pieces, n_units = len(pieces), len(units)
    last_of = [max(i for i, (u, _, _) in enumerate(pieces) if u == w) for w in range(n_units)]
    with Stage(nc, name, old) as s:
        scores = s.sb("scores", [P, SCORES, T])
        turned = s.sb("turned", [P, 2, T])
        peak = s.sb("peak", [P, 8, 4])
        sums = s.sb("sums", [P, 8, 4])
        weight = s.sb("weight", [P, 8])
        spacer = s.sb("spacer", [1, 8])
        psum = s.ps("psum", 8)
        prepared = s.sem("prepared")
        tabled = [s.sem(f"tabled{n}") for n in range(len(tables))]
        scored, biased, peaked, exped = s.sem("scored"), s.sem("biased"), s.sem("peaked"), s.sem("exped")
        turn, copied, weighed, finished = s.sem("turn"), s.sem("copied"), s.sem("weighed"), s.sem("finished")
        small = s.sem("small")
        if beside is not None:
            beside.place(s)
            first_beside = n_pieces - beside.steps
        block = s.block()

        @block.sync
        def _(sp):
            if tables_out is not None:
                sp.wait_ge(tables_out, 16 * TABLE_STORES)
            for n, (dst, src) in enumerate(tables):
                sp.dma_start(dst, src).then_inc(tabled[n], 16)
        n_prepared = 0
        if prepare is not None:
            @block.gpsimd
            def _(pool):
                nonlocal n_prepared
                n_prepared = prepare(pool, prepared)

        @block.tensor
        def _(pe):
            pe.sem_inc(turn, SCORES)
            pe.sem_inc(weighed, 2)
            warm_up(pe, psum[:, 0], attention.square)

            if n_prepared:
                pe.wait_ge(prepared, n_prepared)
            for i in range(n_pieces + LAG + 1):
                if i < n_pieces:
                    u, c, x = pieces[i]
                    if i >= 4:
                        pe.wait_ge(biased, i - 3)
                    if keep_warm and i > LAG:
                        warm_up(pe, psum[:, i % 4, 0:keep_warm], attention.square, 1)
                    cols = slice(x.lo * P, x.lo * P + x.keys)
                    mm = pe.matmul(psum[:, i % 4, 0:x.keys], x.q, x.k[:, cols], start=True,
                                   stop=x.extra is None)
                    if x.extra is not None:
                        mm = pe.matmul(psum[:, i % 4, 0:x.keys], x.extra[0], x.extra[1][:, cols],
                                       start=False, stop=True)
                    mm.then_inc(scored, 1)
                if LAG <= i < n_pieces + LAG:
                    t = i - LAG
                    x = pieces[t][2]
                    pe.wait_ge(exped, t + 1)
                    pe.wait_ge(copied, t + 1)
                    for j in range(-(-x.keys // P)):
                        n = min(P, x.keys - j * P)
                        mm = pe.transpose(psum[0:n, 4 + t % 2, j * P:j * P + P],
                                          scores[:, t % SCORES, j * P:j * P + n], attention.ident)
                    mm.then_inc(turn, 1)
                if i >= LAG + 1:
                    t = i - LAG - 1
                    u, c, x = pieces[t]
                    pe.wait_ge(copied, t + 3)
                    if c == 0:
                        pe.wait_ge(finished, u + 1)
                    blocks = -(-x.keys // P)
                    for j in range(blocks):
                        n = min(P, x.keys - j * P)
                        mm = pe.matmul(psum[:, 6 + u % 2, 0:width],
                                       turned[0:n, t % 2, j * P:j * P + P], x.v(x.lo + j),
                                       start=c == 0 and j == 0, stop=t == last_of[u] and j == blocks - 1)
                    mm.then_inc(weighed, 1)

        @block.scalar
        def _(act):
            act.sem_inc(copied, 2)

            for i in range(n_pieces + AHEAD):
                if i >= AHEAD:
                    t = i - AHEAD
                    x = pieces[t][2]
                    act.wait_ge(turn, t + 1 + SCORES)
                    act.wait_ge(weighed, t + 1)
                    n = min(P, x.keys)
                    w = -(-x.keys // P) * P
                    act.activation(turned[0:n, t % 2, 0:w], psum[0:n, 4 + t % 2, 0:w], ACT.Copy)\
                       .then_inc(copied, 1)
                if i < n_pieces:
                    u, c, x = pieces[i]
                    act.wait_ge(peaked, u + 1)
                    b = scores[:, i % SCORES, 0:x.keys]
                    act.activation(b, b, ACT.Exp, bias=peak[:, u % 8, 3:4],
                                   accum_out=sums[:, u % 8, c:c + 1]).then_inc(exped, 1)

        @block.vector
        def _(dve):
            dve.sem_inc(finished, 2)
            small_c = Count(dve, small)

            def end(u, count):
                dve.wait_ge(weighed, last_of[u] + 3)
                total = sums[:, u % 8, 0:1]
                for c in range(1, len(units[u])):
                    count.link(dve.tensor_tensor(total, total, sums[:, u % 8, c:c + 1], ALU.add))
                count.link(dve.tensor_scalar(total, total, 1e-30, None, ALU.max))
                count.link(dve.reciprocal(weight[:, u % 8:u % 8 + 1], total))
                finish(dve, u, psum[:, 6 + u % 2, 0:width], weight[:, u % 8:u % 8 + 1], count,
                       finished)

            for i in range(n_pieces + LAG + 2):
                if i < n_pieces:
                    u, c, x = pieces[i]
                    dve.wait_ge(tabled[x.table_no], 16)
                    dve.wait_ge(scored, i + 1)
                    dve.wait_ge(turn, i + 1)
                    raw = psum[:, i % 4, 0:x.keys]
                    out = scores[:, i % SCORES, 0:x.keys]
                    if x.plus is not None:
                        small_c.link(dve.tensor_tensor(out, raw, x.plus, ALU.add))
                        raw = out
                    dve.memset(spacer[:, i % 8:i % 8 + 1], 0.0)
                    dve.tensor_tensor_reduce(out, raw, x.table, 1.0, LOWEST, ALU.add, ALU.max,
                                             peak[:, u % 8, c:c + 1]).then_inc(biased, 1)
                    if i == last_of[u]:
                        dve.wait_ge(biased, i + 1)
                        for d in range(1, c + 1):
                            small_c.link(dve.tensor_tensor(peak[:, u % 8, 0:1], peak[:, u % 8, 0:1],
                                                           peak[:, u % 8, d:d + 1], ALU.max))
                        dve.tensor_scalar(peak[:, u % 8, 3:4], peak[:, u % 8, 0:1], -1.0, None, ALU.mult)\
                           .then_inc(peaked, 1)
                t = i - LAG - 2
                if t >= 0 and last_of[pieces[t][0]] == t:
                    end(pieces[t][0], small_c)
                if beside is not None and 0 <= i - first_beside < beside.steps:
                    beside.add(dve, i - first_beside)
        if beside is not None:
            beside.rest(block, psum[:, 0], biased, n_pieces)


def to_channels(nc, old, name, ident, tiles, scale=1.0):
    with Stage(nc, name, old) as s:
        psum = s.ps("psum", 2)
        done, kept, lowered = s.sem("done"), s.sem("kept"), s.sem("lowered")
        pairs = isinstance(tiles[0][1], list)
        block = s.block()

        @block.tensor
        def _(pe):
            for n, (src, _) in enumerate(tiles):
                if n >= 2:
                    pe.wait_ge(lowered if pairs else kept, n - 1)
                for i in range(TT):
                    mm = pe.transpose(psum[:, n % 2, i * P:(i + 1) * P], src[:, i], ident)
                mm.then_inc(done, 1)

        @block.scalar
        def _(act):
            for n, (_, dst) in enumerate(tiles):
                act.wait_ge(done, n + 1)
                act.activation(dst[0] if pairs else dst, psum[:, n % 2], ACT.Copy, scale=scale).then_inc(kept, 1)

        @block.vector
        def _(dve):
            for n, (_, dst) in enumerate(tiles if pairs else []):
                dve.wait_ge(kept, n + 1)
                dve.tensor_tensor(dst[1], psum[:, n % 2], dst[0].bitcast(F32), ALU.subtract).then_inc(lowered, 1)


def fox_decay(s, block, logit, b_f, heads, left, right):
    x = s.sb("fox_x", [H_FOX, T])
    e = s.sb("fox_e", [H_FOX, T])
    n = s.sb("fox_n", [H_FOX, T])
    ones = s.sb("fox_ones", [H_FOX, T])
    v, a = s.sem("fox_dve"), s.sem("fox_act")
    r = slice(0, H_FOX)

    @block.vector
    def _(dve):
        c = Count(dve, v)
        c.add(dve.memset(left[:], 1.0))
        c.add(dve.memset(right[:], 1.0))
        c.add(dve.memset(ones[:], 1.0))
        c.link(dve.tensor_scalar(x[:], logit[0:H_FOX], b_f, None, ALU.add))
        c.link(dve.scalar_tensor_tensor(e[:], x[:], -1.0, x[:], ALU.mult, ALU.min))
        c.link(dve.tensor_scalar(x[:], x[:], 0.0, None, ALU.min))
        dve.wait_ge(a, 2)
        c.link(dve.tensor_tensor(n[:], x[:], e[:], ALU.subtract))
        c.link(dve.tensor_tensor_scan(left[0:H_FOX], ones[:], n[:], 0.0, ALU.mult, ALU.add))
        c.add(dve.tensor_copy(left[HD:HD + H_FOX], left[0:H_FOX]))
        for base in (32, HD + 32):
            c.add(dve.tensor_scalar(right[base:base + H_FOX], left[0:H_FOX], -1.0, None, ALU.mult))

    @block.scalar
    def _(act):
        act.wait_ge(v, 6)
        act.activation(e[:], e[:], ACT.Exp).then_inc(a, 1)
        act.wait_ge(a, 1)
        act.activation(e[:], e[:], ACT.Ln, bias=1.0).then_inc(a, 1)


def fox_attention(nc, old, pj, fv, left, right, heads, tables_dram, tables_out, out):
    with nc.sbuf_tensor("fox_gates", [P, H_FOX // 2, T], F32) as gates, nc.sbuf_tensor("fox_table", [P, T], F32) as table:
        def prepare(pool, prepared):
            for p in range(H_FOX // 2):
                pool.tensor_tensor(gates[:, p], right[:], heads[:, p:p + 1].to_broadcast([P, T]), ALU.mult)\
                    .then_inc(prepared, 1)
            return H_FOX // 2

        units, where = [], []
        for h in range(H_FOX):
            p, a = divmod(h, 2)
            rows = slice(a * HD, (a + 1) * HD)
            q, k = pj[rows, RW_TILES + p, 1:T + 1], pj[rows, RW_TILES + 3 + p, 1:T + 1]
            for i in reversed(range(TT)):
                tokens = slice(i * P, (i + 1) * P)
                units.append([Piece(q[:, tokens], k, lambda j, h=h: fv[:, j, h * HD:(h + 1) * HD], 0, (i + 1) * P,
                                    table[:, (TT - 1 - i) * P:], extra=(left[rows, tokens], gates[rows, p]))])
                where.append((h, i))

        def finish(dve, u, o, w, count, finished):
            h, i = where[u]
            dve.tensor_scalar(out[:, i, h * HD:(h + 1) * HD], o, w, None, ALU.mult).then_inc(finished, 1)
        attention(nc, old, "fox", units, HD, [(table[:], tables_dram[TAB_FOX])], finish, prepare,
                  tables_out=tables_out)


def nsa_compress(nc, old, nk, pe_cols, w1s, w2s, kcmp, vcmp, beside):
    blocks = T // D_CMP
    width = 2 * blocks + 1
    with Stage(nc, "compress", old) as s:
        w1 = s.sb("w1", [P, 2, L_CMP // 2, CMP_HID])
        w2 = s.sb("w2", [P, 2, HD])
        tokens = s.sb("tokens", [P, 2, 2 * T + L_CMP])
        rows = s.sb("rows", [width, 2, CMP_HID])
        pos = s.sb("pos", [P, 2])
        hid = s.sb("hid", [P, 4, blocks])
        x = s.sb("x", [P, 4, blocks])
        w = s.sb("w", [P, 4, blocks])
        psum = s.ps("psum", 7)
        loaded = [s.sem(f"loaded{n}") for n in range(2)]
        moved, placed = s.sem("moved"), s.sem("placed")
        done, v, a, kept = s.sem("done"), s.sem("dve"), s.sem("act"), s.sem("kept")
        block = s.block()

        @block.sync
        def _(sp):
            for n in range(2):
                for c in range(2):
                    part = slice(c * (L_CMP // 4), (c + 1) * (L_CMP // 4))
                    sp.dma_start(w1[:, n, part], w1s[n][:, part]).then_inc(loaded[n], 16)
                sp.dma_start(w2[:, n], w2s[n]).then_inc(loaded[n], 16)

        @block.scalar
        def _(act):
            for n in range(2):
                act.dma_start(tokens[0:HD, n, T:2 * T], nk[HD:P, n, :]).then_inc(moved, 16)
                act.dma_start(tokens[HD:P, n, 0:T - 1], nk[0:HD, n, 1:T]).then_inc(moved, 16)

        @block.gpsimd
        def _(pool):
            for n in range(2):
                pool.tensor_copy(tokens[0:HD, n, 0:T], nk[0:HD, n, :])
                pool.tensor_copy(tokens[HD:P, n, T:2 * T - 1], nk[HD:P, n, 1:T]).then_inc(placed, 1)

        @block.tensor
        def _(pe):
            pe.wait_ge(placed, 3)
            pe.wait_ge(moved, 64)
            for n in range(2):
                pe.wait_ge(loaded[n], 48)
                for j in range(L_CMP // 2):
                    mm = pe.matmul(psum[0:width, n, 0:CMP_HID],
                                   tokens[:, n, 2 * j:2 * j + D_CMP * (width - 1) + 1:D_CMP], w1[:, n, j],
                                   start=j == 0, stop=j == L_CMP // 2 - 1)
                mm.then_inc(done, 1)
            for n in range(2):
                pe.wait_ge(a, n + 1)
                pe.transpose(psum[:, 2 + n, 0:width], rows[:, n], attention.ident[0:width, 0:width]).then_inc(done, 1)
            pe.wait_ge(v, 8)
            for g in range(2):
                pe.matmul(psum[g * HD:(g + 1) * HD, 4, 0:N_CMP], w2[:, 0], hid[:, g, 0:N_CMP],
                          start=True, stop=True)
                mm = pe.matmul(psum[0:N_CMP, 5 + g, 0:HD], hid[:, 2 + g, 0:N_CMP], w2[:, 1], start=True, stop=True)
            mm.then_inc(done, 1)

        @block.vector
        def _(dve):
            for a_ in range(2):
                half = slice(a_ * HD, (a_ + 1) * HD)
                last = dve.tensor_copy(tokens[half, :, 2 * T:2 * T + L_CMP:2], pe_cols[half, :, a_::2])
            last.then_inc(placed, 1)
        beside(s, block)

        @block.scalar
        def _(act):
            for n in range(2):
                act.wait_ge(done, n + 1)
                act.activation(rows[:, n], psum[0:width, n, 0:CMP_HID], ACT.Copy).then_inc(a, 1)
            act.wait_ge(v, 7)
            act.activation(w[:, :, 0:N_CMP], w[:, :, 0:N_CMP], ACT.Sigmoid, scale=2.0 * math.sqrt(2.0 / math.pi))\
               .then_inc(a, 1)

        @block.vector
        def _(dve):
            c = Count(dve, v)
            for n in range(2):
                dve.wait_ge(done, 3 + n)
                c.link(dve.tensor_copy(pos[:, n:n + 1], psum[:, 2 + n, width - 1:width]))
                c.add(dve.tensor_scalar(x[:, 2 * n:2 * n + 2, 0:N_CMP],
                                        psum[:, 2 + n, 0:2 * blocks].rearrange("p (g b) -> p g b", g=2)[:, :, 0:N_CMP],
                                        pos[:, n:n + 1], None, ALU.add))
            c.settle()
            xv, wv = x[:, :, 0:N_CMP], w[:, :, 0:N_CMP]
            c.link(dve.tensor_tensor(wv, xv, xv, ALU.mult))
            c.link(dve.tensor_scalar(wv, wv, 0.044715, 1.0, ALU.mult, ALU.add))
            c.link(dve.tensor_tensor(wv, wv, xv, ALU.mult))
            dve.wait_ge(a, 3)
            c.link(dve.tensor_tensor(hid[:, :, 0:N_CMP], wv, xv, ALU.mult))
            dve.wait_ge(done, 5)
            dve.tensor_copy(kcmp[:], psum[:, 4, 0:N_CMP])
            dve.tensor_copy(vcmp[:, 0], psum[0:N_CMP, 5, 0:HD])
            dve.tensor_copy(vcmp[:, 1], psum[0:N_CMP, 6, 0:HD]).then_inc(kept, 1)


def nsa_attention(nc, old, nq, nk, nv, kcmp, vcmp, gates, tables_dram, out, beside):
    with nc.sbuf_tensor("nsa_tables", [P, H_NSA, T], F32) as tables, nc.sbuf_tensor("nsa_scaled", [P, 4], F32) as scaled:
        units, where = [], []
        for p in range(3):
            for a in range(2):
                rows = slice(a * HD, (a + 1) * HD)
                for i in reversed(range(TT)):
                    q = nq[rows, p, i * P:(i + 1) * P]
                    n = 2 * p + a
                    full = tables[:, n, (TT - 1 - i) * P:]
                    n_c = 8 * i + 7
                    first = (TT - 1 - i) * P + L_CMP - 1
                    coarse = tables[:, n, first:first + D_CMP * (n_c - 1) + 1:D_CMP]
                    units.append([Piece(q, kcmp[rows], lambda j, a=a, n_c=n_c: vcmp[0:n_c, a], 0, n_c, coarse,
                                        table_no=n)])
                    for b in range(2):
                        units.append([Piece(q, nk[rows, 2 + b], lambda j, b=b, rows=rows: nv[:, b, j, rows],
                                            0, (i + 1) * P, full, table_no=n)])
                    where += [(p + 3 * a, i, b) for b in range(3)]

        def finish(dve, u, o, w, count, finished):
            h, i, b = where[u]
            dst = out[:, i, h * HD:(h + 1) * HD]
            g = scaled[:, u % 4:u % 4 + 1]
            count.link(dve.tensor_tensor(g, w, gates[:, i, 3 * h + b:3 * h + b + 1], ALU.mult))
            if b == 0:
                dve.tensor_scalar(dst, o, g, None, ALU.mult).then_inc(finished, 1)
            else:
                dve.wait_ge(finished, u + 2)
                dve.scalar_tensor_tensor(dst, o, g, dst, ALU.mult, ALU.add).then_inc(finished, 1)
        attention(nc, old, "nsa", units, HD,
                  [(tables[:, 2 * p + a], tables_dram[TAB_NSA + p + 3 * a]) for p in range(3) for a in range(2)], finish,
                  beside=beside, keep_warm=KEEP_WARM)



def conv_hidden(nc, old, h, up, conv, hidden, before):
    halves = up.rearrange("k (w n) -> k w n", w=2).rearrange("(k p) w n -> p k w n", p=P)
    with Stage(nc, "conv_up", old) as s:
        st = Stream(s, 2 * KF, KD, lambda j, r: halves[:, :, j % 2, bass.ds((r * (RAW // 2) + j // 2) * P, P)],
                    lambda j, k: tile(h, k), before=before)
        mixed = s.sb("mixed", [P, 2, 2, T])
        gate = s.sb("gate", [P, 2, T])
        product = s.sb("product", [P, 2, T])
        based, first, gated, made, hidden_hi = (s.sem(n) for n in ("based", "first", "gated", "made", "hidden_hi"))
        block = s.block()

        @block.sync
        def _(sp):
            st.load(sp)

        @block.tensor
        def _(pe):
            st.multiply(pe)

        @block.scalar
        def _(act):
            def take(u, j, r):
                w, b, t = j % 2, j // 2, r * (RAW // 2) + j // 2
                st.wait_products(act, u)
                if w == 0:
                    act.wait_ge(made, t + 1)
                act.activation(mixed[:, b, w], st.bank(j), ACT.Identity,
                               bias=conv(t, w, 3), scale=conv(t, w, 2)).then_inc(based, 1)
                if w == 1:
                    act.wait_ge(st.free, u + st.banks)
                    act.activation(gate[:, b], mixed[:, b, 0], ACT.Silu).then_inc(gated, 1)
                    act.wait_ge(made, t + 3)
                    act.activation(tile_of(hidden[0], t), product[:, b], ACT.Copy).then_inc(hidden_hi, 1)
            rounds_ahead(act, st.units, lambda u, j, r: st.round_hi(act, u, j, r), take)

        @block.vector
        def _(dve):
            dve.sem_inc(st.free, st.banks)

            def convolve(u, j, r):
                w, b, t = j % 2, j // 2, r * (RAW // 2) + j // 2
                m = mixed[:, b, w]
                dve.wait_ge(based, u + 1)
                dve.scalar_tensor_tensor(m[:, 1:T], st.bank(j)[:, 0:T - 1], conv(t, w, 1), m[:, 1:T],
                                         ALU.mult, ALU.add).then_inc(first, 1)
                dve.wait_ge(first, u + 1)
                dve.scalar_tensor_tensor(m[:, 2:T], st.bank(j)[:, 0:T - 2], conv(t, w, 0), m[:, 2:T],
                                         ALU.mult, ALU.add).then_inc(st.free, 1)
            rounds_ahead(dve, st.units, lambda u, j, r: st.split_lo(dve, u, j, r), convolve)

        @block.gpsimd
        def _(pool):
            pool.sem_inc(made, 2)

            def combine(t, b, r):
                pool.wait_ge(st.free, t * 2 + (2 + st.banks))
                pool.wait_ge(gated, t + 1)
                pool.tensor_tensor(product[:, b], gate[:, b], mixed[:, b, 1], ALU.mult).then_inc(made, 1)
                pool.wait_ge(hidden_hi, t + 1)
                pool.tensor_tensor(tile_of(hidden[1], t), product[:, b], tile_of(hidden[0], t).bitcast(F32),
                                   ALU.subtract)
            rounds(pool, KF, 2, combine)


def glu_hidden(nc, old, name, h, w_gate, w_up, hidden, before, load_next):
    sources = [w.rearrange("(k p) n -> p k n", p=P) for w in (w_gate, w_up)]
    with Stage(nc, name, old) as s:
        st = Stream(s, 2 * KF, KD, lambda j, r: sources[j % 2][:, :, bass.ds((r * (RAW // 2) + j // 2) * P, P)],
                    lambda j, k: tile(h, k), before=before)
        gate = s.sb("gate", [P, 2, T])
        product = s.sb("product", [P, 2, T])
        gated, hidden_hi, hidden_lo = s.sem("gated"), s.sem("hidden_hi"), s.sem("hidden_lo")
        block = s.block()

        @block.sync
        def _(sp):
            st.load(sp)
            load_next(sp)

        @block.tensor
        def _(pe):
            st.multiply(pe)

        @block.scalar
        def _(act):
            def take(u, j, r):
                b, t = j // 2, r * (RAW // 2) + j // 2
                if j % 2 == 0:
                    st.wait_products(act, u)
                    act.activation(gate[:, b], st.bank(j), ACT.Silu).then_inc(gated, 1)
                else:
                    act.wait_ge(st.free, t * 2 + (2 + st.banks))
                    act.activation(tile_of(hidden[0], t), product[:, b], ACT.Copy).then_inc(hidden_hi, 1)
            rounds_ahead(act, st.units, lambda u, j, r: st.round_hi(act, u, j, r), take)

        @block.vector
        def _(dve):
            dve.sem_inc(st.free, st.banks)

            def combine(u, j, r):
                if j % 2 == 1:
                    b, t = j // 2, r * (RAW // 2) + j // 2
                    st.wait_products(dve, u)
                    dve.wait_ge(gated, t + 1)
                    dve.wait_ge(hidden_lo, t + 1)
                    dve.tensor_tensor(product[:, b], gate[:, b], st.bank(j), ALU.mult).then_inc(st.free, 2)
            rounds_ahead(dve, st.units, lambda u, j, r: st.split_lo(dve, u, j, r), combine)

        @block.gpsimd
        def _(pool):
            pool.sem_inc(hidden_lo, 2)

            def lower(t, b, r):
                pool.wait_ge(hidden_hi, t + 1)
                pool.tensor_tensor(tile_of(hidden[1], t), product[:, b], tile_of(hidden[0], t).bitcast(F32),
                                   ALU.subtract).then_inc(hidden_lo, 1)
            rounds(pool, KF, 2, lower)



class Pair:

    def __init__(self, nc, name, n):
        self.nc, self.name, self.n = nc, name, n

    def __enter__(self):
        self.ctx = ExitStack()
        return [self.ctx.enter_context(self.nc.sbuf_tensor(f"{self.name}_{part}", [P, self.n, T], F32R))
                for part in ("hi", "lo")]

    def __exit__(self, *exc):
        self.ctx.close()


def tile(pair, k):
    return [x[:, k] for x in pair]


def view(w):
    return w.rearrange("(k p) n -> p k n", p=P)


def first_block(nc, old, A, x_t, store_scale, tables_out, late_modulation, gains, mod, cols, square, scratch, heads, b_f):
    with ExitStack() as top:
        def sb(name, shape):
            return top.enter_context(nc.sbuf_tensor("one_" + name, shape, F32))

        y_r = sb("y_r", [P, 2, T])
        w_in = view(A["w_in"][0])
        with ExitStack() as mix:
            def mb(name, shape):
                return mix.enter_context(nc.sbuf_tensor("mix_" + name, shape, F32))
            nq = mb("nq", [P, 3, T])
            nk = mb("nk", [P, 4, T])
            nv = mb("nv", [P, 2, TT, P])
            gates = mb("gates", [P, TT, 3 * H_NSA])
            fv = mb("fv", [P, TT, C_FOX])
            logit = mb("logit", [H_FOX, T])
            pj = mb("pj", [P, RW_TILES + 6, T + 1])

            with Stage(nc, "zero", old) as s:
                block = s.block()
                @block.vector
                def _(dve):
                    dve.memset(pj[:, :, 0:1], 0.0)

            def store(act, t, psum):
                dst = pj[:, t, 1:T + 1] if isinstance(t, int) else flat(pj[:, bass.ds(t, 1), 1:T + 1])
                return act.activation(dst, psum, ACT.Identity, scale=store_scale[:, bass.ds(t, 1)])

            def columns_job(loads, dsts, func=ACT.Copy):
                return (loads, len(dsts) * P, [("columns", c * P, dst, func) for c, dst in enumerate(dsts)])

            def load_of(start, w, at=0):
                return (slice(at, at + w), w_in[:, :, start:start + w])

            def adjoining(start, n):
                return [(slice(0, n * P), w_in[:, :, start:start + n * P])]

            def heads_of_groups(c0, n):
                return [(slice((c - c0) * P + g * HD, (c - c0) * P + (g + 1) * HD),
                         w_in[:, :, NSA_Q + (g * 3 + c) * HD:NSA_Q + (g * 3 + c + 1) * HD])
                        for c in range(c0, c0 + n) for g in range(2)]
            jobs = [
                columns_job(adjoining(NSA_KW, 1), [nk[:, 3]]),
                ([load_of(FOX_V, 2 * P)], 2 * P,
                 [("tokens", [(0, 2 * P, [fv[:, i, 0:2 * P] for i in range(TT)], ACT.Copy)])]),
                ([load_of(FOX_V + 2 * P, P), load_of(NSA_VS, P, P)], 2 * P,
                 [("tokens", [(0, P, [fv[:, i, 2 * P:3 * P] for i in range(TT)], ACT.Copy),
                              (P, 2 * P, [nv[:, 0, i] for i in range(TT)], ACT.Copy)])]),
                ([load_of(NSA_VW, P), load_of(NSA_GATE, 3 * H_NSA, P)], P + 3 * H_NSA,
                 [("tokens", [(0, P, [nv[:, 1, i] for i in range(TT)], ACT.Copy),
                              (P, P + 3 * H_NSA, [gates[:, i] for i in range(TT)], ACT.Sigmoid)])]),
                columns_job(heads_of_groups(0, 2), [nq[:, 0], nq[:, 1]], (ACT.Copy, ATT_SCALE)),
                columns_job(heads_of_groups(2, 1), [nq[:, 2]], (ACT.Copy, ATT_SCALE)),
                columns_job(adjoining(NSA_KC, 2), [nk[:, 0], nk[:, 1]]),
                columns_job(adjoining(NSA_KC + 2 * P, 1), [nk[:, 2]]),
                columns_job(adjoining(FOX_F, 1), [logit[0:H_FOX]]),
            ]
            with Pair(nc, "h1", KD) as h:

                def norm(load):
                    normalise(nc, old, "norm0", lambda k: x_t[:, k], lambda k: gains[:, k:k + 1],
                              shift=lambda k: mod[:, k:k + 1], pair=h, load_next=load)

                def in_a(load):
                    column_products(nc, old, "in_a", lambda t, c: w_in[:, :, bass.ds(t * P, P)], RW_TILES + 6,
                                    lambda k: tile(h, k), store, before=norm, load_next=load)
                mixed_products(nc, old, "in_b", h, jobs, 2 * P, before=in_a)

            with ExitStack() as ctx:
                def b(name, shape):
                    return ctx.enter_context(nc.sbuf_tensor("rw_" + name, shape, F32))
                gate, bonus, v_in = b("gate", [P, 2, T]), b("bonus", [P, 2, T]), b("v", [P, 2, T])
                r_in, a_in, k_in, b_in = (b(n, [P, 2, T]) for n in ("r", "a", "k", "b"))
                tot, mid = b("tot", [P, 2, NCH]), b("mid", [P, 2, NCH])
                rwkv_inputs(nc, old, pj, cols, [A["rwkv_" + n + "_up"][0] for n in "wag"], square, r_in, a_in, k_in, b_in,
                            v_in, gate, bonus, tot, mid)
                rwkv_chunks(nc, old, square, r_in, a_in, k_in, b_in, v_in, tot, mid, y_r)
                rwkv_output(nc, old, y_r, gate, bonus, cols, square, y_r)

            with Pair(nc, "y1", KD) as y_pair:
                with nc.sbuf_tensor("nsa_kcmp", [P, N_CMP], F32) as kcmp, nc.sbuf_tensor("nsa_vcmp", [N_CMP, 2, HD], F32) as vcmp:
                    with nc.sbuf_tensor("fox_left", [P, T], F32) as left, nc.sbuf_tensor("fox_right", [P, T], F32) as right:
                        nsa_compress(nc, old, nk, cols["pe"],
                                     [A[w][0].rearrange("(j p) c -> p j c", p=P) for w in ("nsa_ck_w1", "nsa_cv_w1")],
                                     [A[w][0] for w in ("nsa_ck_w2", "nsa_cv_w2")], kcmp, vcmp,
                                     lambda s, block: fox_decay(s, block, logit, b_f, heads, left, right))
                        with nc.sbuf_tensor("fox_tok", [P, TT, C_FOX], F32) as tok:
                            fox_attention(nc, old, pj, fv, left, right, heads, scratch, tables_out, tok)
                            to_channels(nc, old, "fox_turn", square[:, IDENT],
                                        [(tok[:, :, c * P:(c + 1) * P], tile(y_pair, 2 + c)) for c in range(3)])
                    with nc.sbuf_tensor("nsa_tok", [P, TT, C_NSA], F32) as tok:
                        nsa_attention(nc, old, nq, nk, nv, kcmp, vcmp, gates, scratch, tok, late_modulation)
                        to_channels(nc, old, "nsa_turn", square[:, IDENT],
                                    [(tok[:, :, c * P:(c + 1) * P], tile(y_pair, 5 + c)) for c in range(3)])
                late_gains(nc, old, mod, cols["norm_g"], gains)
                project_and_add(nc, old, "out1", A["w_out"][0], lambda k: tile(y_pair, k), x_t,
                                lambda k: gains[:, KD + k:KD + k + 1],
                                before=lambda load: split_tiles(nc, old, "split1", [y_r[:, k] for k in range(2)], y_pair,
                                                                load))
    with Pair(nc, "hidden1", KF) as hidden:
        with Pair(nc, "h2", KD) as h:
            conv_hidden(nc, old, h, A["ffn_up"][0], cols["conv"], hidden,
                        lambda load: normalise(nc, old, "norm2", lambda k: x_t[:, k],
                                               lambda k: gains[:, 2 * KD + k:2 * KD + k + 1],
                                               shift=lambda k: mod[:, 3 * KD + k:3 * KD + k + 1], pair=h, load_next=load))
        project_and_add(nc, old, "down1", A["ffn_down"][0], lambda k: tile(hidden, k), x_t,
                        lambda k: gains[:, 3 * KD + k:3 * KD + k + 1], chunks=2)


def chunk_view(w, t, c, chunks):
    kt = w.shape[0] // P // chunks
    return view(w)[:, c * kt:(c + 1) * kt, bass.ds(t * P, P)]


def project_and_add(nc, old, name, w, rhs, x_t, gain, chunks=1, before=None):
    with nc.sbuf_tensor(name + "_y", [P, KD, T], F32) as y:
        column_products(nc, old, name, lambda t, c: chunk_view(w, t, c, chunks), KD, rhs,
                        lambda act, t, psum: act.activation(tile_of(y, t), psum, ACT.Copy), chunks, before=before)
        normalise(nc, old, name + "_norm", lambda k: y[:, k], gain, add_to=lambda k: x_t[:, k])





def dilated_attention(nc, old, qa, va, tables_dram, out):
    with nc.sbuf_tensor("dil_tables", [P, A_HEADS, T], F32) as tables:
        units, where = [], []
        for slot in range(A_SLOTS):
            a = slot % 2
            rows = slice(a * HD, (a + 1) * HD)
            for i in reversed(range(TT)):
                unit = []
                for g in range(A_GROUPS):
                    head = g * A_SLOTS + slot
                    lo = max(0, i - 1) if g == 0 else 0
                    unit.append(Piece(
                        qa[rows, head // 2, i * P:(i + 1) * P], qa[rows, (A_HEADS + head) // 2],
                        lambda j, head=head: va[:, j, head * HD:(head + 1) * HD],
                        lo, (i + 1 - lo) * P, tables[:, head, (TT - 1 - i + lo) * P:], table_no=slot * A_GROUPS + g))
                units.append(unit)
                where.append((slot, i))

        def finish(dve, u, o, w, count, finished):
            slot, i = where[u]
            dve.tensor_scalar(out[:, i, slot * HD:(slot + 1) * HD], o, w, None, ALU.mult).then_inc(finished, 1)
        order = [g * A_SLOTS + slot for slot in range(A_SLOTS) for g in range(A_GROUPS)]
        attention(nc, old, "dil", units, HD, [(tables[:, head], tables_dram[TAB_A + head]) for head in order], finish)


def diff_attention(nc, old, qb, vb, minus_lam, tables_dram, out):
    with nc.sbuf_tensor("diff_tables", [P, B_HEADS, T], F32) as tables, nc.sbuf_tensor("diff_scaled", [P, 4], F32) as scaled:
        units, where = [], []
        for h in range(B_HEADS):
            rows = slice(h % 2 * HD, (h % 2 + 1) * HD)
            for i in reversed(range(TT)):
                for m in range(2):
                    units.append([Piece(
                        qb[rows, 2 * m + h // 2, i * P:(i + 1) * P], qb[rows, 4 + 2 * m + h // 2],
                        lambda j, h=h: vb[:, j, h * P:(h + 1) * P], 0, (i + 1) * P, tables[:, h, (TT - 1 - i) * P:],
                        table_no=h)])
                    where.append((h, i, m))

        def finish(dve, u, o, w, count, finished):
            h, i, m = where[u]
            dst = out[:, i, h * P:(h + 1) * P]
            g = scaled[:, u % 4:u % 4 + 1]
            if m == 0:
                dve.tensor_scalar(dst, o, w, None, ALU.mult).then_inc(finished, 1)
            else:
                count.link(dve.tensor_scalar(g, w, minus_lam, None, ALU.mult))
                dve.wait_ge(finished, u + 2)
                dve.scalar_tensor_tensor(dst, o, g, dst, ALU.mult, ALU.add).then_inc(finished, 1)
        attention(nc, old, "diff", units, P, [(tables[:, h], tables_dram[TAB_B + h]) for h in range(B_HEADS)], finish)


def diff_factor(nc, old, lam_in, minus_lam):
    with Stage(nc, "lam", old) as s:
        prod = s.sb("prod", [P, 2, HD])
        sums = s.sb("sums", [P, 2])
        v, a = s.sem("dve"), s.sem("act")
        block = s.block()
        lv = lam_in[:].rearrange("p (m t d) -> p m t d", m=2, t=2)

        @block.vector
        def _(dve):
            c = Count(dve, v)
            c.link(dve.tensor_tensor(prod[:], lv[:, :, 0], lv[:, :, 1], ALU.mult))
            c.link(dve.tensor_reduce(sums[:], prod[:], AX.X, ALU.add))
            dve.wait_ge(a, 1)
            c.link(dve.tensor_tensor(minus_lam[:], sums[:, 1:2], sums[:, 0:1], ALU.subtract))
            c.link(dve.tensor_scalar(minus_lam[:], minus_lam[:], -LAM_INIT, None, ALU.add))

        @block.scalar
        def _(act):
            act.wait_ge(v, 2)
            act.activation(sums[:], sums[:], ACT.Exp).then_inc(a, 1)


def diff_norm(nc, old, tok):
    with Stage(nc, "diff_norm", old) as s:
        squares = s.sb("squares", [P, TT, B_HEADS, P])
        rstd = s.sb("rstd", [P, TT, B_HEADS])
        v, a = s.sem("dve"), s.sem("act")
        eps = s.sb("eps", [P, 1])
        block = s.block()
        view4 = tok[:].rearrange("p i (h d) -> p (i h) d", h=B_HEADS)
        sq = squares[:].rearrange("p i h d -> p (i h) d")
        r = rstd[:].rearrange("p i h -> p (i h)")

        @block.vector
        def _(dve):
            c = Count(dve, v)
            c.add(dve.memset(eps[:], EPS))
            dve.wait_ge(a, 1)
            c.link(dve.tensor_reduce(r, sq, AX.X, ALU.add))
            dve.wait_ge(a, 3)
            c.link(dve.tensor_scalar(r, r, 1.0 - LAM_INIT, None, ALU.mult))
            c.link(dve.tensor_tensor(view4, view4, r.unsqueeze(2).to_broadcast([P, TT * B_HEADS, P]), ALU.mult))

        @block.scalar
        def _(act):
            act.activation(sq, view4, ACT.Square).then_inc(a, 1)
            act.wait_ge(v, 2)
            act.activation(r, r, ACT.Ln, bias=eps[:, 0:1], scale=1.0 / P).then_inc(a, 1)
            act.wait_ge(a, 2)
            act.activation(r, r, ACT.Exp, scale=-0.5).then_inc(a, 1)


def select_and_norm(nc, old, qi, ki, w_idx, causal_dram, penalty, heads, gain, square):
    rounds_of_8 = TOPK // 8
    group = 4
    groups = [list(range(g, min(g + group, len(heads)))) for g in range(0, len(heads), group)]
    tiles = list(range(1, TT))
    n_scores = len(tiles) * IDX_HEADS
    with Stage(nc, "select", old) as s:
        causal = s.sb("causal", [P, T])
        causal_in = s.sem("causal_in")
        relu = s.sb("relu", [P, 4, T])
        score = s.sb("score", [P, TT - 1, T])
        left = s.sb("left", [P, TT - 1, 2, T])
        top = s.sb("top", [P, TT - 1, 8])
        place = s.sb("place", [P, TT - 1, T])
        ones = s.sb("ones", [P, T])
        count_above = s.sb("count_above", [P, TT - 1])
        weight = s.sb("weight", [P, TT, IDX_HEADS])
        squares = s.sb("squares", [P, 2 * group, T])
        rstd = s.sb("rstd", [P, 2, group, T])
        eps = s.sb("eps", [P, 1])
        psum = s.ps("psum", 4 + group)
        done, act_done, summed, v = s.sem("done"), s.sem("relu"), s.sem("summed"), s.sem("dve")
        squared, totals, logged, rooted, scaled, normed = (s.sem(n) for n in
                                                           ("squared", "totals", "logged", "rooted", "scaled", "normed"))
        block = s.block()

        @block.sync
        def _(sp):
            sp.dma_start(causal[:], causal_dram).then_inc(causal_in, 16)

        @block.tensor
        def _(pe):
            warm_up(pe, psum[:, 0], square)
            for m in range(n_scores):
                i, h = tiles[m // IDX_HEADS], m % IDX_HEADS
                if m >= 4:
                    pe.wait_ge(act_done, m - 3)
                rows = slice(HD * (h % 2), HD * (h % 2) + HD)
                pe.matmul(psum[:, m % 4, 0:(i + 1) * P], qi[rows, h // 2, i * P:(i + 1) * P],
                          ki[rows, 0:(i + 1) * P], start=True, stop=True).then_inc(done, 1)
            for g, members in enumerate(groups):
                if g >= 1:
                    pe.wait_ge(logged, g)
                for n in members:
                    pe.wait_ge(squared, n + 1)
                    pe.matmul(psum[:, 4 + n % group], square[:, HEADS], squares[:, n % (2 * group)],
                              start=True, stop=True).then_inc(totals, 1)

        @block.scalar
        def _(act):
            for m in range(n_scores):
                keys = (tiles[m // IDX_HEADS] + 1) * P
                act.wait_ge(done, m + 1)
                if m >= 4:
                    act.wait_ge(summed, m - 3)
                act.activation(relu[:, m % 4, 0:keys], psum[:, m % 4, 0:keys], ACT.Relu, scale=HD ** -0.5)\
                   .then_inc(act_done, 1)
                if m % 2 == 1 and m // 2 < 2 * group:
                    act.activation(squares[:, m // 2], heads[m // 2], ACT.Square).then_inc(squared, 1)

            def take_squares(g):
                for n in groups[g]:
                    act.wait_ge(totals, n - 2 * group + 1)
                    act.activation(squares[:, n % (2 * group)], heads[n], ACT.Square).then_inc(squared, 1)
            act.wait_ge(v, 1)
            for g, members in enumerate(groups):
                if 2 <= g + 1 < len(groups):
                    take_squares(g + 1)
                act.wait_ge(totals, members[-1] + 1)
                if g >= 2:
                    act.wait_ge(normed, groups[g - 2][-1] + 1)
                part = rstd[:, g % 2, 0:len(members)]
                act.activation(part, psum[:, 4:4 + len(members)], ACT.Ln, bias=eps[:, 0:1], scale=1.0 / HD)\
                   .then_inc(logged, 1)
                act.wait_ge(logged, g + 1)
                act.activation(part, part, ACT.Exp, scale=-0.5).then_inc(rooted, 1)
                for n in members:
                    act.activation(heads[n], heads[n], ACT.Identity, scale=gain(n)).then_inc(scaled, 1)

        @block.gpsimd
        def _(pool):
            for g, members in enumerate(groups):
                pool.wait_ge(rooted, g + 1)
                for n in members:
                    pool.wait_ge(scaled, n + 1)
                    pool.tensor_tensor(heads[n], heads[n], rstd[:, g % 2, n % group], ALU.mult).then_inc(normed, 1)

        @block.vector
        def _(dve):
            c = Count(dve, v)
            c.add(dve.memset(eps[:], EPS))
            c.add(dve.memset(ones[:], 1.0))
            c.add(dve.memset(penalty[:, 0], 0.0))
            c.link(dve.tensor_scalar(weight[:], w_idx[:], IDX_HEADS ** -0.5, None, ALU.mult))
            dve.wait_ge(causal_in, 16)
            for m in range(n_scores):
                n, h = divmod(m, IDX_HEADS)
                i, keys = tiles[n], (tiles[n] + 1) * P
                dve.wait_ge(act_done, m + 1)
                if h:
                    dve.wait_ge(summed, m)
                dve.scalar_tensor_tensor(score[:, n, 0:keys], relu[:, m % 4, 0:keys], weight[:, i, h:h + 1],
                                         score[:, n, 0:keys] if h else causal[:, (TT - 1 - i) * P:],
                                         ALU.mult, ALU.add).then_inc(summed, 1)
            dve.wait_ge(summed, n_scores)

            def each_tile(step):
                for n, i in enumerate(tiles):
                    dve.wait_ge(v, c.n - (len(tiles) - 1))
                    c.add(step(n, (i + 1) * P))
            sources = [score[:, n, 0:(i + 1) * P] for n, i in enumerate(tiles)]
            for r in range(rounds_of_8):
                each_tile(lambda n, keys: dve.max(top[:, n], sources[n]))
                if r < rounds_of_8 - 1:
                    each_tile(lambda n, keys: dve.match_replace(left[:, n, r % 2, 0:keys], top[:, n], sources[n], -3.0e38))
                    sources = [left[:, n, r % 2, 0:(i + 1) * P] for n, i in enumerate(tiles)]
            above, equal = left[:, :, 0], left[:, :, 1]
            each_tile(lambda n, keys: dve.tensor_scalar(above[:, n, 0:keys], score[:, n, 0:keys], top[:, n, 7:8], 0.0,
                                                        ALU.is_gt, ALU.add, accum_out=count_above[:, n:n + 1]))
            each_tile(lambda n, keys: dve.tensor_scalar(equal[:, n, 0:keys], score[:, n, 0:keys], top[:, n, 7:8], None,
                                                        ALU.is_equal))
            each_tile(lambda n, keys: dve.tensor_tensor_scan(place[:, n, 0:keys], ones[:, 0:keys], equal[:, n, 0:keys],
                                                             count_above[:, n:n + 1], ALU.mult, ALU.add))
            each_tile(lambda n, keys: dve.scalar_tensor_tensor(equal[:, n, 0:keys], place[:, n, 0:keys], float(TOPK),
                                                               equal[:, n, 0:keys], ALU.is_le, ALU.mult))
            each_tile(lambda n, keys: dve.tensor_tensor(above[:, n, 0:keys], above[:, n, 0:keys], equal[:, n, 0:keys],
                                                        ALU.add))
            each_tile(lambda n, keys: dve.tensor_scalar(penalty[:, tiles[n], 0:keys], above[:, n, 0:keys], -MASKED,
                                                        MASKED, ALU.mult, ALU.add))


def selected_attention(nc, old, qc, kc, vc, penalty, tables_dram, out):
    with nc.sbuf_tensor("sel_tables", [P, C_HEADS, T], F32) as tables:
        units, where = [], []
        for h in range(C_HEADS):
            rows = slice(h % 2 * HD, (h % 2 + 1) * HD)
            for i in reversed(range(TT)):
                units.append([Piece(qc[rows, h // 2, i * P:(i + 1) * P], kc[rows], lambda j: vc[:, j], 0, (i + 1) * P,
                                    tables[:, h, (TT - 1 - i) * P:], plus=penalty[:, i, 0:(i + 1) * P], table_no=h)])
                where.append((h, i))

        def finish(dve, u, o, w, count, finished):
            h, i = where[u]
            dve.tensor_scalar(out[:, i, h * HD:(h + 1) * HD], o, w, None, ALU.mult).then_inc(finished, 1)
        attention(nc, old, "sel", units, HD, [(tables[:, h], tables_dram[TAB_C + h]) for h in range(C_HEADS)], finish)


def gated_branches(nc, old, h, o, kts, w_in, branches, y, before):
    views = [view(w) for w in branches]
    first = [sum(kts[:b]) for b in range(3)]
    with Stage(nc, "branches", old) as s:
        st = Stream(s, RAW * KD, KD,
                    lambda j, r: w_in[:, :, GATES + j * D:][:, :, bass.ds((r * RAW) * (P // RAW), P)] if j < 3 else
                    [(slice(first[b], first[b] + kts[b]), views[b][:, :, bass.ds(r * P, P)]) for b in range(3)],
                    lambda j, k: tile(h if j < 3 else o, k),
                    outputs=lambda j: [(j, 0, KD)] if j < 3 else
                    [(3 + b, first[b], first[b] + kts[b]) for b in range(3)], banks=6, before=before)
        gate = s.sb("gate", [P, 3, T])
        part = s.sb("part", [P, 3, T])
        total = s.sb("total", [P, 2, T])
        added, total_hi, total_lo = s.sem("added"), s.sem("total_hi"), s.sem("total_lo")
        gates_read, products_read = s.sem("gates_read"), s.sem("products_read")
        block = s.block()

        @block.sync
        def _(sp):
            st.load(sp)

        @block.tensor
        def _(pe):
            def banks_free(j, r):
                if j == 0:
                    pe.wait_ge(gates_read, r * 3 + 3)
                if j == 3:
                    pe.wait_ge(products_read, r * 3 + 3)
            st.multiply(pe, banks_free)

        @block.scalar
        def _(act):
            act.sem_inc(gates_read, 3)

            def take(u, j, r):
                if j < 3:
                    st.wait_products(act, u)
                    if j == 0:
                        act.wait_ge(products_read, r * 3 + 3)
                    act.activation(gate[:, j], st.psum[:, j], ACT.Sigmoid).then_inc(gates_read, 1)
                else:
                    act.wait_ge(added, r * 2 + 2)
                    act.activation(tile_of(y[0], r), total[:, 1], ACT.Copy).then_inc(total_hi, 1)
            rounds_ahead(act, st.units, lambda u, j, r: st.round_hi(act, u, j, r), take)

        @block.vector
        def _(dve):
            dve.sem_inc(products_read, 3)

            def combine(u, j, r):
                if j == 3:
                    st.wait_products(dve, u)
                    dve.wait_ge(gates_read, r * 3 + 6)
                    for b in range(3):
                        dve.tensor_tensor(part[:, b], gate[:, b], st.psum[:, 3 + b], ALU.mult)\
                           .then_inc(products_read, 1)
                    dve.wait_ge(products_read, r * 3 + 5)
                    dve.tensor_tensor(total[:, 0], part[:, 0], part[:, 1], ALU.add).then_inc(added, 1)
                    dve.wait_ge(products_read, r * 3 + 6)
                    dve.wait_ge(added, r * 2 + 1)
                    dve.wait_ge(total_lo, r + 1)
                    dve.tensor_tensor(total[:, 1], total[:, 0], part[:, 2], ALU.add).then_inc(added, 1)
            rounds_ahead(dve, st.units, lambda u, j, r: st.split_lo(dve, u, j, r), combine)

        @block.gpsimd
        def _(pool):
            pool.sem_inc(total_lo, 1)

            def lower(t, j, r):
                pool.wait_ge(total_hi, t + 1)
                pool.tensor_tensor(tile_of(y[1], t), total[:, 1], tile_of(y[0], t).bitcast(F32), ALU.subtract)\
                    .then_inc(total_lo, 1)
            rounds(pool, KD, 1, lower)


def half_feed_forward(nc, old, name, A, x_t, norm, half):
    with Pair(nc, name + "_hidden", KF) as hidden:
        def up(load_down):
            with Pair(nc, name + "_h", KD) as h:
                glu_hidden(nc, old, name + "_up", h, A[name + "_w_gate_2"][0], A[name + "_w_up_2"][0], hidden,
                           lambda load: normalise(nc, old, name + "_n", lambda k: x_t[:, k], lambda k: norm[:, k:k + 1],
                                                  pair=h, load_next=load), load_down)
        project_and_sum(nc, old, name + "_down", A[name + "_w_down_2"][0], lambda k: tile(hidden, k), x_t, half,
                        chunks=2, before=up)


def project_and_sum(nc, old, name, w, rhs, x_t, factor, chunks=1, before=None):
    def add(dve, t, psum):
        x = tile_of(x_t, t)
        return dve.scalar_tensor_tensor(x, psum, factor, x, ALU.mult, ALU.add)
    column_products(nc, old, name, lambda t, c: chunk_view(w, t, c, chunks), KD, rhs, add, chunks, by_vector=True,
                    before=before)


def second_block(nc, old, A, x_t, cols, square, scratch, lam_in):
    half_feed_forward(nc, old, "ffn1", A, x_t, cols["ffn1_norm_2"], 0.5)

    def mix_norm(name, h, load, again=False, beside=None):
        normalise(nc, old, name, lambda k: x_t[:, k], lambda k: cols["mix_norm_2"][:, k:k + 1], pair=h, load_next=load,
                  rstd=mix_rstd, rooted_before=again, beside=beside)
    w_in = view(A["w_in_2"][0])
    gain = cols["qk_gain"]
    with ExitStack() as top:
        def sb(name, shape):
            return top.enter_context(nc.sbuf_tensor("two_" + name, shape, F32))
        kts = [2, 4, 2]
        o = sb("o", [P, sum(kts), T])
        mix_rstd = sb("mix_rstd", [P, T])
        o_a, o_b, o_c = o[:, 0:2], o[:, 2:6], o[:, 6:8]
        with ExitStack() as mix:
            def mb(name, shape):
                return mix.enter_context(nc.sbuf_tensor("mix2_" + name, shape, F32))
            qa = mb("qa", [P, 12, T])
            va = mb("va", [P, TT, A_HEADS * HD])
            qb = mb("qb", [P, 8, T])
            vb = mb("vb", [P, TT, B_HEADS * P])
            qc, kc = mb("qc", [P, 3, T]), None
            kc = qc[:, 2]
            vc = mb("vc", [P, TT, HD])
            qi = mb("qi", [P, 5, T])
            ki = qi[:, 4]
            w_idx = mb("w_idx", [P, TT, IDX_HEADS])

            def copy_to(dst):
                return lambda act, t, psum: act.activation(tile_of(dst, t), psum, ACT.Copy)

            def cols_job(start, n, dst):
                return ([(slice(0, n * P), w_in[:, :, start:start + n * P])], n * P,
                        [("columns", c * P, dst(c), ACT.Copy) for c in range(n)])

            def tok_job(start, w, dst):
                return ([(slice(0, w), w_in[:, :, start:start + w])], w,
                        [("tokens", [(0, w, [dst(i) for i in range(TT)], ACT.Copy)])])

            def twice_job(start, dst):
                return ([(slice(a * HD, (a + 1) * HD), w_in[:, :, start:start + HD]) for a in range(2)], P,
                        [("columns", 0, dst, ACT.Copy)])
            jobs = [tok_job(VA + c * 256, 256, lambda i, c=c: va[:, i, c * 256:(c + 1) * 256]) for c in range(3)]
            jobs += [tok_job(VB + c * 256, 256, lambda i, c=c: vb[:, i, c * 256:(c + 1) * 256]) for c in range(2)]
            jobs += [cols_job(QC, 2, lambda c: qc[:, c]), twice_job(KC, kc),
                     ([(slice(0, HD), w_in[:, :, VC:VC + HD]), (slice(HD, HD + IDX_HEADS), w_in[:, :, WI:WI + IDX_HEADS])],
                      HD + IDX_HEADS,
                      [("tokens", [(0, HD, [vc[:, i] for i in range(TT)], ACT.Copy),
                                   (HD, HD + IDX_HEADS, [w_idx[:, i] for i in range(TT)], ACT.Copy)])]),
                     cols_job(QI, 2, lambda c: qi[:, c]), cols_job(QI + 2 * P, 2, lambda c: qi[:, 2 + c]),
                     twice_job(KI, ki)]
            with Pair(nc, "h3", KD) as h:
                column_products(nc, old, "in_2a", lambda t, c: w_in[:, :, bass.ds(t * P + QA, P)], 12,
                                lambda k: tile(h, k), copy_to(qa), before=lambda load: mix_norm("mix_norm", h, load))

                def in_2b(load):
                    column_products(nc, old, "in_2b", lambda t, c: w_in[:, :, bass.ds(t * P + QB, P)], 8,
                                    lambda k: tile(h, k), copy_to(qb), load_next=load)
                mixed_products(nc, old, "in_2c", h, jobs, 2 * P, before=in_2b)
            tiles = [(qa[:, t], 0 if t < 6 else 1) for t in range(12)] + [(qb[:, t], 2 if t < 4 else 3) for t in range(8)]
            tiles += [(qc[:, t], 4 if t < 2 else 5) for t in range(3)]
            penalty = mb("penalty", [P, TT, T])
            select_and_norm(nc, old, qi, ki, w_idx, scratch[TAB_FOX], penalty, [t for t, _ in tiles],
                            lambda n: gain[:, tiles[n][1]:tiles[n][1] + 1], square)

            def turn(name, tok, dst):
                to_channels(nc, old, name, square[:, IDENT],
                            [(tok[:, :, c * P:(c + 1) * P], dst[:, c]) for c in range(tok.shape[2] // P)])
            with nc.sbuf_tensor("dil_tok", [P, TT, 2 * P], F32) as tok:
                dilated_attention(nc, old, qa, va, scratch, tok)
                turn("dil_turn", tok, o_a)
            with nc.sbuf_tensor("diff_tok", [P, TT, 4 * P], F32) as tok, nc.sbuf_tensor("minus_lam", [P, 1], F32) as lam:
                diff_factor(nc, old, lam_in, lam)
                diff_attention(nc, old, qb, vb, lam[:], scratch, tok)
                diff_norm(nc, old, tok)
                to_channels(nc, old, "diff_turn", square[:, IDENT],
                            [(tok[:, :, c * P:(c + 1) * P], o_b[:, c]) for c in range(4)], scale=cols["diff_norm"][:, 0:1])
            with nc.sbuf_tensor("sel_tok", [P, TT, 2 * P], F32) as tok:
                selected_attention(nc, old, qc, kc, vc, penalty, scratch, tok)
                turn("sel_turn", tok, o_c)
        with Pair(nc, "two_y", KD) as y:
            with Pair(nc, "h4", KD) as h, Pair(nc, "two_o", KD) as o_pair:
                def before(load):
                    mix_norm("mix_norm_again", h, load, True,
                             lambda s, block: split_beside(s, block, [o[:, k] for k in range(KD)], o_pair))
                gated_branches(nc, old, h, o_pair, kts, w_in, [A[f"w_branch_{b}_2"][0] for b in "abc"], y, before)
            project_and_sum(nc, old, "out2", A["w_out_2"][0], lambda k: tile(y, k), x_t, 1.0)
    half_feed_forward(nc, old, "ffn2", A, x_t, cols["ffn2_norm_2"], 0.5)



def build(nc, A, C, out):
    scratch = nc.dram_tensor("distance_rows", (N_TABLES, TABLE_LEN), F32, kind="Internal").ap()
    tables = nc.dram_tensor("distance_tables", (N_TABLES, P, T), F32, kind="Internal").ap()
    old = []
    with ExitStack() as top:
        def sb(name, shape):
            return top.enter_context(nc.sbuf_tensor(name, shape, F32))

        tables_out = top.enter_context(nc.semaphore("tables_out"))
        x_t = sb("x_t", [P, KD, T])
        square = sb("square", [P, LEVELS + 7, P])
        mod = sb("mod", [P, 6 * KD])
        gains = sb("gains", [P, 4 * KD])
        heads = sb("heads", [P, H_FOX // 2])
        b_f = sb("b_f", [H_FOX, 1])
        bias = sb("bias", [33, N_TABLES])
        lam_in = sb("lam_in", [P, 4 * HD])
        columns = sb("columns", [P, 5, P])
        store_scale = sb("store_scale", [P, RW_TILES + 6])
        attention.ident, attention.square = square[:, IDENT], square

        rows, used, col = [], [0] * 5, {}

        def put(name, pack, n, src):
            rows.append((pack, used[pack], n, slice(0, P), src))
            col[name] = columns[:, pack, used[pack]:used[pack] + n]
            used[pack] += n

        def put_both(name, pack, n, src):
            for a in range(2):
                rows.append((pack, used[pack], n, slice(a * HD, (a + 1) * HD), src))
            col[name] = columns[:, pack, used[pack]:used[pack] + n]
            used[pack] += n

        def line(w):
            return w.rearrange("a (n p) -> (a n) p", p=P)
        put("norm_g", 0, 4 * KD, A["norm_g"][0].rearrange("a (n p) -> (a n) p", p=P))
        put("c", 0, KD, line(A["c"]))
        put("ada_b", 0, 6 * KD, line(A["ada_b"]))
        for n in ("ffn1_norm_2", "mix_norm_2", "ffn2_norm_2"):
            put(n, 0, KD, line(A[n]))
        cw = A["ffn_conv_w"][0].rearrange("a (n p) -> (a n) p", p=P)
        put("conv01", 1, 4 * KF, cw[0:4 * KF, :])
        put("conv2", 2, 2 * KF, cw[4 * KF:6 * KF, :])
        put("conv_b", 2, 2 * KF, line(A["ffn_conv_b"]))
        put("mu", 3, RW_TILES, line(A["rwkv_mu"]))
        for n in ("w0", "a0", "k_k", "k_a", "ln_w", "ln_b"):
            put(n, 3, 2, line(A["rwkv_" + n]))
        put("r_k", 3, 2, A["rwkv_r_k"][0].rearrange("(n a) d -> n (a d)", a=2))
        put("diff_norm", 3, 1, A["diff_out_norm_2"])
        put_both("qk_gain", 3, 6, A["qk_gain_2"][0].rearrange("a b d -> (a b) d"))
        put_both("pe_k", 4, L_CMP, A["nsa_pe_k"][0])
        put_both("pe_v", 4, L_CMP, A["nsa_pe_v"][0])
        extra = [
            (b_f[:], A["fox_b_f"].rearrange("a h -> h a")),
            (bias[0:32, 0:H_NSA], A["rel_bias"]),
            (bias[0:32, H_NSA:N_TABLES - 1], A["rel_bias_2"]),
            (lam_in[:], A["diff_lambda_2"].rearrange("a b d -> a (b d)")[0].partition_broadcast(P)),
            (heads[:], C["heads"]),
        ]
        with Stage(nc, "zero_bias", old) as s:
            block = s.block()
            @block.vector
            def _(dve):
                dve.memset(bias[0:32, N_TABLES - 1:N_TABLES], 0.0)
                dve.memset(bias[32:33], MASKED)
        cols = dict(col)
        cols["pe"] = columns[:, 4, 0:2 * L_CMP].rearrange("p (a l) -> p a l", a=2)

        def conv(t, w, tap_no):
            pack, start = {0: (1, 0), 1: (1, 2 * KF), 2: (2, 0), 3: (2, 2 * KF)}[tap_no]
            return columns[:, pack, bass.ds(t + (start + w * KF), 1)]
        cols["conv"] = conv
        silu = sb("silu", [P, KD])
        modulation(nc, old, col["c"], silu, view(A["ada_w"][0]), col["ada_b"], mod,
                   lambda load: load_parameters(nc, old, rows, used, columns, square, C["square"], A["x"][0], x_t,
                                                extra, load),
                   lambda s, block: distance_tables(s, block, C["onehot"], bias, scratch, tables, tables_out))
        early_gains(nc, old, mod, col["norm_g"], gains, col["qk_gain"], store_scale)
        first_block(nc, old, A, x_t, store_scale, tables_out, LateModulation(silu, view(A["ada_w"][0]), col["ada_b"], mod), gains, mod, cols, square, tables, heads, b_f[:])
        second_block(nc, old, A, x_t, cols, square, tables, lam_in)

        with Stage(nc, "store", old) as s:
            tok = s.sb("tok", [P, TT, D])
            psum = s.ps("psum", 4)
            done, kept, stored = s.sem("done"), s.sem("kept"), s.sem("stored")
            block = s.block()

            @block.tensor
            def _(pe):
                for n in range(2 * TT):
                    i, half = divmod(n, 2)
                    if n >= 4:
                        pe.wait_ge(kept, n - 3)
                    for k in range(4):
                        mm = pe.transpose(psum[:, n % 4, k * P:(k + 1) * P],
                                          x_t[:, half * 4 + k, i * P:(i + 1) * P], square[:, IDENT])
                    mm.then_inc(done, 1)

            @block.vector
            def _(dve):
                for n in range(2 * TT):
                    i, half = divmod(n, 2)
                    dve.wait_ge(done, n + 1)
                    dve.tensor_copy(tok[:, i, half * T:(half + 1) * T], psum[:, n % 4]).then_inc(kept, 1)

            @block.sync
            def _(sp):
                for i in range(TT):
                    sp.wait_ge(kept, 2 * i + 2)
                    sp.dma_start(out[0, i * P:(i + 1) * P, :], tok[:, i]).then_inc(stored, 16)
                sp.wait_ge(stored, 16 * TT)


def kernel(**inputs):
    import concourse.bacc as _bacc
    from concourse.bass_utils import run_bass_kernel_spmd as _run

    nc = _bacc.Bacc("TRN2", target_bir_lowering=False, num_devices=1)
    arrays, A, C = {}, {}, {}
    constants = {"square": square_constants(), "onehot": distance_buckets(), "heads": head_rows()}
    for group, into in ((inputs, A), (constants, C)):
        for name, value in group.items():
            a = np.ascontiguousarray(value)
            arrays[f"in_{name}_dram"] = a
            into[name] = nc.dram_tensor(f"in_{name}_dram", a.shape, F32, kind="ExternalInput").ap()
    out = nc.dram_tensor("out_0_dram", (1, T, D), F32, kind="ExternalOutput").ap()
    build(nc, A, C, out)
    r = _run(nc, [arrays], core_ids=[0])
    return r.results[0]["out_0_dram"]
```
